# Optimizing a Trainium2 kernel written in Bass

```python
import math
import jax, jax.numpy as jnp
from jax import lax
import numpy as np

D_MODEL = 1024
BATCH = 1
SEQ = 512
DEPTH = 1

MEM_LEN = 256
MLA_HEADS = 8
MLA_Q_RANK = 384
MLA_KV_RANK = 128
MLA_NOPE = 64
MLA_ROPE = 32
MLA_V = 64
Q_BLOCK = 128
RET_HEADS = 4
RET_DK = 64
RET_DV = 128
RET_CHUNK = 128
X_HEADS = 4
X_DH = 128
N_BRANCH = 3
PEER_HEADS = 8
PEER_N_KEYS = 128
PEER_N_EXPERTS = PEER_N_KEYS * PEER_N_KEYS
PEER_TOPK = 16
PEER_DQ = 256
PEER_DHALF = PEER_DQ // 2
PEER_TOKEN_BLOCK = 128

ROPE_BASE = 10000.0
EPS = 1e-6
IN_SPLITS = (MLA_Q_RANK, MLA_KV_RANK, MLA_ROPE,
             RET_HEADS * RET_DK, RET_HEADS * RET_DK, RET_HEADS * RET_DV, RET_HEADS * RET_DV,
             X_HEADS * X_DH, N_BRANCH * D_MODEL)
IN_COLS = sum(IN_SPLITS)

kernel_name = "hybrid_mla_retention_memxattn_peer"

def rmsnorm(x, g):
    xf = x.astype(jnp.float32)
    y = xf * lax.rsqrt(jnp.mean(xf * xf, axis=-1, keepdims=True) + EPS)
    return (y * g.astype(jnp.float32)).astype(x.dtype)

def rope(x, positions):
    d = x.shape[-1]
    inv_freq = ROPE_BASE ** (-jnp.arange(0, d, 2, dtype=jnp.float32) / d)
    ang = positions.astype(jnp.float32)[..., None] * inv_freq
    cos = jnp.cos(ang)[:, :, None, :].astype(x.dtype)
    sin = jnp.sin(ang)[:, :, None, :].astype(x.dtype)
    x1, x2 = x[..., : d // 2], x[..., d // 2:]
    return jnp.concatenate([x1 * cos - x2 * sin, x1 * sin + x2 * cos], axis=-1)

def causal_attention_blocked(q, k, v, scale):
    B, H, S, dqk = q.shape
    nb = S // Q_BLOCK
    qb = q.reshape(B, H, nb, Q_BLOCK, dqk).transpose(2, 0, 1, 3, 4)
    kpos = jnp.arange(S)

    def one_block(args):
        q_blk, bi = args
        qpos = bi * Q_BLOCK + jnp.arange(Q_BLOCK)
        s = jnp.einsum('bhqd,bhkd->bhqk', q_blk, k).astype(jnp.float32) * scale
        s = jnp.where(kpos[None, :] <= qpos[:, None], s, jnp.float32(-1e30))
        p = jax.nn.softmax(s, axis=-1).astype(v.dtype)
        return jnp.einsum('bhqk,bhkd->bhqd', p, v)

    o = lax.map(one_block, (qb, jnp.arange(nb)))
    return o.transpose(1, 2, 0, 3, 4).reshape(B, H, S, v.shape[-1])

def mla_branch(c_q, c_kv, k_r, positions, q_norm_g, w_uq, kv_norm_g, w_ukv, qn_g, kn_g, w_o):
    B, S, _ = c_q.shape
    q = (rmsnorm(c_q, q_norm_g) @ w_uq).reshape(B, S, MLA_HEADS, MLA_NOPE + MLA_ROPE)
    kv = (rmsnorm(c_kv, kv_norm_g) @ w_ukv).reshape(B, S, MLA_HEADS, MLA_NOPE + MLA_V)
    k_nope, v = kv[..., :MLA_NOPE], kv[..., MLA_NOPE:]
    k_rope = jnp.broadcast_to(k_r[:, :, None, :], (B, S, MLA_HEADS, MLA_ROPE))
    k = jnp.concatenate([k_nope, k_rope], axis=-1)
    q = rmsnorm(q, qn_g)
    k = rmsnorm(k, kn_g)
    q = jnp.concatenate([q[..., :MLA_NOPE], rope(q[..., MLA_NOPE:], positions)], axis=-1)
    k = jnp.concatenate([k[..., :MLA_NOPE], rope(k[..., MLA_NOPE:], positions)], axis=-1)
    scale = (MLA_NOPE + MLA_ROPE) ** -0.5
    o = causal_attention_blocked(q.transpose(0, 2, 1, 3), k.transpose(0, 2, 1, 3),
                                 v.transpose(0, 2, 1, 3), scale)
    o = o.transpose(0, 2, 1, 3).reshape(B, S, MLA_HEADS * MLA_V)
    return o @ w_o

def retention_chunkwise(q, k, v, log_gamma):
    B, H, S, dk = q.shape
    dv = v.shape[-1]
    L = RET_CHUNK
    C = S // L
    dt = q.dtype
    qc = q.reshape(B, H, C, L, dk)
    kc = k.reshape(B, H, C, L, dk)
    vc = v.reshape(B, H, C, L, dv)
    idx = jnp.arange(L, dtype=jnp.float32)
    diff = idx[:, None] - idx[None, :]
    lg = log_gamma[:, None, None]
    decay = jnp.where(diff >= 0, jnp.exp(lg * jnp.maximum(diff, 0.0)), 0.0).astype(dt)
    xi = jnp.exp(log_gamma[:, None] * (idx + 1.0)).astype(dt)
    zeta = jnp.exp(log_gamma[:, None] * (L - 1.0 - idx)).astype(dt)
    inner = jnp.einsum('bhcid,bhcjd->bhcij', qc, kc) * decay[None, :, None]
    inner_out = jnp.einsum('bhcij,bhcje->bhcie', inner, vc)
    incr = jnp.einsum('bhcjd,bhcje->cbhde', kc * zeta[None, :, None, :, None], vc)
    chunk_decay = jnp.exp(log_gamma * L).astype(incr.dtype)[None, :, None, None]

    def step(R, inc):
        return chunk_decay * R + inc, R

    _, R_prev = lax.scan(step, jnp.zeros((B, H, dk, dv), incr.dtype), incr)
    cross = jnp.einsum('bhcid,cbhde->bhcie', qc * xi[None, :, None, :, None], R_prev)
    return (inner_out + cross).reshape(B, H, S, dv)

def retention_branch(r_q, r_k, r_v, r_g, positions, gn_g, w_o):
    B, S, _ = r_q.shape
    q = rope(r_q.reshape(B, S, RET_HEADS, RET_DK), positions)
    k = rope(r_k.reshape(B, S, RET_HEADS, RET_DK), positions) * (RET_DK ** -0.5)
    v = r_v.reshape(B, S, RET_HEADS, RET_DV)
    log_gamma = jnp.log(1.0 - 2.0 ** (-5.0 - jnp.arange(RET_HEADS, dtype=jnp.float32)))
    o = retention_chunkwise(q.transpose(0, 2, 1, 3), k.transpose(0, 2, 1, 3),
                            v.transpose(0, 2, 1, 3), log_gamma)
    o = rmsnorm(o.transpose(0, 2, 1, 3), gn_g)
    o = o.reshape(B, S, RET_HEADS * RET_DV) * jax.nn.silu(r_g)
    return o @ w_o

def memory_branch(x_q, mem, mem_g, w_mem_kv, qn_g, kn_g, w_o):
    B, S, _ = x_q.shape
    M = mem.shape[1]
    q = rmsnorm(x_q.reshape(B, S, X_HEADS, X_DH), qn_g)
    kv = (rmsnorm(mem, mem_g) @ w_mem_kv).reshape(B, M, X_HEADS, 2 * X_DH)
    k = rmsnorm(kv[..., :X_DH], kn_g)
    v = kv[..., X_DH:]
    s = jnp.einsum('bshd,bmhd->bhsm', q, k).astype(jnp.float32) * (X_DH ** -0.5)
    p = jax.nn.softmax(s, axis=-1).astype(v.dtype)
    o = jnp.einsum('bhsm,bmhd->bshd', p, v).reshape(B, S, X_HEADS * X_DH)
    return o @ w_o

def peer_ffn(xn, w_q, sub_keys, u_tab, v_tab):
    B, S, D = xn.shape
    T = B * S
    xt = xn.reshape(T, D)
    q = (xt @ w_q).reshape(T, PEER_HEADS, 2, PEER_DHALF)
    s = jnp.einsum('thcd,hcnd->thcn', q, sub_keys)
    sv, si = lax.top_k(s, PEER_TOPK)
    cand = (sv[:, :, 0, :, None] + sv[:, :, 1, None, :]).reshape(T, PEER_HEADS, PEER_TOPK * PEER_TOPK)
    cand_idx = (si[:, :, 0, :, None] * PEER_N_KEYS + si[:, :, 1, None, :]).reshape(
        T, PEER_HEADS, PEER_TOPK * PEER_TOPK)
    best, pos = lax.top_k(cand, PEER_TOPK)
    experts = jnp.take_along_axis(cand_idx, pos, axis=-1)
    gate = jax.nn.softmax(best.astype(jnp.float32), axis=-1).astype(xn.dtype)
    nb = T // PEER_TOKEN_BLOCK

    def one_block(args):
        xb, eb, gb = args
        u = u_tab[eb]
        a = jax.nn.gelu(jnp.einsum('thkd,td->thk', u, xb))
        vv = v_tab[eb]
        return jnp.einsum('thk,thkd->td', gb * a, vv)

    out = lax.map(one_block, (xt.reshape(nb, PEER_TOKEN_BLOCK, D),
                              experts.reshape(nb, PEER_TOKEN_BLOCK, PEER_HEADS, PEER_TOPK),
                              gate.reshape(nb, PEER_TOKEN_BLOCK, PEER_HEADS, PEER_TOPK)))
    return out.reshape(B, S, D)

def setup_inputs(seed: int = 0) -> dict:
    key = jax.random.key(seed)
    ks = jax.random.split(key, 32)
    f32 = jnp.float32

    def nrm(k, shape, scale):
        return jax.random.normal(k, shape, f32) * scale

    def gain(k, shape):
        return 1.0 + 0.02 * jax.random.normal(k, shape, f32)

    start = jax.random.randint(ks[2], (BATCH, 1), 0, 1024, dtype=jnp.int32)
    positions = (start + jnp.arange(SEQ, dtype=jnp.int32)[None, :]).astype(jnp.int32)
    return {
        "x": nrm(ks[0], (BATCH, SEQ, D_MODEL), 1.0),
        "mem": nrm(ks[1], (BATCH, MEM_LEN, D_MODEL), 1.0),
        "positions": positions,
        "attn_norm_g": gain(ks[3], (DEPTH, D_MODEL)),
        "w_in": nrm(ks[4], (DEPTH, D_MODEL, IN_COLS), D_MODEL ** -0.5),
        "mla_q_norm_g": gain(ks[5], (DEPTH, MLA_Q_RANK)),
        "w_uq": nrm(ks[6], (DEPTH, MLA_Q_RANK, MLA_HEADS * (MLA_NOPE + MLA_ROPE)), MLA_Q_RANK ** -0.5),
        "mla_kv_norm_g": gain(ks[7], (DEPTH, MLA_KV_RANK)),
        "w_ukv": nrm(ks[8], (DEPTH, MLA_KV_RANK, MLA_HEADS * (MLA_NOPE + MLA_V)), MLA_KV_RANK ** -0.5),
        "mla_qn_g": gain(ks[9], (DEPTH, MLA_NOPE + MLA_ROPE)),
        "mla_kn_g": gain(ks[10], (DEPTH, MLA_NOPE + MLA_ROPE)),
        "w_o_mla": nrm(ks[11], (DEPTH, MLA_HEADS * MLA_V, D_MODEL), (MLA_HEADS * MLA_V) ** -0.5),
        "ret_gn_g": gain(ks[12], (DEPTH, RET_HEADS, RET_DV)),
        "w_o_ret": nrm(ks[13], (DEPTH, RET_HEADS * RET_DV, D_MODEL), (RET_HEADS * RET_DV) ** -0.5),
        "mem_norm_g": gain(ks[14], (DEPTH, D_MODEL)),
        "w_mem_kv": nrm(ks[15], (DEPTH, D_MODEL, X_HEADS * 2 * X_DH), D_MODEL ** -0.5),
        "x_qn_g": gain(ks[16], (DEPTH, X_DH)),
        "x_kn_g": gain(ks[17], (DEPTH, X_DH)),
        "w_o_cross": nrm(ks[18], (DEPTH, X_HEADS * X_DH, D_MODEL), (X_HEADS * X_DH) ** -0.5),
        "w_out": nrm(ks[19], (DEPTH, D_MODEL, D_MODEL), D_MODEL ** -0.5),
        "ffn_norm_g": gain(ks[20], (DEPTH, D_MODEL)),
        "peer_w_q": nrm(ks[21], (DEPTH, D_MODEL, PEER_HEADS * PEER_DQ), D_MODEL ** -0.5),
        "peer_keys": nrm(ks[22], (DEPTH, PEER_HEADS, 2, PEER_N_KEYS, PEER_DHALF), PEER_DHALF ** -0.5),
        "peer_u": nrm(ks[23], (DEPTH, PEER_N_EXPERTS, D_MODEL), D_MODEL ** -0.5),
        "peer_v": nrm(ks[24], (DEPTH, PEER_N_EXPERTS, D_MODEL), (PEER_HEADS * PEER_TOPK) ** -0.5),
    }

def reference(x, mem, positions, attn_norm_g, w_in, mla_q_norm_g, w_uq, mla_kv_norm_g, w_ukv,
              mla_qn_g, mla_kn_g, w_o_mla, ret_gn_g, w_o_ret, mem_norm_g, w_mem_kv, x_qn_g, x_kn_g,
              w_o_cross, w_out, ffn_norm_g, peer_w_q, peer_keys, peer_u, peer_v):
    B, S, _ = x.shape
    split_points = []
    acc = 0
    for sz in IN_SPLITS[:-1]:
        acc += sz
        split_points.append(acc)
    h = x
    for layer in range(DEPTH):
        n = rmsnorm(h, attn_norm_g[layer])
        proj = n @ w_in[layer]
        c_q, c_kv, k_r, r_q, r_k, r_v, r_g, x_q, gates = jnp.split(proj, split_points, axis=-1)
        y_mla = mla_branch(c_q, c_kv, k_r, positions, mla_q_norm_g[layer], w_uq[layer],
                           mla_kv_norm_g[layer], w_ukv[layer], mla_qn_g[layer], mla_kn_g[layer],
                           w_o_mla[layer])
        y_ret = retention_branch(r_q, r_k, r_v, r_g, positions, ret_gn_g[layer], w_o_ret[layer])
        y_mem = memory_branch(x_q, mem, mem_norm_g[layer], w_mem_kv[layer], x_qn_g[layer],
                              x_kn_g[layer], w_o_cross[layer])
        g = jax.nn.sigmoid(gates.reshape(B, S, N_BRANCH, D_MODEL))
        merged = g[:, :, 0] * y_mla + g[:, :, 1] * y_ret + g[:, :, 2] * y_mem
        h = h + merged @ w_out[layer]
        h = h + peer_ffn(rmsnorm(h, ffn_norm_g[layer]), peer_w_q[layer], peer_keys[layer],
                         peer_u[layer], peer_v[layer])
    return h


_drawn_inputs = setup_inputs


def setup_inputs(seed=0):
    import zlib

    import numpy as np

    out = dict(_drawn_inputs(seed))
    spreads = {}
    factors = {'attn_norm_g': 4.216,
     'mla_q_norm_g': 8.0,
     'mla_kv_norm_g': 8.0,
     'mla_qn_g': 8.0,
     'mla_kn_g': 8.0,
     'ret_gn_g': 24.725,
     'mem_norm_g': 8.0,
     'x_qn_g': 8.0,
     'x_kn_g': 8.0,
     'ffn_norm_g': 64.0}
    for name, (base, spread) in spreads.items():
        noise = np.random.default_rng([zlib.crc32(name.encode()), seed]).standard_normal(out[name].shape)
        drawn = base * np.exp(spread * noise) if base else spread * noise
        out[name] = __import__('jax').numpy.asarray(drawn.astype(out[name].dtype))
    for name, factor in factors.items():
        out[name] = (out[name] * factor).astype(out[name].dtype)
    return out
```

```python
from contextlib import ExitStack

import numpy as np

import concourse.bass as bass
from concourse import mybir

F32 = mybir.dt.float32
I32 = mybir.dt.int32
U32 = mybir.dt.uint32
ALU = mybir.AluOpType
ACT = mybir.ActivationFunctionType
AX = mybir.AxisListType

P = 128
D = 1024
S = 512
M = 256
T = S // P
KD = D // P
HA, NOPE, ROPE, VD = 8, 64, 32, 64
QK = NOPE + ROPE
QR, KVR = 384, 128
HR, RK, RV = 4, 64, 128
HX, XD = 4, 128
HP, NK, TOP = 8, 128, 16
EPS = 1e-6
SPLITS = (QR, KVR, ROPE, HR * RK, HR * RK, HR * RV, HR * RV, HX * XD, 3 * D)
OFF = [sum(SPLITS[:i]) for i in range(len(SPLITS))]
(C_Q, C_KV, C_KR, R_Q, R_K, R_V, R_G, X_Q, GATES) = OFF
COLS = sum(SPLITS)
CHUNKS = 12
CW = COLS // CHUNKS
SLOT = KD * 512
NEG = -1e30
ATT_SCALE = QK ** -0.5
MEM_SCALE = XD ** -0.5
RING = 4
CONSTANT_LOADS = 13
TWO_PI = 6.283185307179586
TP1 = 6.28125
TP2 = float(np.round((TWO_PI - TP1) * 2 ** 24) / 2 ** 24)
TP3 = TWO_PI - TP1 - TP2
PI_LOW = 3.1415925
ROUND = 12582912.0
GELU_A, GELU_B = 0.7978845608028654, 0.044715

K_ID = 0
K_DECAY = K_ID + P
K_XI = K_DECAY + HR * P
K_ZETA = K_XI + HR * P
K_IOTA = K_ZETA + HR
K_INV = K_IOTA + TOP
K_END = K_INV + 48

FRONT_USES = ([("cT", 4), ("xqT", 5), ("q0", 2), ("q1", 3), ("kv0", 2), ("kv1", 3),
               ("rqT", 4), ("rkT", 5), ("rin", 6), ("ro", 7), ("rinc", 6),
               ("qT0", 4), ("qT1", 5), ("kT0", 4), ("kT1", 5)]
              + [u for h in range(HA) for u in ((f"s{h}", 2 + h % 2), (f"pT{h}", 4 + h % 2))]
              + [("o", 7), ("oT", 4), ("y0a", 2), ("y0b", 3), ("roT", 5), ("y1a", 2), ("y1b", 3),
                 ("ms0", 6), ("ms1", 7), ("mp0", 4), ("mp1", 5), ("mo", 6), ("moT", 4),
                 ("y2a", 2), ("y2b", 3), ("mT0", 4), ("mT1", 5), ("ha", 2), ("hb", 3),
                 ("xT0", 4), ("xT1", 5)]
              + [u for c in range(4) for u in ((f"pq{c}", 6 + c % 2), (f"sc{c}", 2 + c % 2))])
SETUP_USES = {2: CHUNKS, 3: CHUNKS, 4: CHUNKS, 5: CHUNKS, 6: 4, 7: 4}
BANK, ORDER, PER_BANK = {}, {}, {b: 0 for b in SETUP_USES}
for _name, _bank in FRONT_USES:
    BANK[_name], ORDER[_name] = _bank, PER_BANK[_bank]
    PER_BANK[_bank] += 1

EVENTS = {"c_stats": 6, "c_rstd": 1, "c_normed": 6, "r_roped": 1, "kz": 1, "rg_tanh": 1,
          "qk_roped": 1, "ro_stats": 4, "ro_done": 1, "p_exp": HA, "gate_tanh": 3, "merged": 1, "mem_max": 2,
          "f_stats": 1, "f_rstd": 1, "xn_scaled": 1, "xn_done": 1, "best_sub": 1, "best_exp": 1, "handed": 1}
LAST_PRODUCT = ["kv1", "y0b", "y1b", "y2b", "ha", "hb", "pq0", "pq1", "pq2", "pq3"]
CHUNKS_PER_TILE = len(LAST_PRODUCT)
DVE_LINKS = 90
PEER_LINKS = HP * 3


def build(nc, a, out):
    with ExitStack() as ctx:
        def sb(name, shape, dt=F32):
            return ctx.enter_context(nc.sbuf_tensor(name, shape, dt))

        def sem(name):
            return ctx.enter_context(nc.semaphore(name))

        wring = sb("wring", [P, 2, SLOT])
        ub = sb("ub", [P, RING, D])
        vb = sb("vb", [P, RING, D])
        pa = sb("pa", [P, GATES])
        gt = sb("gt", [P, D])
        kT = sb("kT", [P, HA * S])
        vc = sb("vc", [P, T, HA * VD])
        mkT = sb("mkT", [P, HX, M])
        mv = sb("mv", [P, 2, HX, XD])
        keysT = sb("keysT", [P, 2 * HP, NK])
        hx = sb("hx", [P, 4, D])
        mT = sb("mT", [P, KD, P])
        work = sb("work", [P, 4096])
        ssb = sb("ssb", [P, 2, S])
        pT = sb("pT", [P, 2, S])
        ob = sb("ob", [P, 512])
        oT = sb("oT", [P, 4, P])
        merged = sb("merged", [P, D])
        tmp = sb("tmp", [P, D])
        xqT = sb("xqT", [P, 4, P])
        kz = sb("kz", [P, HR, RK])
        state = sb("state", [RK, HR, RV])
        ro = sb("ro", [P, HR, RV])
        rth = sb("rth", [P, 512])
        mask = sb("mask", [P, S])
        cst = sb("cst", [P, K_END])
        grow = sb("grow", [P, D])
        gnrow = sb("gnrow", [P, HR * RV])
        qkrow = sb("qkrow", [P, 2, QK])
        mkrow = sb("mkrow", [P, XD])
        gcols = sb("gcols", [P, 2 * KD + 5])
        rope = sb("rope", [P, T, 2, 48])
        ropet = sb("ropet", [P, 2, 48])
        posi = sb("posi", [P, T], I32)
        diag = sb("diag", [P, RING, P])
        small = sb("small", [P, 512])
        topv = sb("topv", [P, 2 * HP, TOP])
        topi = sb("topi", [P, 2 * HP, TOP], U32)
        idx = sb("idx", [P, HP * TOP], U32)
        idxn = sb("idxn", [P, HP * TOP], U32)
        gate = sb("gate", [P, HP * TOP])
        gaten = sb("gaten", [P, HP * TOP])
        acts = sb("acts", [P, 5, TOP])
        wts = sb("wts", [P, 2, TOP])

        ps = [ctx.enter_context(nc.psum_tensor(f"bank{b}", [P, 512], F32)) for b in range(8)]
        proj = nc.dram_tensor("proj_scratch", (S, COLS), F32, kind="Internal").ap()

        ident = cst[:, K_ID:K_ID + P]
        decayT = cst[:, K_DECAY:K_DECAY + HR * P]
        xiT = cst[0:RK, K_XI:K_XI + HR * P]
        zeta = cst[:, K_ZETA:K_ZETA + HR]
        iota = cst[:, K_IOTA:K_IOTA + TOP]
        h_next, xn_next, h_cur, xn_cur = (hx[:, i, :] for i in range(4))
        qk = work[:, 0:2 * HA * QK].rearrange("p (h d) -> p h d", d=QK)
        sq = work[:, 1536:1536 + 1536].rearrange("p (h d) -> p h d", d=QK)
        qT = work[:, 3072:4096].rearrange("p (h n) -> p h n", n=P)
        scores = work[:, 0:2048].rearrange("p (h n) -> p h n", n=NK)
        cand = work[:, 2048:4096].rearrange("p (h n) -> p h n", n=TOP * TOP)
        hot = work[:, 0:2048].rearrange("p (h k j) -> p h k j", k=TOP, j=TOP)
        kTh = kT[:, :].rearrange("p (h s) -> p h s", s=S)
        memT = kT[:, 0:KD * M].rearrange("p (k m) -> p k m", m=M)
        memN = kT[:, KD * M:KD * M + 2 * D].rearrange("p (m d) -> p m d", d=D)
        xT = ub[:, :, :].rearrange("p r d -> p (r d)").rearrange("p (k s) -> p k s", s=S)
        stage = vb[:, :, :].rearrange("p r d -> p (r d)")[:, 0:2 * T * CW].rearrange("p (b t n) -> p b t n", b=2, t=T)
        pqT, cT, res = ssb, oT, merged
        rqT, rkT = mT[0:RK, 0:HR, :], mT[0:RK, HR:2 * HR, :]
        inner = merged[:, 0:HR * P].rearrange("p (h n) -> p h n", n=P)
        rxT = merged[0:RK, HR * P:2 * HR * P].rearrange("p (h n) -> p h n", n=P)
        rstd_x, rstd_m, c_st, qk_st = small[:, 0:4], small[:, 4:6], small[:, 8:14], small[:, 16:32]
        ro_st, f_st, mem_st, l_att = small[:, 32:36], small[:, 36:37], small[:, 40:42], small[:, 48:56]
        nmax, mmax, l_mem, gsum = small[:, 56:64], small[:, 64:68], small[:, 68:72], small[:, 72:80]
        nwt = small[:, 80:112]
        posf = small[:, 112:116]
        seli = small[:, 128:256].rearrange("p (h k) -> p h k", k=TOP)
        seli2 = small[:, 256:384].rearrange("p (h k) -> p h k", k=TOP)
        besub = small[:, 384:512].rearrange("p (h k) -> p h k", k=TOP)
        bval = topv[:, 0:HP, :]

        s_const, s_x, s_xT, s_mem = sem("constants_in"), sem("x_in"), sem("xT_in"), sem("memory_in")
        w_in = [sem("weights_in_0"), sem("weights_in_1")]
        full = {b: sem(f"psum_full_{b}") for b in SETUP_USES}
        drained = {b: sem(f"psum_drained_{b}") for b in SETUP_USES}
        ev = {n: sem("ev_" + n) for n in EVENTS}
        s_parked = [sem("stage_parked_0"), sem("stage_parked_1")]
        s_pa, s_gt, s_h, s_mask = sem("projection_in"), sem("gates_in"), sem("residual_in"), sem("mask_in")
        s_sums, s_rope = sem("setup_sums"), sem("setup_rope")
        s_rstd, s_angles, s_mem_g, s_mem_keys = sem("setup_rstd"), sem("setup_angles"), sem("setup_mem_gain"), sem("memory_keys")
        s_ready = sem("setup_ready")
        dve_chain, act_chain = sem("dve_chain"), sem("act_chain")
        peer_chain = sem("peer_chain")
        u_in = [sem(f"u_in_{r}") for r in range(RING)]
        v_in = [sem(f"v_in_{r}") for r in range(RING)]
        dots, gelu_in, gelu_tanh = sem("dots_done"), sem("gelu_in"), sem("gelu_tanh")
        s_wts, s_diag, v_used = sem("weights_ready"), sem("diag_ready"), sem("v_used")
        s_taken, s_out = sem("sum_taken"), sem("out_stored")

        FULL = {name: full[b] for name, b in BANK.items()}
        DRAINED = {name: drained[b] for name, b in BANK.items()}

        def bank_free(name, t):
            return DRAINED[name], SETUP_USES[BANK[name]] + t * PER_BANK[BANK[name]] + ORDER[name]

        def computed(name, t):
            return FULL[name], SETUP_USES[BANK[name]] + t * PER_BANK[BANK[name]] + ORDER[name] + 1

        def in_sbuf(name, t):
            return DRAINED[name], SETUP_USES[BANK[name]] + t * PER_BANK[BANK[name]] + ORDER[name] + 1

        def event(name, t, k=None):
            return ev[name], t * EVENTS[name] + (EVENTS[name] if k is None else k)

        block = ctx.enter_context(nc.Block())

        @block.sync
        def _(sp):
            def consts():
                sp.dma_start(cst[:, :], a["consts"]).then_inc(s_const, 16)
                sp.dma_start(posi[:, :], a["positions"]).then_inc(s_const, 16)
                for k, (name, n) in enumerate((("attn_norm_g", KD), ("mem_norm_g", KD), ("mla_q_norm_g", 3),
                                               ("mla_kv_norm_g", 1), ("x_qn_g", 1))):
                    at = (0, KD, 2 * KD, 2 * KD + 3, 2 * KD + 4)[k]
                    sp.dma_start(gcols[:, at:at + n], a[name]).then_inc(s_const, 16)
                for dst, name in ((grow[:, :], "ffn_norm_g"), (gnrow[:, :], "ret_gn_g"), (qkrow[:, 0, :], "mla_qn_g"),
                                  (qkrow[:, 1, :], "mla_kn_g"), (mkrow[:, :], "x_kn_g")):
                    src = a[name]
                    if name == "ret_gn_g":
                        src = src.rearrange("o h d -> o (h d)")
                    sp.dma_start(dst, src.broadcast_to((P, src.shape[1]))).then_inc(s_const, 16)
                sp.dma_start(keysT[:, :, :], a["keysT"]).then_inc(s_const, 16)

            def w_in_chunk(i, b):
                if not isinstance(i, int):
                    sp.wait_ge(full[5], 2 * i + b - 1)
                    sp.nop(nofuse=True)
                sp.dma_start(wring[:, b, 0:KD * CW].rearrange("p (k n) -> p k n", n=CW),
                             a["w_in"][2 * i + b] if isinstance(i, int) else
                             a["w_in"][bass.ds(2 * i + b, 1), :, :, :].rearrange("o p k n -> p (o k) n"))\
                    .then_inc(w_in[b], 16)

            def park(i, b):
                for t in range(T):
                    sp.wait_ge(drained[2 + t], 2 * i + b + 1)
                sp.nop(nofuse=True)
                sp.dma_start(proj[:, bass.ds((2 * i + b) * CW, CW)].rearrange("(t p) n -> p t n", p=P),
                             stage[:, b, :, :]).then_inc(s_parked[b], 16)

            sp.dma_start(hx[:, :, :], a["x"].rearrange("o (t p) d -> p (o t) d", p=P)).then_inc(s_x, 16)
            sp.dma_start(xT, a["xT"].rearrange("(k p) s -> p k s", p=P)).then_inc(s_xT, 16)
            w_in_chunk(0, 0)
            consts()
            w_in_chunk(0, 1)
            sp.dma_start(memT, a["memT"].rearrange("(k p) m -> p k m", p=P)).then_inc(s_mem, 16)
            sp.dma_start(memN, a["mem"].rearrange("o (m p) d -> p (o m) d", p=P)).then_inc(s_mem, 16)
            with sp.Fori(1, CHUNKS // 2) as i:
                for b in range(2):
                    w_in_chunk(i, b)
                    park(i - 1, b)
            for b in range(2):
                sp.wait_ge(full[5], CHUNKS + b - 1)
                sp.dma_start(wring[:, b, :].rearrange("p (k n) -> p k n", n=512),
                             a["w_mem_kv"].rearrange("o (k p) n -> p (o k) n", p=P)[:, :, b * 512:b * 512 + 512])\
                    .then_inc(w_in[b], 16)
                park(CHUNKS // 2 - 1, b)

            def chunk_sources():
                for name in ("w_o_mla", "w_o_ret", "w_o_cross"):
                    yield a[name].rearrange("o (k p) n -> p (o k) n", p=P), 1024, 4
                w_out = a["w_out"].rearrange("o (k p) n -> p (o k) n", p=P)
                for c in range(2):
                    yield w_out[:, :, c * 512:c * 512 + 512], 512, 8
                w_q = a["peer_w_q"].rearrange("o (k p) n -> p (o k) n", p=P)
                for c in range(4):
                    yield w_q[:, :, c * 512:c * 512 + 512], 512, 8

            def weights(t, c):
                b = c % 2
                if c >= 2:
                    sp.wait_ge(*computed(LAST_PRODUCT[c - 2], t))
                elif isinstance(t, int) and t == 0:
                    sp.wait_ge(full[6], 2 * (b + 1))
                else:
                    sp.wait_ge(*computed(LAST_PRODUCT[c - 2], t - 1))
                sp.nop(nofuse=True)
                if c == 0:
                    sp.dma_start(wring[:, b, 0:3 * HA * QK].rearrange("p (k n) -> p k n", n=HA * QK),
                                 a["w_uq"].rearrange("o (k p) n -> p (o k) n", p=P)).then_inc(w_in[b], 16)
                    sp.dma_start(wring[:, b, 2304:2304 + 1024], a["w_ukv"].rearrange("o p n -> (o p) n"))\
                        .then_inc(w_in[b], 16)
                else:
                    src, n, k = list(chunk_sources())[c - 1]
                    sp.dma_start(wring[:, b, :].rearrange("p (k n) -> p k n", n=n), src).then_inc(w_in[b], 16)

            def front(t):
                rows = bass.ds(t * P, P)
                first = isinstance(t, int) and t == 0
                if not first:
                    sp.wait_ge(*event("ro_done", t - 1))
                    sp.nop(nofuse=True)
                sp.dma_start(pa[:, :], proj[rows, 0:GATES]).then_inc(s_pa, 16)
                if not first:
                    sp.wait_ge(*in_sbuf(f"s{HA - 1}", t - 1))
                    sp.nop(nofuse=True)
                sp.dma_start(mask[:, :], a["mask"][rows, :]).then_inc(s_mask, 16)
                if not first:
                    sp.wait_ge(*event("handed", t - 1))
                    sp.nop(nofuse=True)
                sp.dma_start(h_next, a["x"].rearrange("o s d -> (o s) d")[rows, :]).then_inc(s_h, 16)
                weights(t, 0)
                weights(t, 1)
                for br in range(3):
                    if br or not first:
                        sp.wait_ge(*in_sbuf(f"y{(br - 1) % 3}b", t if br else t - 1))
                        sp.nop(nofuse=True)
                    sp.dma_start(gt[:, :], proj[rows, GATES + br * D:GATES + br * D + D]).then_inc(s_gt, 16)
                    weights(t, 2 + br)
                for c in range(5, CHUNKS_PER_TILE):
                    weights(t, c)

            def store(t):
                sp.wait_ge(s_taken, t + 2)
                sp.nop(nofuse=True)
                sp.dma_start(out.rearrange("o s d -> (o s) d")[bass.ds(t * P, P), :], res[:, :]).then_inc(s_out, 16)
                sp.wait_ge(s_out, 16 * (t + 1))
                sp.nop(nofuse=True)

            sp.wait_ge(s_parked[0], 16 * (CHUNKS // 2))
            sp.wait_ge(s_parked[1], 16 * (CHUNKS // 2))
            sp.wait_ge(s_ready, 1)
            front(0)
            with sp.Fori(1, T) as t:
                front(t)
                store(t - 1)
            store(T - 1)

        @block.gpsimd
        def _(pool):
            def gather(dst, table, t, h, k, arrived, used):
                n = t * (HP * TOP) + h * TOP + k
                pool.wait_ge(used, n + 1)
                pool.nop(nofuse=True)
                pool.indirect_dma_start(dst[:, k % RING, :], None, table, bass.IndirectOffsetOnAxis(
                    ap=idx[:, h * TOP + k:h * TOP + k + 1], axis=0)).then_inc(arrived[k % RING], 16)

            def peer(t):
                pool.wait_ge(*event("handed", t))
                for h in range(HP + 1):
                    for k in range(TOP):
                        if h < HP:
                            gather(ub, a["peer_u"], t, h, k, u_in, dots)
                        if h > 0:
                            gather(vb, a["peer_v"], t, h - 1, k, v_in, v_used)

            peer(0)
            with pool.Fori(1, T) as t:
                peer(t)

        @block.scalar
        def _(act):
            A = nc.scalar.activation

            def setup():
                act.wait_ge(s_x, 16)
                for t in range(T):
                    if t:
                        act.wait_ge(s_sums, t)
                    A(tmp[:, :], hx[:, t, :], ACT.Square, scale=D ** -0.5,
                      accum_out=rstd_x[:, t:t + 1]).then_inc(s_sums, 1)
                act.wait_ge(s_mem, 32)
                for m in range(2):
                    act.wait_ge(s_sums, T + m)
                    A(tmp[:, :], memN[:, m, :], ACT.Square, scale=D ** -0.5,
                      accum_out=rstd_m[:, m:m + 1]).then_inc(s_sums, 1)
                act.wait_ge(s_angles, 1)
                for i in range(2):
                    A(rope[:, :, i, :], work[:, 192 * (1 + i):192 * (2 + i)].rearrange("p (t n) -> p t n", n=48),
                      ACT.Sin).then_inc(s_rope, 1)

            def drain_projection(i):
                for b in range(2):
                    for t in (0, 2):
                        act.wait_ge(full[2 + t], 2 * i + b + 1)
                        if not isinstance(i, int):
                            act.wait_ge(s_parked[b], 16 * i)
                        A(stage[:, b, t, :], ps[2 + t][:, 0:CW], ACT.Copy, scale=rstd_x[:, t:t + 1])\
                            .then_inc(drained[2 + t], 1)

            setup()
            act.wait_ge(s_rstd, 1)
            drain_projection(0)
            with act.Fori(1, CHUNKS // 2) as i:
                drain_projection(i)

            def gate_tanh(t, br):
                act.wait_ge(s_gt, 16 * (3 * t + br + 1))
                A(gt[:, :], gt[:, :], ACT.Tanh, scale=0.5).then_inc(ev["gate_tanh"], 1)

            def front(t):
                act.wait_ge(s_pa, 16 * (t + 1))
                parts = [(C_Q, QR), (C_KV, KVR)] + [(X_Q + h * XD, XD) for h in range(HX)]
                junk = [0, QR] + [QR + KVR + h * XD for h in range(HX)]
                for j, (at, n) in enumerate(parts):
                    A(tmp[:, junk[j]:junk[j] + n], pa[:, at:at + n], ACT.Square, scale=n ** -0.5,
                      accum_out=c_st[:, j:j + 1]).then_inc(ev["c_stats"], 1)
                A(rth[:, :], pa[:, R_G:R_G + 512], ACT.Tanh, scale=0.5).then_inc(ev["rg_tanh"], 1)
                act.wait_ge(*event("c_rstd", t))
                for j, (at, n) in enumerate(parts):
                    A(pa[:, at:at + n], pa[:, at:at + n], ACT.Copy, scale=c_st[:, j:j + 1]).then_inc(ev["c_normed"], 1)
                act.wait_ge(*computed("cT", t))
                bank = ps[BANK["cT"]]
                for j in range(4):
                    ins = A(cT[:, j, :], bank[:, j * P:(j + 1) * P], ACT.Copy, scale=gcols[:, 2 * KD + j:2 * KD + j + 1])
                ins.then_inc(DRAINED["cT"], 1)
                act.wait_ge(*computed("xqT", t))
                bank = ps[BANK["xqT"]]
                A(xqT[:, :, :], bank[:, :], ACT.Copy, scale=gcols[:, 2 * KD + 4:2 * KD + 5]).then_inc(DRAINED["xqT"], 1)
                yield
                act.wait_ge(*computed("ro", t))
                bank = ps[BANK["ro"]]
                for h in range(HR):
                    ins = A(ob[:, h * RV:(h + 1) * RV], bank[:, h * RV:(h + 1) * RV], ACT.Square, scale=RV ** -0.5,
                            accum_out=ro_st[:, h:h + 1])
                    ins.then_inc(ev["ro_stats"], 1)
                nc.scalar.copy(ro[:, :, :], bank[:, :]).then_inc(DRAINED["ro"], 1)
                yield
                for i in range(2):
                    act.wait_ge(*computed(f"qT{i}", t))
                    bank = ps[BANK[f"qT{i}"]]
                    nc.scalar.copy(qT[0:QK, 4 * i:4 * i + 4, :], bank[0:QK, :]).then_inc(DRAINED[f"qT{i}"], 1)
                for i in range(2):
                    act.wait_ge(*computed(f"kT{i}", t))
                    bank = ps[BANK[f"kT{i}"]]
                    act.nop(nofuse=True)
                    nc.scalar.copy(kTh[0:QK, 4 * i:4 * i + 4, bass.ds(t * P, P)],
                                   bank[0:QK, :].rearrange("p (h n) -> p h n", n=P)).then_inc(DRAINED[f"kT{i}"], 1)
                for h in range(HA):
                    act.wait_ge(*in_sbuf(f"s{h}", t))
                    A(ssb[:, h % 2, :], ssb[:, h % 2, :], ACT.Exp, scale=-1.0, bias=nmax[:, h:h + 1],
                      accum_out=l_att[:, h:h + 1]).then_inc(ev["p_exp"], 1)
                    act.wait_ge(*computed(f"pT{h}", t))
                    bank = ps[BANK[f"pT{h}"]]
                    nc.scalar.copy(pT[:, h % 2, :], bank[:, :]).then_inc(DRAINED[f"pT{h}"], 1)
                    if h == 3:
                        yield
                yield
                act.wait_ge(*computed("oT", t))
                bank = ps[BANK["oT"]]
                nc.scalar.copy(oT[:, :, :], bank[:, :]).then_inc(DRAINED["oT"], 1)
                gate_tanh(t, 0)
                act.wait_ge(*computed("roT", t))
                bank = ps[BANK["roT"]]
                A(oT[:, :, :], bank[:, :], ACT.Copy, scale=0.5).then_inc(DRAINED["roT"], 1)
                gate_tanh(t, 1)
                yield
                for h in range(HX):
                    act.wait_ge(*event("mem_max", t, h // 2 + 1))
                    ins = A(ssb[:, h // 2, (h % 2) * M:(h % 2) * M + M], ps[6 + h // 2][:, (h % 2) * M:(h % 2) * M + M],
                            ACT.Exp, scale=MEM_SCALE, bias=mmax[:, h:h + 1], accum_out=l_mem[:, h:h + 1])
                    if h % 2:
                        ins.then_inc(DRAINED[f"ms{h // 2}"], 1)
                for i in range(2):
                    act.wait_ge(*computed(f"mp{i}", t))
                    bank = ps[BANK[f"mp{i}"]]
                    nc.scalar.copy(pT[:, i, :], bank[:, :]).then_inc(DRAINED[f"mp{i}"], 1)
                act.wait_ge(*computed("moT", t))
                bank = ps[BANK["moT"]]
                nc.scalar.copy(oT[:, :, :], bank[:, :]).then_inc(DRAINED["moT"], 1)
                gate_tanh(t, 2)
                yield
                for i in range(2):
                    act.wait_ge(*computed(f"mT{i}", t))
                    bank = ps[BANK[f"mT{i}"]]
                    A(mT[:, 4 * i:4 * i + 4, :], bank[:, :], ACT.Copy, scale=0.5).then_inc(DRAINED[f"mT{i}"], 1)
                act.wait_ge(*in_sbuf("ha", t))
                act.wait_ge(*in_sbuf("hb", t))
                A(tmp[:, :], h_next, ACT.Square, scale=D ** -0.5, accum_out=f_st).then_inc(ev["f_stats"], 1)
                act.wait_ge(*event("f_rstd", t))
                A(xn_next, h_next, ACT.Copy, scale=f_st).then_inc(ev["xn_scaled"], 1)
                for i in range(2):
                    act.wait_ge(*computed(f"xT{i}", t))
                    bank = ps[BANK[f"xT{i}"]]
                    nc.scalar.copy(mT[:, 4 * i:4 * i + 4, :], bank[:, :]).then_inc(DRAINED[f"xT{i}"], 1)
                yield
                for c in range(4):
                    act.wait_ge(*computed(f"pq{c}", t))
                    bank = ps[BANK[f"pq{c}"]]
                    nc.scalar.copy(pqT[:, c % 2, :], bank[:, :]).then_inc(DRAINED[f"pq{c}"], 1)
                    act.wait_ge(*computed(f"sc{c}", t))
                    bank = ps[BANK[f"sc{c}"]]
                    nc.scalar.copy(scores[:, 4 * c:4 * c + 4, :], bank[:, :]).then_inc(DRAINED[f"sc{c}"], 1)
                yield
                act.wait_ge(*event("best_sub", t))
                A(besub, besub, ACT.Exp).then_inc(ev["best_exp"], 1)

            def peer_tanh(t, h):
                act.wait_ge(gelu_in, t * HP + h + 1)
                A(acts[:, 2, :], acts[:, 2, :], ACT.Tanh, scale=GELU_A).then_inc(gelu_tanh, 1)

            def peer_diag(t, h):
                act.wait_ge(s_wts, t * HP + h + 1)
                for k in range(TOP):
                    n = t * (HP * TOP) + h * TOP + k
                    act.wait_ge(v_used, n + 1)
                    A(diag[:, k % RING, :], ident, ACT.Copy, scale=wts[:, h % 2, k:k + 1]).then_inc(s_diag, 1)

            def peer_head(t, h):
                if h > 0:
                    peer_diag(t, h - 1)
                if h < HP:
                    peer_tanh(t, h)

            weave(front, peer_head, act)

        @block.tensor
        def _(pe):
            mm, tr = nc.tensor.matmul, nc.tensor.transpose

            def project(i):
                for b in range(2):
                    pe.wait_ge(w_in[b], 16 * (i + 1))
                    w = wring[:, b, 0:KD * CW].rearrange("p (k n) -> p k n", n=CW)
                    for t in range(T):
                        if b or not isinstance(i, int):
                            pe.wait_ge(drained[2 + t], 2 * i + b)
                        for k in range(KD):
                            ins = mm(ps[2 + t][:, 0:CW], xT[:, k, t * P:(t + 1) * P], w[:, k, :],
                                     start=(k == 0), stop=(k == KD - 1))
                        ins.then_inc(full[2 + t], 1)

            pe.wait_ge(s_const, 16 * CONSTANT_LOADS)
            pe.wait_ge(s_rstd, 1)
            project(0)
            with pe.Fori(1, CHUNKS // 2) as i:
                project(i)
            pe.wait_ge(s_mem_g, 1)
            for j in range(4):
                c, m = divmod(j, 2)
                pe.wait_ge(w_in[c], 16 * (CHUNKS // 2 + 1))
                if j:
                    pe.wait_ge(drained[6], j)
                w = wring[:, c, :].rearrange("p (k n) -> p k n", n=512)
                for k in range(KD):
                    ins = mm(ps[6][:, :], memT[:, k, m * P:(m + 1) * P], w[:, k, :], start=(k == 0), stop=(k == KD - 1))
                ins.then_inc(full[6], 1)
                pe.wait_ge(s_mem_keys, j + 1)
                if j:
                    pe.wait_ge(drained[7], j)
                for h in range(2):
                    ins = tr(ps[7][:, h * P:(h + 1) * P], tmp[:, 256 * h:256 * h + XD], ident)
                ins.then_inc(full[7], 1)

            def weights(t, c):
                b = c % 2
                loads = CHUNKS // 2 + 1 + t * (6 if b == 0 else 5)
                order = c // 2 + (2 if b == 0 else 1)
                pe.wait_ge(w_in[b], 16 * (loads + order))
                return wring[:, b, :]

            def turn(bank, src, n, rows=P):
                for j in range(n):
                    ins = tr(bank[0:rows, j * P:(j + 1) * P], src(j), ident)
                return ins

            def branch_out(t, c, names, src):
                pe.wait_ge(*in_sbuf(src, t))
                w = weights(t, c).rearrange("p (k n) -> p k n", n=1024)
                for i, name in enumerate(names):
                    pe.wait_ge(*bank_free(name, t))
                    bank = ps[BANK[name]]
                    for k in range(4):
                        ins = mm(bank[:, :], oT[:, k, :], w[:, k, i * 512:i * 512 + 512], start=(k == 0), stop=(k == 3))
                    ins.then_inc(FULL[name], 1)

            def front(t):
                pe.wait_ge(*event("c_normed", t))
                pe.wait_ge(*bank_free("cT", t))
                bank = ps[BANK["cT"]]
                turn(bank, lambda j: pa[:, C_Q + j * P:C_Q + (j + 1) * P], 4).then_inc(FULL["cT"], 1)
                pe.wait_ge(*bank_free("xqT", t))
                bank = ps[BANK["xqT"]]
                turn(bank, lambda j: pa[:, X_Q + j * P:X_Q + (j + 1) * P], 4).then_inc(FULL["xqT"], 1)
                pe.wait_ge(*in_sbuf("cT", t))
                w = weights(t, 0)
                wq = w[:, 0:2304].rearrange("p (k n) -> p k n", n=HA * QK)
                for i in range(2):
                    pe.wait_ge(*bank_free(f"q{i}", t))
                    bank = ps[BANK[f"q{i}"]]
                    for k in range(3):
                        ins = mm(bank[:, 0:384], cT[:, k, :], wq[:, k, i * 384:i * 384 + 384], start=(k == 0), stop=(k == 2))
                    ins.then_inc(FULL[f"q{i}"], 1)
                for i in range(2):
                    pe.wait_ge(*bank_free(f"kv{i}", t))
                    bank = ps[BANK[f"kv{i}"]]
                    mm(bank[:, :], cT[:, 3, :], w[:, 2304 + 512 * i:2304 + 512 * i + 512], start=True, stop=True)\
                        .then_inc(FULL[f"kv{i}"], 1)
                pe.wait_ge(*event("r_roped", t))
                for name, at in (("rqT", R_Q), ("rkT", R_K)):
                    pe.wait_ge(*bank_free(name, t))
                    bank = ps[BANK[name]]
                    pe.nop(nofuse=True)
                    turn(bank, lambda j: pa[:, at + j * RK:at + (j + 1) * RK], 4, RK).then_inc(FULL[name], 1)
                yield
                pe.wait_ge(*in_sbuf("rqT", t))
                pe.wait_ge(*in_sbuf("rkT", t))
                pe.wait_ge(*bank_free("rin", t))
                bank = ps[BANK["rin"]]
                for h in range(HR):
                    ins = mm(bank[:, h * P:(h + 1) * P], rkT[:, h, :], rqT[:, h, :], start=True, stop=True)
                ins.then_inc(FULL["rin"], 1)
                pe.wait_ge(*in_sbuf("rin", t))
                pe.wait_ge(*bank_free("ro", t))
                bank = ps[BANK["ro"]]
                for h in range(HR):
                    o = bank[:, h * RV:(h + 1) * RV]
                    mm(o, inner[:, h, :], pa[:, R_V + h * RV:R_V + (h + 1) * RV], start=True, stop=False)
                    ins = mm(o, rxT[:, h, :], state[:, h, :], start=False, stop=True)
                ins.then_inc(FULL["ro"], 1)
                pe.wait_ge(*event("kz", t))
                pe.wait_ge(*bank_free("rinc", t))
                bank = ps[BANK["rinc"]]
                for h in range(HR):
                    ins = mm(bank[0:RK, h * RV:(h + 1) * RV], kz[:, h, :], pa[:, R_V + h * RV:R_V + (h + 1) * RV],
                             start=True, stop=True)
                ins.then_inc(FULL["rinc"], 1)
                yield
                pe.wait_ge(*event("qk_roped", t))
                for i, name in enumerate(("qT0", "qT1", "kT0", "kT1")):
                    pe.wait_ge(*bank_free(name, t))
                    bank = ps[BANK[name]]
                    turn(bank, lambda j: qk[:, 4 * i + j, :], 4, QK).then_inc(FULL[name], 1)
                pe.wait_ge(*in_sbuf("kT1", t))
                pe.wait_ge(*in_sbuf("qT1", t))
                pe.wait_ge(*in_sbuf("kT0", t))

                def score(h):
                    pe.wait_ge(*bank_free(f"s{h}", t))
                    bank = ps[BANK[f"s{h}"]]
                    mm(bank[:, :], qT[0:QK, h, :], kTh[0:QK, h, :], start=True, stop=True).then_inc(FULL[f"s{h}"], 1)

                score(0)
                o = None
                for h in range(HA):
                    if h + 1 < HA:
                        score(h + 1)
                    pe.wait_ge(*event("p_exp", t, h + 1))
                    pe.wait_ge(*bank_free(f"pT{h}", t))
                    bank = ps[BANK[f"pT{h}"]]
                    turn(bank, lambda j: ssb[:, h % 2, j * P:(j + 1) * P], 4).then_inc(FULL[f"pT{h}"], 1)
                    pe.wait_ge(*in_sbuf(f"pT{h}", t))
                    if h == 0:
                        pe.wait_ge(*bank_free("o", t))
                        o = ps[BANK["o"]]
                    for j in range(T):
                        ins = mm(o[:, h * VD:(h + 1) * VD], pT[:, h % 2, j * P:(j + 1) * P],
                                 vc[:, j, h * VD:(h + 1) * VD], start=(j == 0), stop=(j == T - 1))
                    if h == 3:
                        yield
                ins.then_inc(FULL["o"], 1)
                yield
                pe.wait_ge(*in_sbuf("o", t))
                pe.wait_ge(*bank_free("oT", t))
                turn(ps[BANK["oT"]], lambda j: ob[:, j * P:(j + 1) * P], 4).then_inc(FULL["oT"], 1)
                branch_out(t, 1, ("y0a", "y0b"), "oT")
                pe.wait_ge(*event("ro_done", t))
                pe.wait_ge(*bank_free("roT", t))
                turn(ps[BANK["roT"]], lambda j: ro[:, j, :], 4).then_inc(FULL["roT"], 1)
                branch_out(t, 2, ("y1a", "y1b"), "roT")
                yield
                pe.wait_ge(*in_sbuf("xqT", t))
                for i in range(2):
                    pe.wait_ge(*bank_free(f"ms{i}", t))
                    bank = ps[BANK[f"ms{i}"]]
                    for h in range(2):
                        ins = mm(bank[:, h * M:h * M + M], xqT[:, 2 * i + h, :], mkT[:, 2 * i + h, :], start=True, stop=True)
                    ins.then_inc(FULL[f"ms{i}"], 1)
                for i in range(2):
                    pe.wait_ge(*in_sbuf(f"ms{i}", t))
                    pe.wait_ge(*bank_free(f"mp{i}", t))
                    bank = ps[BANK[f"mp{i}"]]
                    turn(bank, lambda j: ssb[:, i, j * P:(j + 1) * P], 4).then_inc(FULL[f"mp{i}"], 1)
                pe.wait_ge(*in_sbuf("mp0", t))
                pe.wait_ge(*in_sbuf("mp1", t))
                pe.wait_ge(*bank_free("mo", t))
                bank = ps[BANK["mo"]]
                for h in range(HX):
                    for j in range(2):
                        ins = mm(bank[:, h * XD:(h + 1) * XD], pT[:, h // 2, (h % 2) * M + j * P:(h % 2) * M + (j + 1) * P],
                                 mv[:, j, h, :], start=(j == 0), stop=(j == 1))
                ins.then_inc(FULL["mo"], 1)
                pe.wait_ge(*in_sbuf("mo", t))
                pe.wait_ge(*bank_free("moT", t))
                turn(ps[BANK["moT"]], lambda j: ob[:, j * P:(j + 1) * P], 4).then_inc(FULL["moT"], 1)
                branch_out(t, 3, ("y2a", "y2b"), "moT")
                yield
                pe.wait_ge(*event("merged", t))
                for i in range(2):
                    pe.wait_ge(*bank_free(f"mT{i}", t))
                    turn(ps[BANK[f"mT{i}"]], lambda j: merged[:, (4 * i + j) * P:(4 * i + j + 1) * P], 4).then_inc(FULL[f"mT{i}"], 1)
                pe.wait_ge(*in_sbuf("mT0", t))
                pe.wait_ge(*in_sbuf("mT1", t))
                for c, name in ((4, "ha"), (5, "hb")):
                    w = weights(t, c).rearrange("p (k n) -> p k n", n=512)
                    pe.wait_ge(*bank_free(name, t))
                    bank = ps[BANK[name]]
                    for k in range(KD):
                        ins = mm(bank[:, :], mT[:, k, :], w[:, k, :], start=(k == 0), stop=(k == KD - 1))
                    ins.then_inc(FULL[name], 1)
                pe.wait_ge(*event("xn_done", t))
                for i in range(2):
                    pe.wait_ge(*bank_free(f"xT{i}", t))
                    turn(ps[BANK[f"xT{i}"]], lambda j: xn_next[:, (4 * i + j) * P:(4 * i + j + 1) * P], 4).then_inc(FULL[f"xT{i}"], 1)
                pe.wait_ge(*in_sbuf("xT0", t))
                pe.wait_ge(*in_sbuf("xT1", t))
                yield
                for c in range(4):
                    w = weights(t, 6 + c).rearrange("p (k n) -> p k n", n=512)
                    pe.wait_ge(*bank_free(f"pq{c}", t))
                    bank = ps[BANK[f"pq{c}"]]
                    for j in range(4):
                        for k in range(KD):
                            ins = mm(bank[:, j * P:(j + 1) * P], w[:, k, j * P:(j + 1) * P], mT[:, k, :],
                                     start=(k == 0), stop=(k == KD - 1))
                    ins.then_inc(FULL[f"pq{c}"], 1)
                    pe.wait_ge(*in_sbuf(f"pq{c}", t))
                    pe.wait_ge(*bank_free(f"sc{c}", t))
                    bank = ps[BANK[f"sc{c}"]]
                    for j in range(4):
                        ins = mm(bank[:, j * P:(j + 1) * P], pqT[:, c % 2, j * P:(j + 1) * P], keysT[:, 4 * c + j, :],
                                 start=True, stop=True)
                    ins.then_inc(FULL[f"sc{c}"], 1)
                yield

            def peer_head(t, h):
                if h == 0:
                    return
                h -= 1
                if h == 0:
                    pe.wait_ge(s_taken, t + 1)
                for k in range(TOP):
                    n = t * (HP * TOP) + h * TOP + k
                    pe.wait_ge(s_diag, n + 1)
                    pe.wait_ge(v_in[k % RING], 16 * (t * (HP * TOP // RING) + h * (TOP // RING) + k // RING + 1))
                    for i in range(2):
                        ins = mm(ps[i][:, :], diag[:, k % RING, :], vb[:, k % RING, i * 512:i * 512 + 512],
                                 start=(h == 0 and k == 0), stop=(h == HP - 1 and k == TOP - 1))
                    ins.then_inc(v_used, 1)

            weave(front, peer_head, pe)

        @block.vector
        def _(dve):
            V = nc.vector
            def make_link(chain, base):
                state_ = {"n": 0}

                def link(ins, hold=False):
                    state_["n"] += 1
                    ins.then_inc(chain, 1)
                    dve.wait_ge(chain, base + state_["n"])
                    if hold:
                        dve.nop(nofuse=True)
                return link, state_

            def rsqrt(link, x, n):
                y, s = nwt[:, 0:n], nwt[:, 16:16 + n]
                link(V.tensor_scalar(x, x, EPS, None, ALU.add))
                link(V.tensor_scalar(y.bitcast(U32), x.bitcast(U32), 1, None, ALU.logical_shift_right))
                link(V.tensor_scalar(y.bitcast(I32), y.bitcast(I32), -1.0, 1597463007.0, ALU.mult, ALU.add))
                for _ in range(3):
                    link(V.scalar_tensor_tensor(out=s, in0=y, scalar=-0.5, in1=y, op0=ALU.mult, op1=ALU.mult))
                    link(V.tensor_tensor(s, s, x, ALU.mult))
                    link(V.scalar_tensor_tensor(out=y, in0=s, scalar=1.5, in1=y, op0=ALU.add, op1=ALU.mult))
                return y

            def rotate(link, x, half, cos, sin, heads):
                x1, x2 = x[:, :, 0:half], x[:, :, half:2 * half]
                c = cos.rearrange("p (o n) -> p o n", o=1).broadcast_to((P, heads, half))
                s = sin.rearrange("p (o n) -> p o n", o=1).broadcast_to((P, heads, half))
                r = [tmp[:, 256 * i:256 * i + heads * half].rearrange("p (h n) -> p h n", n=half) for i in range(4)]
                V.tensor_tensor(r[0], x1, c, ALU.mult)
                V.tensor_tensor(r[1], x2, s, ALU.mult)
                V.tensor_tensor(r[2], x1, s, ALU.mult)
                link(V.tensor_tensor(r[3], x2, c, ALU.mult))
                V.tensor_tensor(x1, r[0], r[1], ALU.subtract)
                return V.tensor_tensor(x2, r[2], r[3], ALU.add)

            link, _n = make_link(dve_chain, 0)
            V.memset(state[:, :, :], 0.0).then_inc(v_used, RING)
            V.memset(vc[:, :, :], 0.0).then_inc(s_taken, 1)
            V.memset(acts[:, 4, :], 0.0).then_inc(dots, RING)
            dve.wait_ge(s_const, 16 * CONSTANT_LOADS)
            dve.wait_ge(s_xT, 16)
            for k in range(KD):
                V.tensor_scalar(xT[:, k, :], xT[:, k, :], gcols[:, k:k + 1], None, ALU.mult)
            dve.wait_ge(s_sums, 4)
            y = rsqrt(link, rstd_x, T)
            V.tensor_copy(rstd_x, y).then_inc(s_rstd, 1)
            dve.wait_ge(s_rstd, 1)
            ang = work[:, 0:192].rearrange("p (t n) -> p t n", n=48)
            sn = work[:, 384:576].rearrange("p (t n) -> p t n", n=48)
            cs = work[:, 192:384].rearrange("p (t n) -> p t n", n=48)
            turns = work[:, 576:768].rearrange("p (t n) -> p t n", n=48)
            link(V.tensor_copy(posf, posi[:, :]))
            link(V.tensor_tensor(ang, posf.rearrange("p (t o) -> p t o", o=1).broadcast_to((P, T, 48)),
                                 cst[:, K_INV:K_INV + 48].rearrange("p (o n) -> p o n", o=1).broadcast_to((P, T, 48)),
                                 ALU.mult))
            link(V.tensor_scalar(turns, ang, 1.0 / TWO_PI, ROUND, ALU.mult, ALU.add))
            link(V.tensor_scalar(turns, turns, ROUND, None, ALU.subtract))
            for part in (TP1, TP2, TP3):
                link(V.scalar_tensor_tensor(out=ang, in0=turns, scalar=-part, in1=ang, op0=ALU.mult, op1=ALU.add))
            link(V.tensor_scalar(sn, ang, PI_LOW, -PI_LOW, ALU.min, ALU.max))
            link(V.tensor_scalar(ang, ang, TWO_PI / 4, None, ALU.add))
            link(V.tensor_scalar(turns, ang, PI_LOW, -TWO_PI, ALU.is_gt, ALU.mult))
            link(V.tensor_tensor(cs, ang, turns, ALU.add))
            V.tensor_scalar(cs, cs, PI_LOW, -PI_LOW, ALU.min, ALU.max).then_inc(s_angles, 1)
            dve.wait_ge(s_mem, 32)
            for k in range(KD):
                ins = V.tensor_scalar(memT[:, k, :], memT[:, k, :], gcols[:, KD + k:KD + k + 1], None, ALU.mult)
            ins.then_inc(s_mem_g, 1)
            dve.wait_ge(s_sums, 6)
            y = rsqrt(link, rstd_m, 2)
            link(V.tensor_copy(rstd_m, y))

            def drain_projection(i):
                for b in range(2):
                    for t in (1, 3):
                        if not isinstance(i, int):
                            dve.wait_ge(s_parked[b], 16 * i)
                        dve.wait_ge(full[2 + t], 2 * i + b + 1)
                        V.tensor_scalar(stage[:, b, t, :], ps[2 + t][:, 0:CW], rstd_x[:, t:t + 1], None, ALU.mult)\
                            .then_inc(drained[2 + t], 1)

            drain_projection(0)
            with dve.Fori(1, CHUNKS // 2) as i:
                drain_projection(i)
            for j in range(4):
                c, m = divmod(j, 2)
                dve.wait_ge(full[6], j + 1)
                if j:
                    dve.wait_ge(full[7], j)
                dst = mv[:, m, 2 * c:2 * c + 2, :]
                kv = ps[6][:, :].rearrange("p (h n) -> p h n", n=2 * XD)
                V.tensor_scalar(dst, kv[:, :, XD:2 * XD], rstd_m[:, m:m + 1], None, ALU.mult)
                keys = tmp[:, 0:512].rearrange("p (h n) -> p h n", n=2 * XD)[:, :, 0:XD]
                sqk = tmp[:, 512:768].rearrange("p (h n) -> p h n", n=XD)
                V.tensor_scalar(keys, kv[:, :, 0:XD], rstd_m[:, m:m + 1], None, ALU.mult).then_inc(drained[6], 1)
                dve.wait_ge(drained[6], j + 1)
                link(V.tensor_tensor(sqk, keys, keys, ALU.mult))
                link(V.tensor_reduce(mem_st, sqk, AX.X, ALU.add))
                link(V.tensor_scalar(mem_st, mem_st, 1.0 / XD, None, ALU.mult))
                y = rsqrt(link, mem_st, 2)
                link(V.tensor_tensor(keys, keys, y.rearrange("p (h o) -> p h o", o=1).broadcast_to((P, 2, XD)), ALU.mult))
                V.tensor_tensor(keys, keys, mkrow[:, :].rearrange("p (o n) -> p o n", o=1).broadcast_to((P, 2, XD)),
                                ALU.mult).then_inc(s_mem_keys, 1)
                dve.wait_ge(full[7], j + 1)
                V.tensor_copy(mkT[:, 2 * c:2 * c + 2, m * P:(m + 1) * P],
                              ps[7][:, 0:256].rearrange("p (h n) -> p h n", n=P)).then_inc(drained[7], 1)
            dve.wait_ge(s_rope, 2)
            V.memset(kT[:, :], 0.0).then_inc(s_ready, 1)
            setup_links = _n["n"]

            def topk(link, rows, heads, vals, inds):
                for h in range(heads):
                    ins = V.max(vals[:, h, 0:8], rows[:, h, :])
                link(ins, hold=True)
                for h in range(heads):
                    V.max_index(inds[:, h, 0:8], vals[:, h, 0:8], rows[:, h, :])
                for h in range(heads):
                    ins = V.match_replace(rows[:, h, :], vals[:, h, 0:8], rows[:, h, :], -3.0e38)
                link(ins, hold=True)
                for h in range(heads):
                    ins = V.max(vals[:, h, 8:16], rows[:, h, :])
                link(ins, hold=True)
                for h in range(heads):
                    ins = V.max_index(inds[:, h, 8:16], vals[:, h, 8:16], rows[:, h, :])
                link(ins)

            def merge(t, br, name):
                dve.wait_ge(*event("gate_tanh", t, br + 1))
                link = links["link"]
                for i, bank in enumerate((f"{name}a", f"{name}b")):
                    part = slice(i * 512, i * 512 + 512)
                    dve.wait_ge(*computed(bank, t))
                    y = ps[BANK[bank]]
                    dst = merged if br == 0 else tmp
                    ins = V.scalar_tensor_tensor(out=dst[:, part], in0=gt[:, part], scalar=1.0, in1=y[:, :],
                                                 op0=ALU.add, op1=ALU.mult)
                    ins.then_inc(DRAINED[bank], 1)
                dve.wait_ge(*in_sbuf(f"{name}a", t))
                dve.wait_ge(*in_sbuf(f"{name}b", t))
                if br == 1:
                    link(V.tensor_tensor(merged[:, :], merged[:, :], tmp[:, :], ALU.add))
                if br == 2:
                    V.tensor_tensor(merged[:, :], merged[:, :], tmp[:, :], ALU.add).then_inc(ev["merged"], 1)

            links = {}

            def front(t):
                link, n = make_link(dve_chain, setup_links + t * DVE_LINKS)
                links["link"] = link
                link(V.tensor_copy(ropet[:, :, :].rearrange("p i n -> p (i n)").rearrange("p (o n) -> p o n", o=1),
                                   rope[:, :, :, :].rearrange("p t i n -> p t (i n)")[:, bass.ds(t, 1), :]))
                cos_a, sin_a = ropet[:, 0, 0:16], ropet[:, 1, 0:16]
                cos_r, sin_r = ropet[:, 0, 16:48], ropet[:, 1, 16:48]
                dve.wait_ge(*event("c_stats", t))
                y = rsqrt(link, c_st, 6)
                V.tensor_copy(c_st, y).then_inc(ev["c_rstd"], 1)
                dve.wait_ge(*event("c_normed", t))
                r = pa[:, R_Q:R_Q + 2 * HR * RK].rearrange("p (h n) -> p h n", n=RK)
                rotate(link, r, 32, cos_r, sin_r, 2 * HR).then_inc(ev["r_roped"], 1)
                dve.wait_ge(*event("r_roped", t))
                V.tensor_tensor(kz[:, :, :], r[:, HR:2 * HR, :],
                                zeta.rearrange("p (h o) -> p h o", o=1).broadcast_to((P, HR, RK)), ALU.mult)\
                    .then_inc(ev["kz"], 1)
                for i in range(2):
                    dve.wait_ge(*computed(f"q{i}", t))
                    bank = ps[BANK[f"q{i}"]]
                    V.tensor_copy(qk[:, 4 * i:4 * i + 4, :], bank[:, 0:384]).then_inc(DRAINED[f"q{i}"], 1)
                for i in range(2):
                    dve.wait_ge(*computed(f"kv{i}", t))
                    bank = ps[BANK[f"kv{i}"]][:, :].rearrange("p (h n) -> p h n", n=NOPE + VD)
                    V.tensor_copy(qk[:, HA + 4 * i:HA + 4 * i + 4, 0:NOPE], bank[:, :, 0:NOPE])
                    V.tensor_copy(vc[:, bass.ds(t, 1), 256 * i:256 * i + 256].rearrange("p o (h n) -> p (o h) n", n=VD),
                                  bank[:, :, NOPE:NOPE + VD]).then_inc(DRAINED[f"kv{i}"], 1)
                link(V.tensor_copy(qk[:, HA:2 * HA, NOPE:QK], pa[:, C_KR:C_KR + ROPE].rearrange(
                    "p (o n) -> p o n", o=1).broadcast_to((P, HA, ROPE))))
                yield
                dve.wait_ge(*computed("rqT", t))
                bank = ps[BANK["rqT"]]
                V.tensor_copy(rqT[:, :, :], bank[0:RK, :])
                V.tensor_tensor(rxT[:, :, :], bank[0:RK, :], xiT, ALU.mult).then_inc(DRAINED["rqT"], 1)
                dve.wait_ge(*computed("rkT", t))
                bank = ps[BANK["rkT"]]
                V.tensor_scalar(rkT[:, :, :], bank[0:RK, :], RK ** -0.5, None, ALU.mult).then_inc(DRAINED["rkT"], 1)
                dve.wait_ge(*computed("rin", t))
                bank = ps[BANK["rin"]]
                V.tensor_tensor(inner[:, :, :], bank[:, :], decayT, ALU.mult).then_inc(DRAINED["rin"], 1)
                link(V.tensor_tensor(sq, qk, qk, ALU.mult))
                link(V.tensor_reduce(qk_st, sq, AX.X, ALU.add))
                link(V.tensor_scalar(qk_st, qk_st, 1.0 / QK, None, ALU.mult))
                y = rsqrt(link, qk_st, 2 * HA)
                link(V.tensor_tensor(qk, qk, y.rearrange("p (h o) -> p h o", o=1).broadcast_to((P, 2 * HA, QK)), ALU.mult))
                for i in range(2):
                    half = qk[:, HA * i:HA * i + HA, :]
                    ins = V.tensor_tensor(half, half, qkrow[:, i, :].rearrange("p (o n) -> p o n", o=1)
                                          .broadcast_to((P, HA, QK)), ALU.mult)
                link(ins)
                rotate(link, qk[:, :, NOPE:QK], ROPE // 2, cos_a, sin_a, 2 * HA).then_inc(ev["qk_roped"], 1)
                dve.wait_ge(*computed("rinc", t))
                bank = ps[BANK["rinc"]]
                for h in range(HR):
                    ins = V.scalar_tensor_tensor(out=state[:, h, :], in0=state[:, h, :], scalar=CHUNK_DECAY[h],
                                                 in1=bank[0:RK, h * RV:(h + 1) * RV], op0=ALU.mult, op1=ALU.add)
                ins.then_inc(DRAINED["rinc"], 1)
                yield
                dve.wait_ge(*event("ro_stats", t))
                y = rsqrt(link, ro_st, HR)
                dve.wait_ge(*in_sbuf("ro", t))
                link(V.tensor_tensor(ro[:, :, :], ro[:, :, :], y.rearrange("p (h o) -> p h o", o=1)
                                     .broadcast_to((P, HR, RV)), ALU.mult))
                dve.wait_ge(*event("rg_tanh", t))
                flat = ro[:, :, :].rearrange("p h n -> p (h n)")
                link(V.tensor_tensor(flat, flat, gnrow[:, :], ALU.mult))
                link(V.scalar_tensor_tensor(out=rth[:, :], in0=rth[:, :], scalar=1.0, in1=pa[:, R_G:R_G + 512],
                                            op0=ALU.add, op1=ALU.mult))
                V.tensor_tensor(flat, flat, rth[:, :], ALU.mult).then_inc(ev["ro_done"], 1)
                dve.wait_ge(s_mask, 16 * (t + 1))
                for h in range(HA):
                    dve.wait_ge(*computed(f"s{h}", t))
                    bank = ps[BANK[f"s{h}"]]
                    if h >= 2:
                        dve.wait_ge(*computed(f"pT{h - 2}", t))
                    dve.nop(nofuse=True)
                    ins = V.tensor_tensor_reduce(out=ssb[:, h % 2, :], in0=bank[:, :], in1=mask[:, :], scale=-ATT_SCALE,
                                                 scalar=3.0e38, op0=ALU.add, op1=ALU.min, accum_out=nmax[:, h:h + 1])
                    ins.then_inc(DRAINED[f"s{h}"], 1)
                    if h == 3:
                        yield
                yield
                dve.wait_ge(*event("p_exp", t))
                link(V.reciprocal(l_att, l_att))
                dve.wait_ge(*computed("o", t))
                bank = ps[BANK["o"]]
                ins = V.tensor_tensor(ob[:, :].rearrange("p (h n) -> p h n", n=VD),
                                      bank[:, :].rearrange("p (h n) -> p h n", n=VD),
                                      l_att.rearrange("p (h o) -> p h o", o=1).broadcast_to((P, HA, VD)), ALU.mult)
                ins.then_inc(DRAINED["o"], 1)
                merge(t, 0, "y0")
                merge(t, 1, "y1")
                yield
                for i in range(2):
                    dve.wait_ge(*computed(f"ms{i}", t))
                    bank = ps[BANK[f"ms{i}"]]
                    link(V.tensor_reduce(mmax[:, 2 * i:2 * i + 2], bank[:, :].rearrange("p (h n) -> p h n", n=M),
                                         AX.X, ALU.max))
                    V.tensor_scalar(mmax[:, 2 * i:2 * i + 2], mmax[:, 2 * i:2 * i + 2], -MEM_SCALE, None, ALU.mult)\
                        .then_inc(ev["mem_max"], 1)
                dve.wait_ge(*computed("mo", t))
                bank = ps[BANK["mo"]]
                link(V.reciprocal(l_mem, l_mem))
                ins = V.tensor_tensor(ob[:, :].rearrange("p (h n) -> p h n", n=XD),
                                      bank[:, :].rearrange("p (h n) -> p h n", n=XD),
                                      l_mem.rearrange("p (h o) -> p h o", o=1).broadcast_to((P, HX, XD)), ALU.mult)
                ins.then_inc(DRAINED["mo"], 1)
                merge(t, 2, "y2")
                yield
                dve.wait_ge(s_h, 16 * (t + 1))
                for i, name in enumerate(("ha", "hb")):
                    part = slice(i * 512, i * 512 + 512)
                    dve.wait_ge(*computed(name, t))
                    bank = ps[BANK[name]]
                    ins = V.tensor_tensor(h_next[:, part], bank[:, :], h_next[:, part], ALU.add)
                    ins.then_inc(DRAINED[name], 1)
                dve.wait_ge(*event("f_stats", t))
                y = rsqrt(link, f_st, 1)
                V.tensor_copy(f_st, y).then_inc(ev["f_rstd"], 1)
                dve.wait_ge(*event("xn_scaled", t))
                V.tensor_tensor(xn_next, xn_next, grow[:, :], ALU.mult).then_inc(ev["xn_done"], 1)
                yield
                dve.wait_ge(*in_sbuf("sc2", t))
                dve.wait_ge(*in_sbuf("sc3", t))
                dve.nop(nofuse=True)
                topk(link, scores, 2 * HP, topv, topi)
                yield
                sides = topv[:, :, :].rearrange("p (h c) k -> p h c k", c=2)
                link(V.tensor_tensor(cand.rearrange("p h (i j) -> p h i j", j=TOP),
                                     sides[:, :, 0, :].rearrange("p h (k o) -> p h k o", o=1)
                                     .broadcast_to((P, HP, TOP, TOP)),
                                     sides[:, :, 1, :].rearrange("p h (o k) -> p h o k", o=1)
                                     .broadcast_to((P, HP, TOP, TOP)), ALU.add))
                ins = V.tensor_copy(nplace, topi[:, :, :])
                link(ins, hold=True)
                topk(link, cand, HP, topv[:, 0:HP, :], topi[:, 0:HP, :])
                V.tensor_tensor(besub, bval, bval[:, :, 0:1].broadcast_to((P, HP, TOP)), ALU.subtract)\
                    .then_inc(ev["best_sub"], 1)
                places = topi[:, 0:HP, :]
                np_ = nplace.rearrange("p (h c) k -> p h c k", c=2)
                for side, (dst, op, arg) in enumerate(((seli, ALU.logical_shift_right, 4), (seli2, ALU.bitwise_and, 15))):
                    link(V.tensor_scalar(topi[:, HP:2 * HP, :], places, arg, None, op))
                    link(V.tensor_copy(dst, topi[:, HP:2 * HP, :]))
                    link(V.tensor_tensor(hot, dst.rearrange("p h (k o) -> p h k o", o=1).broadcast_to((P, HP, TOP, TOP)),
                                         iota.rearrange("p (a b j) -> p a b j", a=1, b=1)
                                         .broadcast_to((P, HP, TOP, TOP)), ALU.is_equal))
                    link(V.tensor_tensor(hot, hot, np_[:, :, side, :].rearrange("p h (o j) -> p h o j", o=1)
                                         .broadcast_to((P, HP, TOP, TOP)), ALU.mult))
                    link(V.tensor_reduce(dst, hot, AX.X, ALU.add))
                link(V.scalar_tensor_tensor(out=idxn[:, :].rearrange("p (h k) -> p h k", k=TOP), in0=seli,
                                            scalar=float(NK), in1=seli2, op0=ALU.mult, op1=ALU.add))
                dve.wait_ge(*event("best_exp", t))
                link(V.tensor_reduce(gsum, besub, AX.X, ALU.add))
                link(V.reciprocal(gsum, gsum))
                link(V.tensor_scalar(gsum, gsum, 0.5, None, ALU.mult))
                link(V.tensor_tensor(gaten[:, :].rearrange("p (h k) -> p h k", k=TOP), besub,
                                     gsum.rearrange("p (h o) -> p h o", o=1).broadcast_to((P, HP, TOP)), ALU.mult))
                assert n["n"] == DVE_LINKS, n["n"]

            nplace = merged[:, 0:256].rearrange("p (h k) -> p h k", k=TOP)

            def handoff(t):
                V.tensor_copy(idx[:, :], idxn[:, :])
                V.tensor_copy(gate[:, :], gaten[:, :])
                V.tensor_copy(xn_cur, xn_next)
                V.tensor_copy(h_cur, h_next).then_inc(ev["handed"], 1)
                dve.wait_ge(*event("handed", t))

            def peer_head(t, h):
                if h == HP:
                    return
                link, n = make_link(peer_chain, t * PEER_LINKS + h * 3)
                for k in range(TOP):
                    dve.wait_ge(u_in[k % RING], 16 * (t * (HP * TOP // RING) + h * (TOP // RING) + k // RING + 1))
                    ins = V.tensor_tensor_reduce(out=ub[:, k % RING, :], in0=ub[:, k % RING, :], in1=xn_cur, scale=1.0,
                                                 scalar=0.0, op0=ALU.mult, op1=ALU.add, accum_out=acts[:, 0, k:k + 1])
                    ins.then_inc(dots, 1)
                dve.wait_ge(dots, RING + t * (HP * TOP) + (h + 1) * TOP)
                x, c = acts[:, 0, :], acts[:, 1, :]
                link(V.tensor_tensor(c, x, x, ALU.mult))
                link(V.tensor_scalar(c, c, GELU_B, 1.0, ALU.mult, ALU.add))
                V.tensor_tensor(acts[:, 2, :], c, x, ALU.mult).then_inc(gelu_in, 1)
                link(V.tensor_tensor(acts[:, 3, :], x, gate[:, h * TOP:(h + 1) * TOP], ALU.mult))
                dve.wait_ge(gelu_tanh, t * HP + h + 1)
                V.scalar_tensor_tensor(out=wts[:, h % 2, :], in0=acts[:, 2, :], scalar=1.0, in1=acts[:, 3, :],
                                       op0=ALU.add, op1=ALU.mult).then_inc(s_wts, 1)

            def finish(t):
                dve.wait_ge(v_used, RING + (t + 1) * HP * TOP)
                if isinstance(t, int):
                    dve.wait_ge(s_out, 16 * t)
                for i in range(2):
                    ins = V.tensor_tensor(res[:, i * 512:i * 512 + 512], ps[i][:, :], h_cur[:, i * 512:i * 512 + 512], ALU.add)
                ins.then_inc(s_taken, 1)
                dve.wait_ge(s_taken, t + 2)

            weave(front, peer_head, dve, finish, handoff)


_LG = np.log(1.0 - 2.0 ** (-5.0 - np.arange(HR, dtype=np.float32))).astype(np.float32)
CHUNK_DECAY = [float(x) for x in np.exp(_LG * np.float32(P))]


def weave(front, peer_head, eng, finish=None, handoff=None):
    for _ in front(0):
        pass
    if handoff:
        handoff(0)
    with eng.Fori(1, T) as t:
        pieces = front(t)
        for h in range(HP + 1):
            peer_head(t - 1, h)
            next(pieces, None)
        for _ in pieces:
            pass
        if finish:
            finish(t - 1)
            handoff(t)
    for h in range(HP + 1):
        peer_head(T - 1, h)
    if finish:
        finish(T - 1)


_DIRECT = ["x", "mem", "ffn_norm_g", "ret_gn_g", "mla_qn_g", "mla_kn_g", "x_kn_g", "w_uq", "w_ukv", "w_o_mla", "w_o_ret", "w_o_cross", "w_out",
           "w_mem_kv", "peer_w_q"]


def kernel(**inputs):
    import concourse.bacc as _bacc
    from concourse.bass_utils import run_bass_kernel_spmd as _run

    f = np.float32
    laid = {n: np.asarray(inputs[n]) for n in _DIRECT}
    laid["positions"] = np.asarray(inputs["positions"])[0].reshape(T, P).T
    for n in ("attn_norm_g", "mem_norm_g", "mla_q_norm_g", "mla_kv_norm_g", "x_qn_g"):
        laid[n] = np.asarray(inputs[n])[0].reshape(-1, P).T
    laid["xT"] = np.asarray(inputs["x"])[0].T
    laid["memT"] = np.asarray(inputs["mem"])[0].T
    laid["w_in"] = np.asarray(inputs["w_in"])[0].reshape(KD, P, CHUNKS, CW).transpose(2, 1, 0, 3)
    laid["keysT"] = np.asarray(inputs["peer_keys"])[0].reshape(2 * HP, NK, P).transpose(2, 0, 1)
    laid["peer_u"] = np.asarray(inputs["peer_u"])[0]
    laid["peer_v"] = np.asarray(inputs["peer_v"])[0]
    i = np.arange(P, dtype=f)
    diff = i[None, :] - i[:, None]
    c = np.zeros((P, K_END), f)
    c[:, K_ID:K_ID + P] = np.eye(P, dtype=f)
    for h in range(HR):
        c[:, K_DECAY + h * P:K_DECAY + (h + 1) * P] = np.where(diff >= 0, np.exp(_LG[h] * np.maximum(diff, 0)), 0)
        c[:, K_XI + h * P:K_XI + (h + 1) * P] = np.exp(_LG[h] * (i + 1))[None, :]
        c[:, K_ZETA + h] = np.exp(_LG[h] * (P - 1 - i)) * f(RK ** -0.5)
    c[:, K_IOTA:K_IOTA + TOP] = np.arange(TOP)
    for at, d in ((K_INV, ROPE), (K_INV + ROPE // 2, RK)):
        c[:, at:at + d // 2] = np.power(f(10000.0), -np.arange(0, d, 2, dtype=f) / f(d))
    laid["consts"] = c
    laid["mask"] = np.where(np.arange(S)[None, :] <= np.arange(S)[:, None], f(0), f(NEG))

    nc = _bacc.Bacc("TRN2", target_bir_lowering=False, num_devices=1)
    arrays, aps = {}, {}
    for name, arr in laid.items():
        arr = np.ascontiguousarray(arr)
        arrays["in_" + name] = arr
        aps[name] = nc.dram_tensor("in_" + name, arr.shape, mybir.dt.from_np(arr.dtype), kind="ExternalInput").ap()
    out = nc.dram_tensor("out_0", (1, S, D), F32, kind="ExternalOutput").ap()
    build(nc, aps, out)
    r = _run(nc, [arrays], core_ids=[0])
    return r.results[0]["out_0"]
```

```python
from contextlib import ExitStack

import numpy as np

import concourse.bass as bass
from concourse import mybir

F32 = mybir.dt.float32
I32 = mybir.dt.int32
U32 = mybir.dt.uint32
ALU = mybir.AluOpType
ACT = mybir.ActivationFunctionType
AX = mybir.AxisListType

P = 128
D = 1024
S = 512
M = 256
T = S // P
KD = D // P
HA, NOPE, ROPE, VD = 8, 64, 32, 64
QK = NOPE + ROPE
QR, KVR = 384, 128
HR, RK, RV = 4, 64, 128
HX, XD = 4, 128
HP, NK, TOP = 8, 128, 16
EPS = 1e-6
SPLITS = (QR, KVR, ROPE, HR * RK, HR * RK, HR * RV, HR * RV, HX * XD, 3 * D)
OFF = [sum(SPLITS[:i]) for i in range(len(SPLITS))]
(C_Q, C_KV, C_KR, R_Q, R_K, R_V, R_G, X_Q, GATES) = OFF
COLS = sum(SPLITS)
CHUNKS = 12
CW = COLS // CHUNKS
SLOT = KD * 512
NEG = -1e30
ATT_SCALE = QK ** -0.5
MEM_SCALE = XD ** -0.5
RING = 4
CONSTANT_LOADS = 13
TWO_PI = 6.283185307179586
TP1 = 6.28125
TP2 = float(np.round((TWO_PI - TP1) * 2 ** 24) / 2 ** 24)
TP3 = TWO_PI - TP1 - TP2
PI_LOW = 3.1415925
ROUND = 12582912.0
GELU_A, GELU_B = 0.7978845608028654, 0.044715

K_ID = 0
K_DECAY = K_ID + P
K_XI = K_DECAY + HR * P
K_ZETA = K_XI + HR * P
K_IOTA = K_ZETA + HR
K_INV = K_IOTA + TOP
K_END = K_INV + 48

FRONT_USES = ([("cT", 4), ("xqT", 5), ("q0", 2), ("q1", 3), ("kv0", 2), ("kv1", 3),
               ("rqT", 4), ("rkT", 5), ("rin", 6), ("ro", 7), ("rinc", 6),
               ("qT0", 4), ("qT1", 5), ("kT0", 4), ("kT1", 5)]
              + [u for h in range(HA) for u in ((f"s{h}", 2 + h % 2), (f"pT{h}", 4 + h % 2))]
              + [("o", 7), ("oT", 4), ("y0a", 2), ("y0b", 3), ("roT", 5), ("y1a", 2), ("y1b", 3),
                 ("ms0", 6), ("ms1", 7), ("mp0", 4), ("mp1", 5), ("mo", 6), ("moT", 4),
                 ("y2a", 2), ("y2b", 3), ("mT0", 4), ("mT1", 5), ("ha", 2), ("hb", 3),
                 ("xT0", 4), ("xT1", 5)]
              + [u for c in range(4) for u in ((f"pq{c}", 6 + c % 2), (f"sc{c}", 2 + c % 2))])
SETUP_USES = {2: CHUNKS, 3: CHUNKS, 4: CHUNKS, 5: CHUNKS, 6: 4, 7: 4}
BANK, ORDER, PER_BANK = {}, {}, {b: 0 for b in SETUP_USES}
for _name, _bank in FRONT_USES:
    BANK[_name], ORDER[_name] = _bank, PER_BANK[_bank]
    PER_BANK[_bank] += 1

EVENTS = {"c_stats": 6, "c_rstd": 1, "c_normed": 6, "r_roped": 1, "kz": 1, "rg_tanh": 1,
          "qk_roped": 1, "ro_stats": 4, "ro_done": 1, "p_exp": HA, "gate_tanh": 3, "merged": 1, "mem_max": 2,
          "f_stats": 1, "f_rstd": 1, "xn_scaled": 1, "xn_done": 1, "best_sub": 1, "best_exp": 1, "handed": 1}
LAST_PRODUCT = ["kv1", "y0b", "y1b", "y2b", "ha", "hb", "pq0", "pq1", "pq2", "pq3"]
CHUNKS_PER_TILE = len(LAST_PRODUCT)
DVE_LINKS = 106
PEER_LINKS = HP * 3


STEPS = (["stats", "latent_rstd", "latent_scale", "turn_latents", "turn_ret", "q_proj", "kv_proj", "ret_scores",
          "qk_stats", "ret_out", "qk_norm", "qk_rope", "turn_q", "turn_k", "ret_norm"]
         + [f"att{i}" for i in range(HA + 3)]
         + ["att_out", "turn_o", "y0", "turn_ro", "y1", "mem_scores", "mem_probs", "mem_turn", "mem_out", "turn_mo", "y2",
            "turn_merged", "h_a", "h_b", "f_stats", "f_rstd", "xn", "turn_xn"]
         + [f"{n}{c}" for c in range(4) for n in ("query", "score")]
         + ["top3", "sums", "best0", "best1", "place0", "place1", "gates"])
STEP = {name: i for i, name in enumerate(STEPS)}
QUANTUM = 2
QUANTA = (HP + 1) * TOP // QUANTUM


def build(nc, a, out):
    with ExitStack() as ctx:
        def sb(name, shape, dt=F32):
            return ctx.enter_context(nc.sbuf_tensor(name, shape, dt))

        def sem(name):
            return ctx.enter_context(nc.semaphore(name))

        wring = sb("wring", [P, 2, SLOT])
        ub = sb("ub", [P, RING, D])
        vb = sb("vb", [P, RING, D])
        pa = sb("pa", [P, GATES])
        gt = sb("gt", [P, D])
        kT = sb("kT", [P, HA * S])
        vc = sb("vc", [P, T, HA * VD])
        mkT = sb("mkT", [P, HX, M])
        mv = sb("mv", [P, 2, HX, XD])
        keysT = sb("keysT", [P, 2 * HP, NK])
        hx = sb("hx", [P, 4, D])
        mT = sb("mT", [P, KD, P])
        work = sb("work", [P, 4096])
        ssb = sb("ssb", [P, 2, S])
        pT = sb("pT", [P, 2, S])
        ob = sb("ob", [P, 512])
        oT = sb("oT", [P, 4, P])
        merged = sb("merged", [P, D])
        tmp = sb("tmp", [P, D])
        xqT = sb("xqT", [P, 4, P])
        kz = sb("kz", [P, HR, RK])
        state = sb("state", [RK, HR, RV])
        ro = sb("ro", [P, HR, RV])
        rth = sb("rth", [P, 512])
        mask = sb("mask", [P, S])
        cst = sb("cst", [P, K_END])
        grow = sb("grow", [P, D])
        gnrow = sb("gnrow", [P, HR * RV])
        qkrow = sb("qkrow", [P, 2, QK])
        mkrow = sb("mkrow", [P, XD])
        gcols = sb("gcols", [P, 2 * KD + 5])
        rope = sb("rope", [P, T, 2, 48])
        ropet = sb("ropet", [P, 2, 48])
        posi = sb("posi", [P, T], I32)
        diag = sb("diag", [P, RING, P])
        small = sb("small", [P, 512])
        topv = sb("topv", [P, 2 * HP, TOP])
        topi = sb("topi", [P, 2 * HP, TOP], U32)
        idx = sb("idx", [P, HP * TOP], U32)
        idxn = sb("idxn", [P, HP * TOP], U32)
        gate = sb("gate", [P, HP * TOP])
        gaten = sb("gaten", [P, HP * TOP])
        acts = sb("acts", [P, 5, TOP])
        wts = sb("wts", [P, 2, TOP])

        ps = [ctx.enter_context(nc.psum_tensor(f"bank{b}", [P, 512], F32)) for b in range(8)]
        proj = nc.dram_tensor("proj_scratch", (S, COLS), F32, kind="Internal").ap()

        ident = cst[:, K_ID:K_ID + P]
        decayT = cst[:, K_DECAY:K_DECAY + HR * P]
        xiT = cst[0:RK, K_XI:K_XI + HR * P]
        zeta = cst[:, K_ZETA:K_ZETA + HR]
        iota = cst[:, K_IOTA:K_IOTA + TOP]
        h_next, xn_next, h_cur, xn_cur = (hx[:, i, :] for i in range(4))
        qk = work[:, 0:2 * HA * QK].rearrange("p (h d) -> p h d", d=QK)
        sq = work[:, 1536:1536 + 1536].rearrange("p (h d) -> p h d", d=QK)
        qT = work[:, 3072:4096].rearrange("p (h n) -> p h n", n=P)
        scores = work[:, 0:2048].rearrange("p (h n) -> p h n", n=NK)
        cand = work[:, 2048:4096].rearrange("p (h n) -> p h n", n=TOP * TOP)
        hot = work[:, 0:2048].rearrange("p (h k j) -> p h k j", k=TOP, j=TOP)
        kTh = kT[:, :].rearrange("p (h s) -> p h s", s=S)
        memT = kT[:, 0:KD * M].rearrange("p (k m) -> p k m", m=M)
        memN = kT[:, KD * M:KD * M + 2 * D].rearrange("p (m d) -> p m d", d=D)
        xT = ub[:, :, :].rearrange("p r d -> p (r d)").rearrange("p (k s) -> p k s", s=S)
        stage = vb[:, :, :].rearrange("p r d -> p (r d)")[:, 0:2 * T * CW].rearrange("p (b t n) -> p b t n", b=2, t=T)
        pqT, cT, res = ssb, oT, merged
        rqT, rkT = mT[0:RK, 0:HR, :], mT[0:RK, HR:2 * HR, :]
        inner = merged[:, 0:HR * P].rearrange("p (h n) -> p h n", n=P)
        rxT = merged[0:RK, HR * P:2 * HR * P].rearrange("p (h n) -> p h n", n=P)
        rstd_x, rstd_m, c_st, qk_st = small[:, 0:4], small[:, 4:6], small[:, 8:14], small[:, 16:32]
        ro_st, f_st, mem_st, l_att = small[:, 32:36], small[:, 36:37], small[:, 40:42], small[:, 48:56]
        nmax, mmax, l_mem, gsum = small[:, 56:64], small[:, 64:68], small[:, 68:72], small[:, 72:80]
        nwt = small[:, 80:112]
        posf = small[:, 112:116]
        seli = small[:, 128:256].rearrange("p (h k) -> p h k", k=TOP)
        seli2 = small[:, 256:384].rearrange("p (h k) -> p h k", k=TOP)
        besub = small[:, 384:512].rearrange("p (h k) -> p h k", k=TOP)
        bval = topv[:, 0:HP, :]

        s_const, s_x, s_xT, s_mem = sem("constants_in"), sem("x_in"), sem("xT_in"), sem("memory_in")
        w_in = [sem("weights_in_0"), sem("weights_in_1")]
        full = {b: sem(f"psum_full_{b}") for b in SETUP_USES}
        drained = {b: sem(f"psum_drained_{b}") for b in SETUP_USES}
        ev = {n: sem("ev_" + n) for n in EVENTS}
        s_parked = [sem("stage_parked_0"), sem("stage_parked_1")]
        s_pa, s_gt, s_h, s_mask = sem("projection_in"), sem("gates_in"), sem("residual_in"), sem("mask_in")
        s_sums, s_rope = sem("setup_sums"), sem("setup_rope")
        s_rstd, s_angles, s_mem_g, s_mem_keys = sem("setup_rstd"), sem("setup_angles"), sem("setup_mem_gain"), sem("memory_keys")
        s_ready = sem("setup_ready")
        dve_chain, act_chain = sem("dve_chain"), sem("act_chain")
        peer_chain = sem("peer_chain")
        u_in = [sem(f"u_in_{r}") for r in range(RING)]
        v_in = [sem(f"v_in_{r}") for r in range(RING)]
        dots, gelu_in, gelu_tanh = sem("dots_done"), sem("gelu_in"), sem("gelu_tanh")
        s_wts, s_diag, v_used = sem("weights_ready"), sem("diag_ready"), sem("v_used")
        s_taken, s_out = sem("sum_taken"), sem("out_stored")

        FULL = {name: full[b] for name, b in BANK.items()}
        DRAINED = {name: drained[b] for name, b in BANK.items()}

        def bank_free(name, t):
            return DRAINED[name], SETUP_USES[BANK[name]] + t * PER_BANK[BANK[name]] + ORDER[name]

        def computed(name, t):
            return FULL[name], SETUP_USES[BANK[name]] + t * PER_BANK[BANK[name]] + ORDER[name] + 1

        def in_sbuf(name, t):
            return DRAINED[name], SETUP_USES[BANK[name]] + t * PER_BANK[BANK[name]] + ORDER[name] + 1

        def event(name, t, k=None):
            return ev[name], t * EVENTS[name] + (EVENTS[name] if k is None else k)

        block = ctx.enter_context(nc.Block())

        @block.sync
        def _(sp):
            def consts():
                sp.dma_start(cst[:, :], a["consts"]).then_inc(s_const, 16)
                sp.dma_start(posi[:, :], a["positions"]).then_inc(s_const, 16)
                for k, (name, n) in enumerate((("attn_norm_g", KD), ("mem_norm_g", KD), ("mla_q_norm_g", 3),
                                               ("mla_kv_norm_g", 1), ("x_qn_g", 1))):
                    at = (0, KD, 2 * KD, 2 * KD + 3, 2 * KD + 4)[k]
                    sp.dma_start(gcols[:, at:at + n], a[name]).then_inc(s_const, 16)
                for dst, name in ((grow[:, :], "ffn_norm_g"), (gnrow[:, :], "ret_gn_g"), (qkrow[:, 0, :], "mla_qn_g"),
                                  (qkrow[:, 1, :], "mla_kn_g"), (mkrow[:, :], "x_kn_g")):
                    src = a[name]
                    if name == "ret_gn_g":
                        src = src.rearrange("o h d -> o (h d)")
                    sp.dma_start(dst, src.broadcast_to((P, src.shape[1]))).then_inc(s_const, 16)
                sp.dma_start(keysT[:, :, :], a["keysT"]).then_inc(s_const, 16)

            def w_in_chunk(i, b):
                if not isinstance(i, int):
                    sp.wait_ge(full[5], 2 * i + b - 1)
                    sp.nop(nofuse=True)
                sp.dma_start(wring[:, b, 0:KD * CW].rearrange("p (k n) -> p k n", n=CW),
                             a["w_in"][2 * i + b] if isinstance(i, int) else
                             a["w_in"][bass.ds(2 * i + b, 1), :, :, :].rearrange("o p k n -> p (o k) n"))\
                    .then_inc(w_in[b], 16)

            def park(i, b):
                for t in range(T):
                    sp.wait_ge(drained[2 + t], 2 * i + b + 1)
                sp.nop(nofuse=True)
                sp.dma_start(proj[:, bass.ds((2 * i + b) * CW, CW)].rearrange("(t p) n -> p t n", p=P),
                             stage[:, b, :, :]).then_inc(s_parked[b], 16)

            sp.dma_start(hx[:, :, :], a["x"].rearrange("o (t p) d -> p (o t) d", p=P)).then_inc(s_x, 16)
            sp.dma_start(xT, a["xT"].rearrange("(k p) s -> p k s", p=P)).then_inc(s_xT, 16)
            w_in_chunk(0, 0)
            consts()
            w_in_chunk(0, 1)
            sp.dma_start(memT, a["memT"].rearrange("(k p) m -> p k m", p=P)).then_inc(s_mem, 16)
            sp.dma_start(memN, a["mem"].rearrange("o (m p) d -> p (o m) d", p=P)).then_inc(s_mem, 16)
            with sp.Fori(1, CHUNKS // 2) as i:
                for b in range(2):
                    w_in_chunk(i, b)
                    park(i - 1, b)
            for b in range(2):
                sp.wait_ge(full[5], CHUNKS + b - 1)
                sp.dma_start(wring[:, b, :].rearrange("p (k n) -> p k n", n=512),
                             a["w_mem_kv"].rearrange("o (k p) n -> p (o k) n", p=P)[:, :, b * 512:b * 512 + 512])\
                    .then_inc(w_in[b], 16)
                park(CHUNKS // 2 - 1, b)

            def chunk_sources():
                for name in ("w_o_mla", "w_o_ret", "w_o_cross"):
                    yield a[name].rearrange("o (k p) n -> p (o k) n", p=P), 1024, 4
                w_out = a["w_out"].rearrange("o (k p) n -> p (o k) n", p=P)
                for c in range(2):
                    yield w_out[:, :, c * 512:c * 512 + 512], 512, 8
                w_q = a["peer_w_q"].rearrange("o (k p) n -> p (o k) n", p=P)
                for c in range(4):
                    yield w_q[:, :, c * 512:c * 512 + 512], 512, 8

            def weights(t, c):
                b = c % 2
                if c >= 2:
                    sp.wait_ge(*computed(LAST_PRODUCT[c - 2], t))
                elif isinstance(t, int) and t == 0:
                    sp.wait_ge(full[6], 2 * (b + 1))
                else:
                    sp.wait_ge(*computed(LAST_PRODUCT[c - 2], t - 1))
                sp.nop(nofuse=True)
                if c == 0:
                    sp.dma_start(wring[:, b, 0:3 * HA * QK].rearrange("p (k n) -> p k n", n=HA * QK),
                                 a["w_uq"].rearrange("o (k p) n -> p (o k) n", p=P)).then_inc(w_in[b], 16)
                    sp.dma_start(wring[:, b, 2304:2304 + 1024], a["w_ukv"].rearrange("o p n -> (o p) n"))\
                        .then_inc(w_in[b], 16)
                else:
                    src, n, k = list(chunk_sources())[c - 1]
                    sp.dma_start(wring[:, b, :].rearrange("p (k n) -> p k n", n=n), src).then_inc(w_in[b], 16)

            def front(t):
                rows = bass.ds(t * P, P)
                first = isinstance(t, int) and t == 0
                if not first:
                    sp.wait_ge(*event("ro_done", t - 1))
                    sp.nop(nofuse=True)
                sp.dma_start(pa[:, :], proj[rows, 0:GATES]).then_inc(s_pa, 16)
                if not first:
                    sp.wait_ge(*in_sbuf(f"s{HA - 1}", t - 1))
                    sp.nop(nofuse=True)
                sp.dma_start(mask[:, :], a["mask"][rows, :]).then_inc(s_mask, 16)
                if not first:
                    sp.wait_ge(*event("handed", t - 1))
                    sp.nop(nofuse=True)
                sp.dma_start(h_next, a["x"].rearrange("o s d -> (o s) d")[rows, :]).then_inc(s_h, 16)
                weights(t, 0)
                weights(t, 1)
                for br in range(3):
                    if br or not first:
                        sp.wait_ge(*in_sbuf(f"y{(br - 1) % 3}b", t if br else t - 1))
                        sp.nop(nofuse=True)
                    sp.dma_start(gt[:, :], proj[rows, GATES + br * D:GATES + br * D + D]).then_inc(s_gt, 16)
                    weights(t, 2 + br)
                for c in range(5, CHUNKS_PER_TILE):
                    weights(t, c)

            def store(t):
                sp.wait_ge(s_taken, t + 2)
                sp.nop(nofuse=True)
                sp.dma_start(out.rearrange("o s d -> (o s) d")[bass.ds(t * P, P), :], res[:, :]).then_inc(s_out, 16)
                sp.wait_ge(s_out, 16 * (t + 1))
                sp.nop(nofuse=True)

            sp.wait_ge(s_parked[0], 16 * (CHUNKS // 2))
            sp.wait_ge(s_parked[1], 16 * (CHUNKS // 2))
            sp.wait_ge(s_ready, 1)
            front(0)
            with sp.Fori(1, T) as t:
                front(t)
                store(t - 1)
            store(T - 1)

        @block.gpsimd
        def _(pool):
            def gather(dst, table, t, h, k, arrived, used):
                n = t * (HP * TOP) + h * TOP + k
                pool.wait_ge(used, n + 1)
                pool.nop(nofuse=True)
                pool.indirect_dma_start(dst[:, k % RING, :], None, table, bass.IndirectOffsetOnAxis(
                    ap=idx[:, h * TOP + k:h * TOP + k + 1], axis=0)).then_inc(arrived[k % RING], 16)

            def peer(t):
                pool.wait_ge(*event("handed", t))
                for h in range(HP + 1):
                    for k in range(TOP):
                        if h < HP:
                            gather(ub, a["peer_u"], t, h, k, u_in, dots)
                        if h > 0:
                            gather(vb, a["peer_v"], t, h - 1, k, v_in, v_used)

            peer(0)
            with pool.Fori(1, T) as t:
                peer(t)

        @block.scalar
        def _(act):
            A = nc.scalar.activation

            def setup():
                act.wait_ge(s_x, 16)
                for t in range(T):
                    if t:
                        act.wait_ge(s_sums, t)
                    A(tmp[:, :], hx[:, t, :], ACT.Square, scale=D ** -0.5,
                      accum_out=rstd_x[:, t:t + 1]).then_inc(s_sums, 1)
                act.wait_ge(s_mem, 32)
                for m in range(2):
                    act.wait_ge(s_sums, T + m)
                    A(tmp[:, :], memN[:, m, :], ACT.Square, scale=D ** -0.5,
                      accum_out=rstd_m[:, m:m + 1]).then_inc(s_sums, 1)
                act.wait_ge(s_angles, 1)
                for i in range(2):
                    A(rope[:, :, i, :], work[:, 192 * (1 + i):192 * (2 + i)].rearrange("p (t n) -> p t n", n=48),
                      ACT.Sin).then_inc(s_rope, 1)

            def drain_projection(i):
                for b in range(2):
                    for t in (0, 2):
                        act.wait_ge(full[2 + t], 2 * i + b + 1)
                        if not isinstance(i, int):
                            act.wait_ge(s_parked[b], 16 * i)
                        A(stage[:, b, t, :], ps[2 + t][:, 0:CW], ACT.Copy, scale=rstd_x[:, t:t + 1])\
                            .then_inc(drained[2 + t], 1)

            setup()
            act.wait_ge(s_rstd, 1)
            drain_projection(0)
            with act.Fori(1, CHUNKS // 2) as i:
                drain_projection(i)

            def gate_tanh(t, br):
                act.wait_ge(s_gt, 16 * (3 * t + br + 1))
                A(gt[:, :], gt[:, :], ACT.Tanh, scale=0.5).then_inc(ev["gate_tanh"], 1)

            def front(t):
                yield STEP["stats"]
                act.wait_ge(s_pa, 16 * (t + 1))
                parts = [(C_Q, QR), (C_KV, KVR)] + [(X_Q + h * XD, XD) for h in range(HX)]
                junk = [0, QR] + [QR + KVR + h * XD for h in range(HX)]
                for j, (at, n) in enumerate(parts):
                    A(tmp[:, junk[j]:junk[j] + n], pa[:, at:at + n], ACT.Square, scale=n ** -0.5,
                      accum_out=c_st[:, j:j + 1]).then_inc(ev["c_stats"], 1)
                A(rth[:, :], pa[:, R_G:R_G + 512], ACT.Tanh, scale=0.5).then_inc(ev["rg_tanh"], 1)
                yield STEP["latent_scale"]
                act.wait_ge(*event("c_rstd", t))
                for j, (at, n) in enumerate(parts):
                    A(pa[:, at:at + n], pa[:, at:at + n], ACT.Copy, scale=c_st[:, j:j + 1]).then_inc(ev["c_normed"], 1)
                yield STEP["turn_latents"]
                act.wait_ge(*computed("cT", t))
                bank = ps[BANK["cT"]]
                for j in range(4):
                    ins = A(cT[:, j, :], bank[:, j * P:(j + 1) * P], ACT.Copy, scale=gcols[:, 2 * KD + j:2 * KD + j + 1])
                ins.then_inc(DRAINED["cT"], 1)
                act.wait_ge(*computed("xqT", t))
                bank = ps[BANK["xqT"]]
                A(xqT[:, :, :], bank[:, :], ACT.Copy, scale=gcols[:, 2 * KD + 4:2 * KD + 5]).then_inc(DRAINED["xqT"], 1)
                yield STEP["ret_out"]
                act.wait_ge(*computed("ro", t))
                bank = ps[BANK["ro"]]
                for h in range(HR):
                    A(ob[:, h * RV:(h + 1) * RV], bank[:, h * RV:(h + 1) * RV], ACT.Square, scale=RV ** -0.5,
                      accum_out=ro_st[:, h:h + 1]).then_inc(ev["ro_stats"], 1)
                nc.scalar.copy(ro[:, :, :], bank[:, :]).then_inc(DRAINED["ro"], 1)
                yield STEP["turn_q"]
                for i in range(2):
                    act.wait_ge(*computed(f"qT{i}", t))
                    nc.scalar.copy(qT[0:QK, 4 * i:4 * i + 4, :], ps[BANK[f"qT{i}"]][0:QK, :]).then_inc(DRAINED[f"qT{i}"], 1)
                yield STEP["turn_k"]
                for i in range(2):
                    act.wait_ge(*computed(f"kT{i}", t))
                    act.nop(nofuse=True)
                    nc.scalar.copy(kTh[0:QK, 4 * i:4 * i + 4, bass.ds(t * P, P)],
                                   ps[BANK[f"kT{i}"]][0:QK, :].rearrange("p (h n) -> p h n", n=P))\
                        .then_inc(DRAINED[f"kT{i}"], 1)
                for step in range(HA + 3):
                    yield STEP[f"att{step}"]
                    if 0 <= step - 1 < HA:
                        h = step - 1
                        act.wait_ge(*in_sbuf(f"s{h}", t))
                        A(ssb[:, h % 2, :], ssb[:, h % 2, :], ACT.Exp, scale=-1.0, bias=nmax[:, h:h + 1],
                          accum_out=l_att[:, h:h + 1]).then_inc(ev["p_exp"], 1)
                    if 0 <= step - 2 < HA:
                        h = step - 2
                        act.wait_ge(*computed(f"pT{h}", t))
                        nc.scalar.copy(pT[:, h % 2, :], ps[BANK[f"pT{h}"]][:, :]).then_inc(DRAINED[f"pT{h}"], 1)
                yield STEP["turn_o"]
                act.wait_ge(*computed("oT", t))
                nc.scalar.copy(oT[:, :, :], ps[BANK["oT"]][:, :]).then_inc(DRAINED["oT"], 1)
                gate_tanh(t, 0)
                yield STEP["turn_ro"]
                act.wait_ge(*computed("roT", t))
                A(oT[:, :, :], ps[BANK["roT"]][:, :], ACT.Copy, scale=0.5).then_inc(DRAINED["roT"], 1)
                gate_tanh(t, 1)
                yield STEP["mem_probs"]
                for h in range(HX):
                    act.wait_ge(*event("mem_max", t, h // 2 + 1))
                    ins = A(ssb[:, h // 2, (h % 2) * M:(h % 2) * M + M], ps[6 + h // 2][:, (h % 2) * M:(h % 2) * M + M],
                            ACT.Exp, scale=MEM_SCALE, bias=mmax[:, h:h + 1], accum_out=l_mem[:, h:h + 1])
                    if h % 2:
                        ins.then_inc(DRAINED[f"ms{h // 2}"], 1)
                yield STEP["mem_turn"]
                for i in range(2):
                    act.wait_ge(*computed(f"mp{i}", t))
                    nc.scalar.copy(pT[:, i, :], ps[BANK[f"mp{i}"]][:, :]).then_inc(DRAINED[f"mp{i}"], 1)
                yield STEP["turn_mo"]
                act.wait_ge(*computed("moT", t))
                nc.scalar.copy(oT[:, :, :], ps[BANK["moT"]][:, :]).then_inc(DRAINED["moT"], 1)
                gate_tanh(t, 2)
                yield STEP["turn_merged"]
                for i in range(2):
                    act.wait_ge(*computed(f"mT{i}", t))
                    A(mT[:, 4 * i:4 * i + 4, :], ps[BANK[f"mT{i}"]][:, :], ACT.Copy, scale=0.5)\
                        .then_inc(DRAINED[f"mT{i}"], 1)
                yield STEP["f_stats"]
                act.wait_ge(*in_sbuf("ha", t))
                act.wait_ge(*in_sbuf("hb", t))
                A(tmp[:, :], h_next, ACT.Square, scale=D ** -0.5, accum_out=f_st).then_inc(ev["f_stats"], 1)
                yield STEP["xn"]
                act.wait_ge(*event("f_rstd", t))
                A(xn_next, h_next, ACT.Copy, scale=f_st).then_inc(ev["xn_scaled"], 1)
                yield STEP["turn_xn"]
                for i in range(2):
                    act.wait_ge(*computed(f"xT{i}", t))
                    nc.scalar.copy(mT[:, 4 * i:4 * i + 4, :], ps[BANK[f"xT{i}"]][:, :]).then_inc(DRAINED[f"xT{i}"], 1)
                for c in range(4):
                    yield STEP[f"query{c}"]
                    act.wait_ge(*computed(f"pq{c}", t))
                    nc.scalar.copy(pqT[:, c % 2, :], ps[BANK[f"pq{c}"]][:, :]).then_inc(DRAINED[f"pq{c}"], 1)
                    yield STEP[f"score{c}"]
                    act.wait_ge(*computed(f"sc{c}", t))
                    nc.scalar.copy(scores[:, 4 * c:4 * c + 4, :], ps[BANK[f"sc{c}"]][:, :]).then_inc(DRAINED[f"sc{c}"], 1)
                yield STEP["gates"]
                act.wait_ge(*event("best_sub", t))
                A(besub, besub, ACT.Exp).then_inc(ev["best_exp"], 1)

            def peer_tanh(t, h):
                act.wait_ge(gelu_in, t * HP + h + 1)
                A(acts[:, 2, :], acts[:, 2, :], ACT.Tanh, scale=GELU_A).then_inc(gelu_tanh, 1)

            def peer(t, h, k0):
                for k in range(k0, k0 + QUANTUM):
                    if h > 0:
                        n = t * (HP * TOP) + (h - 1) * TOP + k
                        if k == 0:
                            act.wait_ge(s_wts, t * HP + h)
                        act.wait_ge(v_used, n + 1)
                        A(diag[:, k % RING, :], ident, ACT.Copy, scale=wts[:, (h - 1) % 2, k:k + 1]).then_inc(s_diag, 1)
                if h < HP and k0 + QUANTUM == TOP:
                    peer_tanh(t, h)

            weave(front, peer, act)

        @block.tensor
        def _(pe):
            mm, tr = nc.tensor.matmul, nc.tensor.transpose

            def project(i):
                for b in range(2):
                    pe.wait_ge(w_in[b], 16 * (i + 1))
                    w = wring[:, b, 0:KD * CW].rearrange("p (k n) -> p k n", n=CW)
                    for t in range(T):
                        if b or not isinstance(i, int):
                            pe.wait_ge(drained[2 + t], 2 * i + b)
                        for k in range(KD):
                            ins = mm(ps[2 + t][:, 0:CW], xT[:, k, t * P:(t + 1) * P], w[:, k, :],
                                     start=(k == 0), stop=(k == KD - 1))
                        ins.then_inc(full[2 + t], 1)

            pe.wait_ge(s_const, 16 * CONSTANT_LOADS)
            pe.wait_ge(s_rstd, 1)
            project(0)
            with pe.Fori(1, CHUNKS // 2) as i:
                project(i)
            pe.wait_ge(s_mem_g, 1)
            for j in range(4):
                c, m = divmod(j, 2)
                pe.wait_ge(w_in[c], 16 * (CHUNKS // 2 + 1))
                if j:
                    pe.wait_ge(drained[6], j)
                w = wring[:, c, :].rearrange("p (k n) -> p k n", n=512)
                for k in range(KD):
                    ins = mm(ps[6][:, :], memT[:, k, m * P:(m + 1) * P], w[:, k, :], start=(k == 0), stop=(k == KD - 1))
                ins.then_inc(full[6], 1)
                pe.wait_ge(s_mem_keys, j + 1)
                if j:
                    pe.wait_ge(drained[7], j)
                for h in range(2):
                    ins = tr(ps[7][:, h * P:(h + 1) * P], tmp[:, 256 * h:256 * h + XD], ident)
                ins.then_inc(full[7], 1)

            def weights(t, c):
                b = c % 2
                loads = CHUNKS // 2 + 1 + t * (6 if b == 0 else 5)
                order = c // 2 + (2 if b == 0 else 1)
                pe.wait_ge(w_in[b], 16 * (loads + order))
                return wring[:, b, :]

            def turn(bank, src, n, rows=P):
                for j in range(n):
                    ins = tr(bank[0:rows, j * P:(j + 1) * P], src(j), ident)
                return ins

            def branch_out(t, c, names, src):
                pe.wait_ge(*in_sbuf(src, t))
                w = weights(t, c).rearrange("p (k n) -> p k n", n=1024)
                for i, name in enumerate(names):
                    pe.wait_ge(*bank_free(name, t))
                    bank = ps[BANK[name]]
                    for k in range(4):
                        ins = mm(bank[:, :], oT[:, k, :], w[:, k, i * 512:i * 512 + 512], start=(k == 0), stop=(k == 3))
                    ins.then_inc(FULL[name], 1)

            def front(t):
                yield STEP["turn_latents"]
                pe.wait_ge(*event("c_normed", t))
                pe.wait_ge(*bank_free("cT", t))
                turn(ps[BANK["cT"]], lambda j: pa[:, C_Q + j * P:C_Q + (j + 1) * P], 4).then_inc(FULL["cT"], 1)
                pe.wait_ge(*bank_free("xqT", t))
                turn(ps[BANK["xqT"]], lambda j: pa[:, X_Q + j * P:X_Q + (j + 1) * P], 4).then_inc(FULL["xqT"], 1)
                yield STEP["turn_ret"]
                pe.wait_ge(*event("r_roped", t))
                for name, at in (("rqT", R_Q), ("rkT", R_K)):
                    pe.wait_ge(*bank_free(name, t))
                    pe.nop(nofuse=True)
                    turn(ps[BANK[name]], lambda j: pa[:, at + j * RK:at + (j + 1) * RK], 4, RK).then_inc(FULL[name], 1)
                yield STEP["q_proj"]
                pe.wait_ge(*in_sbuf("cT", t))
                w = weights(t, 0)
                wq = w[:, 0:2304].rearrange("p (k n) -> p k n", n=HA * QK)
                for i in range(2):
                    pe.wait_ge(*bank_free(f"q{i}", t))
                    bank = ps[BANK[f"q{i}"]]
                    for k in range(3):
                        ins = mm(bank[:, 0:384], cT[:, k, :], wq[:, k, i * 384:i * 384 + 384], start=(k == 0), stop=(k == 2))
                    ins.then_inc(FULL[f"q{i}"], 1)
                yield STEP["kv_proj"]
                for i in range(2):
                    pe.wait_ge(*bank_free(f"kv{i}", t))
                    mm(ps[BANK[f"kv{i}"]][:, :], cT[:, 3, :], w[:, 2304 + 512 * i:2304 + 512 * i + 512], start=True, stop=True)\
                        .then_inc(FULL[f"kv{i}"], 1)
                yield STEP["ret_scores"]
                pe.wait_ge(*in_sbuf("rqT", t))
                pe.wait_ge(*in_sbuf("rkT", t))
                pe.wait_ge(*bank_free("rin", t))
                for h in range(HR):
                    ins = mm(ps[BANK["rin"]][:, h * P:(h + 1) * P], rkT[:, h, :], rqT[:, h, :], start=True, stop=True)
                ins.then_inc(FULL["rin"], 1)
                yield STEP["ret_out"]
                pe.wait_ge(*in_sbuf("rin", t))
                pe.wait_ge(*bank_free("ro", t))
                for h in range(HR):
                    o = ps[BANK["ro"]][:, h * RV:(h + 1) * RV]
                    mm(o, inner[:, h, :], pa[:, R_V + h * RV:R_V + (h + 1) * RV], start=True, stop=False)
                    ins = mm(o, rxT[:, h, :], state[:, h, :], start=False, stop=True)
                ins.then_inc(FULL["ro"], 1)
                pe.wait_ge(*event("kz", t))
                pe.wait_ge(*bank_free("rinc", t))
                for h in range(HR):
                    ins = mm(ps[BANK["rinc"]][0:RK, h * RV:(h + 1) * RV], kz[:, h, :],
                             pa[:, R_V + h * RV:R_V + (h + 1) * RV], start=True, stop=True)
                ins.then_inc(FULL["rinc"], 1)
                for step, names in (("turn_q", ("qT0", "qT1")), ("turn_k", ("kT0", "kT1"))):
                    yield STEP[step]
                    pe.wait_ge(*event("qk_roped", t))
                    for name in names:
                        at = ("qT0", "qT1", "kT0", "kT1").index(name)
                        pe.wait_ge(*bank_free(name, t))
                        turn(ps[BANK[name]], lambda j: qk[:, 4 * at + j, :], 4, QK).then_inc(FULL[name], 1)
                for step in range(HA + 3):
                    yield STEP[f"att{step}"]
                    if step == 0:
                        pe.wait_ge(*in_sbuf("qT1", t))
                        pe.wait_ge(*in_sbuf("kT0", t))
                        pe.wait_ge(*in_sbuf("kT1", t))
                    if step < HA:
                        h = step
                        pe.wait_ge(*bank_free(f"s{h}", t))
                        mm(ps[BANK[f"s{h}"]][:, :], qT[0:QK, h, :], kTh[0:QK, h, :], start=True, stop=True)\
                            .then_inc(FULL[f"s{h}"], 1)
                    if 0 <= step - 2 < HA:
                        h = step - 2
                        pe.wait_ge(*event("p_exp", t, h + 1))
                        pe.wait_ge(*bank_free(f"pT{h}", t))
                        turn(ps[BANK[f"pT{h}"]], lambda j: ssb[:, h % 2, j * P:(j + 1) * P], 4).then_inc(FULL[f"pT{h}"], 1)
                    if 0 <= step - 3 < HA:
                        h = step - 3
                        pe.wait_ge(*in_sbuf(f"pT{h}", t))
                        if h == 0:
                            pe.wait_ge(*bank_free("o", t))
                        for j in range(T):
                            ins = mm(ps[BANK["o"]][:, h * VD:(h + 1) * VD], pT[:, h % 2, j * P:(j + 1) * P],
                                     vc[:, j, h * VD:(h + 1) * VD], start=(j == 0), stop=(j == T - 1))
                ins.then_inc(FULL["o"], 1)
                yield STEP["turn_o"]
                pe.wait_ge(*in_sbuf("o", t))
                pe.wait_ge(*bank_free("oT", t))
                turn(ps[BANK["oT"]], lambda j: ob[:, j * P:(j + 1) * P], 4).then_inc(FULL["oT"], 1)
                yield STEP["y0"]
                branch_out(t, 1, ("y0a", "y0b"), "oT")
                yield STEP["turn_ro"]
                pe.wait_ge(*event("ro_done", t))
                pe.wait_ge(*bank_free("roT", t))
                turn(ps[BANK["roT"]], lambda j: ro[:, j, :], 4).then_inc(FULL["roT"], 1)
                yield STEP["y1"]
                branch_out(t, 2, ("y1a", "y1b"), "roT")
                yield STEP["mem_scores"]
                for i in range(2):
                    pe.wait_ge(*bank_free(f"ms{i}", t))
                    for h in range(2):
                        ins = mm(ps[BANK[f"ms{i}"]][:, h * M:h * M + M], xqT[:, 2 * i + h, :], mkT[:, 2 * i + h, :],
                                 start=True, stop=True)
                    ins.then_inc(FULL[f"ms{i}"], 1)
                yield STEP["mem_turn"]
                for i in range(2):
                    pe.wait_ge(*in_sbuf(f"ms{i}", t))
                    pe.wait_ge(*bank_free(f"mp{i}", t))
                    turn(ps[BANK[f"mp{i}"]], lambda j: ssb[:, i, j * P:(j + 1) * P], 4).then_inc(FULL[f"mp{i}"], 1)
                yield STEP["mem_out"]
                pe.wait_ge(*in_sbuf("mp0", t))
                pe.wait_ge(*in_sbuf("mp1", t))
                pe.wait_ge(*bank_free("mo", t))
                for h in range(HX):
                    for j in range(2):
                        ins = mm(ps[BANK["mo"]][:, h * XD:(h + 1) * XD],
                                 pT[:, h // 2, (h % 2) * M + j * P:(h % 2) * M + (j + 1) * P],
                                 mv[:, j, h, :], start=(j == 0), stop=(j == 1))
                ins.then_inc(FULL["mo"], 1)
                yield STEP["turn_mo"]
                pe.wait_ge(*in_sbuf("mo", t))
                pe.wait_ge(*bank_free("moT", t))
                turn(ps[BANK["moT"]], lambda j: ob[:, j * P:(j + 1) * P], 4).then_inc(FULL["moT"], 1)
                yield STEP["y2"]
                branch_out(t, 3, ("y2a", "y2b"), "moT")
                yield STEP["turn_merged"]
                pe.wait_ge(*event("merged", t))
                for i in range(2):
                    pe.wait_ge(*bank_free(f"mT{i}", t))
                    turn(ps[BANK[f"mT{i}"]], lambda j: merged[:, (4 * i + j) * P:(4 * i + j + 1) * P], 4)\
                        .then_inc(FULL[f"mT{i}"], 1)
                for c, step, name in ((4, "h_a", "ha"), (5, "h_b", "hb")):
                    yield STEP[step]
                    pe.wait_ge(*in_sbuf(f"mT{c - 4}", t))
                    pe.wait_ge(*in_sbuf("mT1", t))
                    w = weights(t, c).rearrange("p (k n) -> p k n", n=512)
                    pe.wait_ge(*bank_free(name, t))
                    for k in range(KD):
                        ins = mm(ps[BANK[name]][:, :], mT[:, k, :], w[:, k, :], start=(k == 0), stop=(k == KD - 1))
                    ins.then_inc(FULL[name], 1)
                yield STEP["turn_xn"]
                pe.wait_ge(*event("xn_done", t))
                for i in range(2):
                    pe.wait_ge(*bank_free(f"xT{i}", t))
                    turn(ps[BANK[f"xT{i}"]], lambda j: xn_next[:, (4 * i + j) * P:(4 * i + j + 1) * P], 4)\
                        .then_inc(FULL[f"xT{i}"], 1)
                for c in range(4):
                    yield STEP[f"query{c}"]
                    if c == 0:
                        pe.wait_ge(*in_sbuf("xT0", t))
                        pe.wait_ge(*in_sbuf("xT1", t))
                    w = weights(t, 6 + c).rearrange("p (k n) -> p k n", n=512)
                    pe.wait_ge(*bank_free(f"pq{c}", t))
                    for j in range(4):
                        for k in range(KD):
                            ins = mm(ps[BANK[f"pq{c}"]][:, j * P:(j + 1) * P], w[:, k, j * P:(j + 1) * P], mT[:, k, :],
                                     start=(k == 0), stop=(k == KD - 1))
                    ins.then_inc(FULL[f"pq{c}"], 1)
                    yield STEP[f"score{c}"]
                    pe.wait_ge(*in_sbuf(f"pq{c}", t))
                    pe.wait_ge(*bank_free(f"sc{c}", t))
                    for j in range(4):
                        ins = mm(ps[BANK[f"sc{c}"]][:, j * P:(j + 1) * P], pqT[:, c % 2, j * P:(j + 1) * P],
                                 keysT[:, 4 * c + j, :], start=True, stop=True)
                    ins.then_inc(FULL[f"sc{c}"], 1)

            def peer(t, h, k0):
                if h == 0:
                    return
                h -= 1
                if h == 0 and k0 == 0:
                    pe.wait_ge(s_taken, t + 1)
                for k in range(k0, k0 + QUANTUM):
                    n = t * (HP * TOP) + h * TOP + k
                    pe.wait_ge(s_diag, n + 1)
                    pe.wait_ge(v_in[k % RING], 16 * (t * (HP * TOP // RING) + h * (TOP // RING) + k // RING + 1))
                    for i in range(2):
                        ins = mm(ps[i][:, :], diag[:, k % RING, :], vb[:, k % RING, i * 512:i * 512 + 512],
                                 start=(h == 0 and k == 0), stop=(h == HP - 1 and k == TOP - 1))
                    ins.then_inc(v_used, 1)

            weave(front, peer, pe)

        @block.vector
        def _(dve):
            V = nc.vector
            def make_link(chain, base):
                state_ = {"n": 0}

                def link(ins, hold=False):
                    state_["n"] += 1
                    ins.then_inc(chain, 1)
                    dve.wait_ge(chain, base + state_["n"])
                    if hold:
                        dve.nop(nofuse=True)
                return link, state_

            def rsqrt(link, x, n):
                y, s = nwt[:, 0:n], nwt[:, 16:16 + n]
                link(V.tensor_scalar(x, x, EPS, None, ALU.add))
                link(V.tensor_scalar(y.bitcast(U32), x.bitcast(U32), 1, None, ALU.logical_shift_right))
                link(V.tensor_scalar(y.bitcast(I32), y.bitcast(I32), -1.0, 1597463007.0, ALU.mult, ALU.add))
                for _ in range(3):
                    link(V.scalar_tensor_tensor(out=s, in0=y, scalar=-0.5, in1=y, op0=ALU.mult, op1=ALU.mult))
                    link(V.tensor_tensor(s, s, x, ALU.mult))
                    link(V.scalar_tensor_tensor(out=y, in0=s, scalar=1.5, in1=y, op0=ALU.add, op1=ALU.mult))
                return y

            def rotate(link, x, half, cos, sin, heads):
                x1, x2 = x[:, :, 0:half], x[:, :, half:2 * half]
                c = cos.rearrange("p (o n) -> p o n", o=1).broadcast_to((P, heads, half))
                s = sin.rearrange("p (o n) -> p o n", o=1).broadcast_to((P, heads, half))
                r = [tmp[:, 256 * i:256 * i + heads * half].rearrange("p (h n) -> p h n", n=half) for i in range(4)]
                V.tensor_tensor(r[0], x1, c, ALU.mult)
                V.tensor_tensor(r[1], x2, s, ALU.mult)
                V.tensor_tensor(r[2], x1, s, ALU.mult)
                link(V.tensor_tensor(r[3], x2, c, ALU.mult))
                V.tensor_tensor(x1, r[0], r[1], ALU.subtract)
                return V.tensor_tensor(x2, r[2], r[3], ALU.add)

            link, _n = make_link(dve_chain, 0)
            V.memset(state[:, :, :], 0.0).then_inc(v_used, RING)
            V.memset(vc[:, :, :], 0.0).then_inc(s_taken, 1)
            V.memset(acts[:, 4, :], 0.0).then_inc(dots, RING)
            dve.wait_ge(s_const, 16 * CONSTANT_LOADS)
            dve.wait_ge(s_xT, 16)
            for k in range(KD):
                V.tensor_scalar(xT[:, k, :], xT[:, k, :], gcols[:, k:k + 1], None, ALU.mult)
            dve.wait_ge(s_sums, 4)
            y = rsqrt(link, rstd_x, T)
            V.tensor_copy(rstd_x, y).then_inc(s_rstd, 1)
            dve.wait_ge(s_rstd, 1)
            ang = work[:, 0:192].rearrange("p (t n) -> p t n", n=48)
            sn = work[:, 384:576].rearrange("p (t n) -> p t n", n=48)
            cs = work[:, 192:384].rearrange("p (t n) -> p t n", n=48)
            turns = work[:, 576:768].rearrange("p (t n) -> p t n", n=48)
            link(V.tensor_copy(posf, posi[:, :]))
            link(V.tensor_tensor(ang, posf.rearrange("p (t o) -> p t o", o=1).broadcast_to((P, T, 48)),
                                 cst[:, K_INV:K_INV + 48].rearrange("p (o n) -> p o n", o=1).broadcast_to((P, T, 48)),
                                 ALU.mult))
            link(V.tensor_scalar(turns, ang, 1.0 / TWO_PI, ROUND, ALU.mult, ALU.add))
            link(V.tensor_scalar(turns, turns, ROUND, None, ALU.subtract))
            for part in (TP1, TP2, TP3):
                link(V.scalar_tensor_tensor(out=ang, in0=turns, scalar=-part, in1=ang, op0=ALU.mult, op1=ALU.add))
            link(V.tensor_scalar(sn, ang, PI_LOW, -PI_LOW, ALU.min, ALU.max))
            link(V.tensor_scalar(ang, ang, TWO_PI / 4, None, ALU.add))
            link(V.tensor_scalar(turns, ang, PI_LOW, -TWO_PI, ALU.is_gt, ALU.mult))
            link(V.tensor_tensor(cs, ang, turns, ALU.add))
            V.tensor_scalar(cs, cs, PI_LOW, -PI_LOW, ALU.min, ALU.max).then_inc(s_angles, 1)
            dve.wait_ge(s_mem, 32)
            for k in range(KD):
                ins = V.tensor_scalar(memT[:, k, :], memT[:, k, :], gcols[:, KD + k:KD + k + 1], None, ALU.mult)
            ins.then_inc(s_mem_g, 1)
            dve.wait_ge(s_sums, 6)
            y = rsqrt(link, rstd_m, 2)
            link(V.tensor_copy(rstd_m, y))

            def drain_projection(i):
                for b in range(2):
                    for t in (1, 3):
                        if not isinstance(i, int):
                            dve.wait_ge(s_parked[b], 16 * i)
                        dve.wait_ge(full[2 + t], 2 * i + b + 1)
                        V.tensor_scalar(stage[:, b, t, :], ps[2 + t][:, 0:CW], rstd_x[:, t:t + 1], None, ALU.mult)\
                            .then_inc(drained[2 + t], 1)

            drain_projection(0)
            with dve.Fori(1, CHUNKS // 2) as i:
                drain_projection(i)
            for j in range(4):
                c, m = divmod(j, 2)
                dve.wait_ge(full[6], j + 1)
                if j:
                    dve.wait_ge(full[7], j)
                dst = mv[:, m, 2 * c:2 * c + 2, :]
                kv = ps[6][:, :].rearrange("p (h n) -> p h n", n=2 * XD)
                V.tensor_scalar(dst, kv[:, :, XD:2 * XD], rstd_m[:, m:m + 1], None, ALU.mult)
                keys = tmp[:, 0:512].rearrange("p (h n) -> p h n", n=2 * XD)[:, :, 0:XD]
                sqk = tmp[:, 512:768].rearrange("p (h n) -> p h n", n=XD)
                V.tensor_scalar(keys, kv[:, :, 0:XD], rstd_m[:, m:m + 1], None, ALU.mult).then_inc(drained[6], 1)
                dve.wait_ge(drained[6], j + 1)
                link(V.tensor_tensor(sqk, keys, keys, ALU.mult))
                link(V.tensor_reduce(mem_st, sqk, AX.X, ALU.add))
                link(V.tensor_scalar(mem_st, mem_st, 1.0 / XD, None, ALU.mult))
                y = rsqrt(link, mem_st, 2)
                link(V.tensor_tensor(keys, keys, y.rearrange("p (h o) -> p h o", o=1).broadcast_to((P, 2, XD)), ALU.mult))
                V.tensor_tensor(keys, keys, mkrow[:, :].rearrange("p (o n) -> p o n", o=1).broadcast_to((P, 2, XD)),
                                ALU.mult).then_inc(s_mem_keys, 1)
                dve.wait_ge(full[7], j + 1)
                V.tensor_copy(mkT[:, 2 * c:2 * c + 2, m * P:(m + 1) * P],
                              ps[7][:, 0:256].rearrange("p (h n) -> p h n", n=P)).then_inc(drained[7], 1)
            dve.wait_ge(s_rope, 2)
            V.memset(kT[:, :], 0.0).then_inc(s_ready, 1)
            setup_links = _n["n"]

            def topk(link, rows, vals, inds, heads):
                dve.nop(nofuse=True)
                for h in heads:
                    ins = V.max(vals[:, h, 0:8], rows[:, h, :])
                link(ins, hold=True)
                for h in heads:
                    V.max_index(inds[:, h, 0:8], vals[:, h, 0:8], rows[:, h, :])
                for h in heads:
                    ins = V.match_replace(rows[:, h, :], vals[:, h, 0:8], rows[:, h, :], -3.0e38)
                link(ins, hold=True)
                for h in heads:
                    ins = V.max(vals[:, h, 8:16], rows[:, h, :])
                link(ins, hold=True)
                for h in heads:
                    ins = V.max_index(inds[:, h, 8:16], vals[:, h, 8:16], rows[:, h, :])
                link(ins)

            def merge(link, t, br):
                dve.wait_ge(*event("gate_tanh", t, br + 1))
                dst = merged if br == 0 else tmp
                for i, name in enumerate((f"y{br}a", f"y{br}b")):
                    part = slice(i * 512, i * 512 + 512)
                    dve.wait_ge(*computed(name, t))
                    V.scalar_tensor_tensor(out=dst[:, part], in0=gt[:, part], scalar=1.0, in1=ps[BANK[name]][:, :],
                                           op0=ALU.add, op1=ALU.mult).then_inc(DRAINED[name], 1)
                dve.wait_ge(*in_sbuf(f"y{br}a", t))
                dve.wait_ge(*in_sbuf(f"y{br}b", t))
                if br == 1:
                    link(V.tensor_tensor(merged[:, :], merged[:, :], tmp[:, :], ALU.add))
                if br == 2:
                    V.tensor_tensor(merged[:, :], merged[:, :], tmp[:, :], ALU.add).then_inc(ev["merged"], 1)

            def spread(x, heads, n):
                return x.rearrange("p (h o) -> p h o", o=1).broadcast_to((P, heads, n))

            def front(t):
                link, n = make_link(dve_chain, setup_links + t * DVE_LINKS)
                r = pa[:, R_Q:R_Q + 2 * HR * RK].rearrange("p (h n) -> p h n", n=RK)
                yield STEP["latent_rstd"]
                link(V.tensor_copy(ropet[:, :, :].rearrange("p i n -> p (i n)").rearrange("p (o n) -> p o n", o=1),
                                   rope[:, :, :, :].rearrange("p t i n -> p t (i n)")[:, bass.ds(t, 1), :]))
                cos_a, sin_a = ropet[:, 0, 0:16], ropet[:, 1, 0:16]
                cos_r, sin_r = ropet[:, 0, 16:48], ropet[:, 1, 16:48]
                dve.wait_ge(*event("c_stats", t))
                y = rsqrt(link, c_st, 6)
                V.tensor_copy(c_st, y).then_inc(ev["c_rstd"], 1)
                yield STEP["latent_scale"]
                dve.wait_ge(*event("c_rstd", t))
                rotate(link, r, 32, cos_r, sin_r, 2 * HR).then_inc(ev["r_roped"], 1)
                dve.wait_ge(*event("r_roped", t))
                V.tensor_tensor(kz[:, :, :], r[:, HR:2 * HR, :], spread(zeta, HR, RK), ALU.mult).then_inc(ev["kz"], 1)
                yield STEP["turn_ret"]
                dve.wait_ge(*computed("rqT", t))
                V.tensor_copy(rqT[:, :, :], ps[BANK["rqT"]][0:RK, :])
                V.tensor_tensor(rxT[:, :, :], ps[BANK["rqT"]][0:RK, :], xiT, ALU.mult).then_inc(DRAINED["rqT"], 1)
                dve.wait_ge(*computed("rkT", t))
                V.tensor_scalar(rkT[:, :, :], ps[BANK["rkT"]][0:RK, :], RK ** -0.5, None, ALU.mult).then_inc(DRAINED["rkT"], 1)
                yield STEP["q_proj"]
                for i in range(2):
                    dve.wait_ge(*computed(f"q{i}", t))
                    V.tensor_copy(qk[:, 4 * i:4 * i + 4, :], ps[BANK[f"q{i}"]][:, 0:384]).then_inc(DRAINED[f"q{i}"], 1)
                yield STEP["kv_proj"]
                for i in range(2):
                    dve.wait_ge(*computed(f"kv{i}", t))
                    bank = ps[BANK[f"kv{i}"]][:, :].rearrange("p (h n) -> p h n", n=NOPE + VD)
                    V.tensor_copy(qk[:, HA + 4 * i:HA + 4 * i + 4, 0:NOPE], bank[:, :, 0:NOPE])
                    V.tensor_copy(vc[:, bass.ds(t, 1), 256 * i:256 * i + 256].rearrange("p o (h n) -> p (o h) n", n=VD),
                                  bank[:, :, NOPE:NOPE + VD]).then_inc(DRAINED[f"kv{i}"], 1)
                link(V.tensor_copy(qk[:, HA:2 * HA, NOPE:QK], pa[:, C_KR:C_KR + ROPE].rearrange(
                    "p (o n) -> p o n", o=1).broadcast_to((P, HA, ROPE))))
                yield STEP["ret_scores"]
                dve.wait_ge(*computed("rin", t))
                V.tensor_tensor(inner[:, :, :], ps[BANK["rin"]][:, :], decayT, ALU.mult).then_inc(DRAINED["rin"], 1)
                yield STEP["qk_stats"]
                link(V.tensor_tensor(sq, qk, qk, ALU.mult))
                link(V.tensor_reduce(qk_st, sq, AX.X, ALU.add))
                yield STEP["ret_out"]
                link(V.tensor_scalar(qk_st, qk_st, 1.0 / QK, None, ALU.mult))
                y = rsqrt(link, qk_st, 2 * HA)
                link(V.tensor_copy(qk_st, y))
                yield STEP["qk_norm"]
                link(V.tensor_tensor(qk, qk, spread(qk_st, 2 * HA, QK), ALU.mult))
                for i in range(2):
                    half = qk[:, HA * i:HA * i + HA, :]
                    ins = V.tensor_tensor(half, half, qkrow[:, i, :].rearrange("p (o n) -> p o n", o=1)
                                          .broadcast_to((P, HA, QK)), ALU.mult)
                link(ins)
                yield STEP["qk_rope"]
                rotate(link, qk[:, :, NOPE:QK], ROPE // 2, cos_a, sin_a, 2 * HA).then_inc(ev["qk_roped"], 1)
                dve.wait_ge(*computed("rinc", t))
                for h in range(HR):
                    ins = V.scalar_tensor_tensor(out=state[:, h, :], in0=state[:, h, :], scalar=CHUNK_DECAY[h],
                                                 in1=ps[BANK["rinc"]][0:RK, h * RV:(h + 1) * RV], op0=ALU.mult, op1=ALU.add)
                ins.then_inc(DRAINED["rinc"], 1)
                yield STEP["ret_norm"]
                dve.wait_ge(*event("ro_stats", t))
                y = rsqrt(link, ro_st, HR)
                dve.wait_ge(*in_sbuf("ro", t))
                link(V.tensor_tensor(ro[:, :, :], ro[:, :, :], spread(y, HR, RV), ALU.mult))
                dve.wait_ge(*event("rg_tanh", t))
                flat = ro[:, :, :].rearrange("p h n -> p (h n)")
                link(V.tensor_tensor(flat, flat, gnrow[:, :], ALU.mult))
                link(V.scalar_tensor_tensor(out=rth[:, :], in0=rth[:, :], scalar=1.0, in1=pa[:, R_G:R_G + 512],
                                            op0=ALU.add, op1=ALU.mult))
                V.tensor_tensor(flat, flat, rth[:, :], ALU.mult).then_inc(ev["ro_done"], 1)
                for h in range(HA):
                    yield STEP[f"att{h + 1}"]
                    if h == 0:
                        dve.wait_ge(s_mask, 16 * (t + 1))
                    dve.wait_ge(*computed(f"s{h}", t))
                    if h >= 2:
                        dve.wait_ge(*computed(f"pT{h - 2}", t))
                    dve.nop(nofuse=True)
                    V.tensor_tensor_reduce(out=ssb[:, h % 2, :], in0=ps[BANK[f"s{h}"]][:, :], in1=mask[:, :],
                                           scale=-ATT_SCALE, scalar=3.0e38, op0=ALU.add, op1=ALU.min,
                                           accum_out=nmax[:, h:h + 1]).then_inc(DRAINED[f"s{h}"], 1)
                yield STEP["att_out"]
                dve.wait_ge(*computed("o", t))
                link(V.reciprocal(l_att, l_att))
                V.tensor_tensor(ob[:, :].rearrange("p (h n) -> p h n", n=VD),
                                ps[BANK["o"]][:, :].rearrange("p (h n) -> p h n", n=VD), spread(l_att, HA, VD), ALU.mult)\
                    .then_inc(DRAINED["o"], 1)
                yield STEP["y0"]
                merge(link, t, 0)
                yield STEP["y1"]
                merge(link, t, 1)
                yield STEP["mem_scores"]
                for i in range(2):
                    dve.wait_ge(*computed(f"ms{i}", t))
                    link(V.tensor_reduce(mmax[:, 2 * i:2 * i + 2],
                                         ps[BANK[f"ms{i}"]][:, :].rearrange("p (h n) -> p h n", n=M), AX.X, ALU.max))
                    V.tensor_scalar(mmax[:, 2 * i:2 * i + 2], mmax[:, 2 * i:2 * i + 2], -MEM_SCALE, None, ALU.mult)\
                        .then_inc(ev["mem_max"], 1)
                yield STEP["mem_out"]
                dve.wait_ge(*computed("mo", t))
                link(V.reciprocal(l_mem, l_mem))
                V.tensor_tensor(ob[:, :].rearrange("p (h n) -> p h n", n=XD),
                                ps[BANK["mo"]][:, :].rearrange("p (h n) -> p h n", n=XD), spread(l_mem, HX, XD), ALU.mult)\
                    .then_inc(DRAINED["mo"], 1)
                yield STEP["y2"]
                merge(link, t, 2)
                for i, (step, name) in enumerate((("h_a", "ha"), ("h_b", "hb"))):
                    yield STEP[step]
                    if i == 0:
                        dve.wait_ge(s_h, 16 * (t + 1))
                    part = slice(i * 512, i * 512 + 512)
                    dve.wait_ge(*computed(name, t))
                    V.tensor_tensor(h_next[:, part], ps[BANK[name]][:, :], h_next[:, part], ALU.add)\
                        .then_inc(DRAINED[name], 1)
                yield STEP["f_rstd"]
                dve.wait_ge(*event("f_stats", t))
                y = rsqrt(link, f_st, 1)
                V.tensor_copy(f_st, y).then_inc(ev["f_rstd"], 1)
                yield STEP["xn"]
                dve.wait_ge(*event("xn_scaled", t))
                V.tensor_tensor(xn_next, xn_next, grow[:, :], ALU.mult).then_inc(ev["xn_done"], 1)
                for c in range(4):
                    yield STEP[f"score{c + 1}" if c < 3 else "top3"]
                    dve.wait_ge(*in_sbuf(f"sc{c}", t))
                    topk(link, scores, topv, topi, range(4 * c, 4 * c + 4))
                yield STEP["sums"]
                sides = topv[:, :, :].rearrange("p (h c) k -> p h c k", c=2)
                V.tensor_copy(nplace, topi[:, :, :])
                link(V.tensor_tensor(cand.rearrange("p h (i j) -> p h i j", j=TOP),
                                     sides[:, :, 0, :].rearrange("p h (k o) -> p h k o", o=1)
                                     .broadcast_to((P, HP, TOP, TOP)),
                                     sides[:, :, 1, :].rearrange("p h (o k) -> p h o k", o=1)
                                     .broadcast_to((P, HP, TOP, TOP)), ALU.add))
                for i in range(2):
                    yield STEP[f"best{i}"]
                    topk(link, cand, topv, topi, range(4 * i, 4 * i + 4))
                V.tensor_tensor(besub, bval, bval[:, :, 0:1].broadcast_to((P, HP, TOP)), ALU.subtract)\
                    .then_inc(ev["best_sub"], 1)
                sides = nplace.rearrange("p (h c) k -> p h c k", c=2)
                for side, (dst, op, arg) in enumerate(((seli, ALU.logical_shift_right, 4), (seli2, ALU.bitwise_and, 15))):
                    yield STEP[f"place{side}"]
                    link(V.tensor_scalar(topi[:, HP:2 * HP, :], topi[:, 0:HP, :], arg, None, op))
                    link(V.tensor_copy(dst, topi[:, HP:2 * HP, :]))
                    link(V.tensor_tensor(hot, dst.rearrange("p h (k o) -> p h k o", o=1).broadcast_to((P, HP, TOP, TOP)),
                                         iota.rearrange("p (a b j) -> p a b j", a=1, b=1)
                                         .broadcast_to((P, HP, TOP, TOP)), ALU.is_equal))
                    link(V.tensor_tensor(hot, hot, sides[:, :, side, :].rearrange("p h (o j) -> p h o j", o=1)
                                         .broadcast_to((P, HP, TOP, TOP)), ALU.mult))
                    link(V.tensor_reduce(dst, hot, AX.X, ALU.add))
                yield STEP["gates"]
                link(V.scalar_tensor_tensor(out=idxn[:, :].rearrange("p (h k) -> p h k", k=TOP), in0=seli,
                                            scalar=float(NK), in1=seli2, op0=ALU.mult, op1=ALU.add))
                dve.wait_ge(*event("best_exp", t))
                link(V.tensor_reduce(gsum, besub, AX.X, ALU.add))
                link(V.reciprocal(gsum, gsum))
                link(V.tensor_scalar(gsum, gsum, 0.5, None, ALU.mult))
                link(V.tensor_tensor(gaten[:, :].rearrange("p (h k) -> p h k", k=TOP), besub,
                                     spread(gsum, HP, TOP), ALU.mult))
                assert n["n"] == DVE_LINKS, n["n"]

            nplace = merged[:, 0:256].rearrange("p (h k) -> p h k", k=TOP)

            def handoff(t):
                V.tensor_copy(idx[:, :], idxn[:, :])
                V.tensor_copy(gate[:, :], gaten[:, :])
                V.tensor_copy(xn_cur, xn_next)
                V.tensor_copy(h_cur, h_next).then_inc(ev["handed"], 1)
                dve.wait_ge(*event("handed", t))

            def peer(t, h, k0):
                if h == HP:
                    return
                for k in range(k0, k0 + QUANTUM):
                    dve.wait_ge(u_in[k % RING], 16 * (t * (HP * TOP // RING) + h * (TOP // RING) + k // RING + 1))
                    V.tensor_tensor_reduce(out=ub[:, k % RING, :], in0=ub[:, k % RING, :], in1=xn_cur, scale=1.0,
                                           scalar=0.0, op0=ALU.mult, op1=ALU.add, accum_out=acts[:, 0, k:k + 1])\
                        .then_inc(dots, 1)
                if k0 + QUANTUM < TOP:
                    return
                link, n = make_link(peer_chain, t * PEER_LINKS + h * 3)
                dve.wait_ge(dots, RING + t * (HP * TOP) + (h + 1) * TOP)
                x, c = acts[:, 0, :], acts[:, 1, :]
                link(V.tensor_tensor(c, x, x, ALU.mult))
                link(V.tensor_scalar(c, c, GELU_B, 1.0, ALU.mult, ALU.add))
                V.tensor_tensor(acts[:, 2, :], c, x, ALU.mult).then_inc(gelu_in, 1)
                link(V.tensor_tensor(acts[:, 3, :], x, gate[:, h * TOP:(h + 1) * TOP], ALU.mult))
                dve.wait_ge(gelu_tanh, t * HP + h + 1)
                V.scalar_tensor_tensor(out=wts[:, h % 2, :], in0=acts[:, 2, :], scalar=1.0, in1=acts[:, 3, :],
                                       op0=ALU.add, op1=ALU.mult).then_inc(s_wts, 1)

            def finish(t):
                dve.wait_ge(v_used, RING + (t + 1) * HP * TOP)
                if isinstance(t, int):
                    dve.wait_ge(s_out, 16 * t)
                for i in range(2):
                    ins = V.tensor_tensor(res[:, i * 512:i * 512 + 512], ps[i][:, :], h_cur[:, i * 512:i * 512 + 512], ALU.add)
                ins.then_inc(s_taken, 1)
                dve.wait_ge(s_taken, t + 2)

            weave(front, peer, dve, finish, handoff)


_LG = np.log(1.0 - 2.0 ** (-5.0 - np.arange(HR, dtype=np.float32))).astype(np.float32)
CHUNK_DECAY = [float(x) for x in np.exp(_LG * np.float32(P))]


def weave(front, peer, eng, finish=None, handoff=None):
    for _ in front(0):
        pass
    if handoff:
        handoff(0)
    with eng.Fori(1, T) as t:
        steps = front(t)
        reached = next(steps)
        for q in range(QUANTA):
            h, k = divmod(q * QUANTUM, TOP)
            peer(t - 1, h, k)
            while reached is not None and reached * QUANTA < (q + 1) * len(STEPS):
                reached = next(steps, None)
        if finish:
            finish(t - 1)
            handoff(t)
    for q in range(QUANTA):
        h, k = divmod(q * QUANTUM, TOP)
        peer(T - 1, h, k)
    if finish:
        finish(T - 1)


_DIRECT = ["x", "mem", "ffn_norm_g", "ret_gn_g", "mla_qn_g", "mla_kn_g", "x_kn_g", "w_uq", "w_ukv", "w_o_mla", "w_o_ret", "w_o_cross", "w_out",
           "w_mem_kv", "peer_w_q"]


def kernel(**inputs):
    import concourse.bacc as _bacc
    from concourse.bass_utils import run_bass_kernel_spmd as _run

    f = np.float32
    laid = {n: np.asarray(inputs[n]) for n in _DIRECT}
    laid["positions"] = np.asarray(inputs["positions"])[0].reshape(T, P).T
    for n in ("attn_norm_g", "mem_norm_g", "mla_q_norm_g", "mla_kv_norm_g", "x_qn_g"):
        laid[n] = np.asarray(inputs[n])[0].reshape(-1, P).T
    laid["xT"] = np.asarray(inputs["x"])[0].T
    laid["memT"] = np.asarray(inputs["mem"])[0].T
    laid["w_in"] = np.asarray(inputs["w_in"])[0].reshape(KD, P, CHUNKS, CW).transpose(2, 1, 0, 3)
    laid["keysT"] = np.asarray(inputs["peer_keys"])[0].reshape(2 * HP, NK, P).transpose(2, 0, 1)
    laid["peer_u"] = np.asarray(inputs["peer_u"])[0]
    laid["peer_v"] = np.asarray(inputs["peer_v"])[0]
    i = np.arange(P, dtype=f)
    diff = i[None, :] - i[:, None]
    c = np.zeros((P, K_END), f)
    c[:, K_ID:K_ID + P] = np.eye(P, dtype=f)
    for h in range(HR):
        c[:, K_DECAY + h * P:K_DECAY + (h + 1) * P] = np.where(diff >= 0, np.exp(_LG[h] * np.maximum(diff, 0)), 0)
        c[:, K_XI + h * P:K_XI + (h + 1) * P] = np.exp(_LG[h] * (i + 1))[None, :]
        c[:, K_ZETA + h] = np.exp(_LG[h] * (P - 1 - i)) * f(RK ** -0.5)
    c[:, K_IOTA:K_IOTA + TOP] = np.arange(TOP)
    for at, d in ((K_INV, ROPE), (K_INV + ROPE // 2, RK)):
        c[:, at:at + d // 2] = np.power(f(10000.0), -np.arange(0, d, 2, dtype=f) / f(d))
    laid["consts"] = c
    laid["mask"] = np.where(np.arange(S)[None, :] <= np.arange(S)[:, None], f(0), f(NEG))

    nc = _bacc.Bacc("TRN2", target_bir_lowering=False, num_devices=1)
    arrays, aps = {}, {}
    for name, arr in laid.items():
        arr = np.ascontiguousarray(arr)
        arrays["in_" + name] = arr
        aps[name] = nc.dram_tensor("in_" + name, arr.shape, mybir.dt.from_np(arr.dtype), kind="ExternalInput").ap()
    out = nc.dram_tensor("out_0", (1, S, D), F32, kind="ExternalOutput").ap()
    build(nc, aps, out)
    r = _run(nc, [arrays], core_ids=[0])
    return r.results[0]["out_0"]
```

```python
from contextlib import ExitStack

import numpy as np

import concourse.bass as bass
from concourse import mybir

F32 = mybir.dt.float32
I32 = mybir.dt.int32
U32 = mybir.dt.uint32
ALU = mybir.AluOpType
ACT = mybir.ActivationFunctionType
AX = mybir.AxisListType

P = 128
D = 1024
S = 512
M = 256
T = S // P
KD = D // P
HA, NOPE, ROPE, VD = 8, 64, 32, 64
QK = NOPE + ROPE
QR, KVR = 384, 128
HR, RK, RV = 4, 64, 128
HX, XD = 4, 128
HP, NK, TOP = 8, 128, 16
EPS = 1e-6
SPLITS = (QR, KVR, ROPE, HR * RK, HR * RK, HR * RV, HR * RV, HX * XD, 3 * D)
OFF = [sum(SPLITS[:i]) for i in range(len(SPLITS))]
(C_Q, C_KV, C_KR, R_Q, R_K, R_V, R_G, X_Q, GATES) = OFF
COLS = sum(SPLITS)
CHUNKS = 12
CW = COLS // CHUNKS
EARLY = 6
NEEDED = [(c, t) for c in range(EARLY, CHUNKS) for t in range(T if c < EARLY + 2 else 1)]
LATE = [(c, t) for c in (CHUNKS - 2, CHUNKS - 1) for t in range(1, T)]
FINAL = [(c, t) for c in (CHUNKS - 4, CHUNKS - 3) for t in range(1, T)]
UNITS = NEEDED + LATE + FINAL
SLOT = KD * 512
NEG = -1e30
ATT_SCALE = QK ** -0.5
MEM_SCALE = XD ** -0.5
RING = 4
GAIN_LOADS, CONSTANT_LOADS = 5, 7
TWO_PI = 6.283185307179586
TP1 = 6.28125
TP2 = float(np.round((TWO_PI - TP1) * 2 ** 24) / 2 ** 24)
TP3 = TWO_PI - TP1 - TP2
PI_LOW = 3.1415925
ROUND = 12582912.0
GELU_A, GELU_B = 0.7978845608028654, 0.044715

K_ID = 0
K_DECAY = K_ID + P
K_XI = K_DECAY + HR * P
K_ZETA = K_XI + HR * P
K_IOTA = K_ZETA + HR
K_INV = K_IOTA + TOP
K_END = K_INV + 48

FRONT_USES = ([("cT", 4), ("xqT", 5), ("q0", 2), ("q1", 3), ("kv0", 2), ("kv1", 3),
               ("rqT", 4), ("rkT", 5), ("rin", 6), ("ro", 7), ("rinc", 6),
               ("qT0", 4), ("qT1", 5), ("kT0", 4), ("kT1", 5)]
              + [u for h in range(HA) for u in ((f"s{h}", 2 + h % 2), (f"pT{h}", 4 + h % 2))]
              + [("o", 7), ("oT", 4), ("y0a", 2), ("y0b", 3), ("roT", 5), ("y1a", 2), ("y1b", 3),
                 ("ms0", 6), ("ms1", 7), ("mp0", 4), ("mp1", 5), ("mo", 6), ("moT", 4),
                 ("y2a", 2), ("y2b", 3), ("mT0", 4), ("mT1", 5), ("ha", 2), ("hb", 3),
                 ("xT0", 4), ("xT1", 5)]
              + [u for c in range(4) for u in ((f"pq{c}", 6 + c % 2), (f"sc{c}", 2 + c % 2))])
SETUP_USES = {2: EARLY, 3: EARLY, 4: EARLY, 5: EARLY, 6: 4, 7: 4}
BANK, ORDER, PER_BANK = {}, {}, {b: 0 for b in SETUP_USES}
for _name, _bank in FRONT_USES:
    BANK[_name], ORDER[_name] = _bank, PER_BANK[_bank]
    PER_BANK[_bank] += 1

EVENTS = {"c_stats": 6, "c_rstd": 1, "c_normed": 6, "r_roped": 1, "kz": 1, "rg_tanh": 1,
          "qk_roped": 1, "ro_stats": 4, "ro_done": 1, "p_exp": HA, "gate_tanh": 3, "merged": 1, "mem_max": 2,
          "f_stats": 1, "f_rstd": 1, "xn_scaled": 1, "xn_done": 1, "best_sub": 1, "best_exp": 1, "handed": 1, "handed_rest": 1}
LAST_PRODUCT = ["kv1", "y0b", "y1b", "y2b", "ha", "hb", "pq0", "pq1", "pq2", "pq3"]
CHUNKS_PER_TILE = len(LAST_PRODUCT)
KEPT = HP - 2
DVE_LINKS = 150
PEER_LINKS = HP * 3


STEPS = (["stats", "latent_rstd", "latent_scale", "turn_latents", "turn_ret", "q_proj", "kv_proj", "ret_scores",
          "qk_stats", "ret_out", "qk_norm", "qk_rope", "turn_q", "turn_k", "ret_norm"]
         + [f"att{i}" for i in range(HA + 3)]
         + ["att_out", "turn_o", "y0", "turn_ro", "y1", "mem_scores", "mem_probs", "mem_turn", "mem_out", "turn_mo", "y2",
            "turn_merged", "h_a", "h_b", "f_stats", "f_rstd", "xn", "turn_xn"]
         + [f"{n}{c}" for c in range(4) for n in ("query", "query_end", "score")]
         + ["top3", "choice3", "place3"])
STEP = {name: i for i, name in enumerate(STEPS)}
QUANTUM = 2
QUANTA = (HP - 1) * TOP // QUANTUM
WEIGHTS = [1.8 if i >= STEP["query1"] else 1.0 for i in range(len(STEPS))]
PLACE = [sum(WEIGHTS[:i]) / (sum(WEIGHTS) + 1) for i in range(len(STEPS))]
UNITS_FIRST = 2
UNITS_AFTER = {"stats": 1, "latent_rstd": 1, "latent_scale": 1, "qk_stats": 1, "ret_out": 1, "qk_norm": 1,
               "qk_rope": 1, "att0": 1, "att2": 1, "att4": 1, "score3": 2, "top3": 4}
assert UNITS_FIRST + sum(UNITS_AFTER.values()) == len(NEEDED + LATE)


def build(nc, a, out):
    with ExitStack() as ctx:
        def sb(name, shape, dt=F32):
            return ctx.enter_context(nc.sbuf_tensor(name, shape, dt))

        def sem(name):
            return ctx.enter_context(nc.semaphore(name))

        wring = sb("wring", [P, 2, SLOT])
        ub = sb("ub", [P, RING, D])
        vb = sb("vb", [P, RING, D])
        pa = sb("pa", [P, GATES])
        gt = sb("gt", [P, D])
        kT = sb("kT", [P, HA * S])
        vc = sb("vc", [P, T, HA * VD])
        mkT = sb("mkT", [P, HX, M])
        mv = sb("mv", [P, 2, HX, XD])
        keysT = sb("keysT", [P, 2 * HP, NK])
        hx = sb("hx", [P, 4, D])
        mT = sb("mT", [P, KD, P])
        work = sb("work", [P, 4096])
        ssb = sb("ssb", [P, 2, S])
        pT = sb("pT", [P, 2, S])
        ob = sb("ob", [P, 512])
        oT = sb("oT", [P, 4, P])
        merged = sb("merged", [P, D])
        tmp = sb("tmp", [P, D])
        xqT = sb("xqT", [P, 4, P])
        kz = sb("kz", [P, HR, RK])
        state = sb("state", [RK, HR, RV])
        ro = sb("ro", [P, HR, RV])
        rth = sb("rth", [P, 512])
        mask = sb("mask", [P, S])
        cst = sb("cst", [P, K_END])
        grow = sb("grow", [P, D])
        gnrow = sb("gnrow", [P, HR * RV])
        qkrow = sb("qkrow", [P, 2, QK])
        mkrow = sb("mkrow", [P, XD])
        gcols = sb("gcols", [P, 2 * KD + 5])
        rope = sb("rope", [P, T, 2, 48])
        ropet = sb("ropet", [P, 2, 48])
        posi = sb("posi", [P, T], I32)
        diag = sb("diag", [P, RING, P])
        small = sb("small", [P, 512])
        topv = sb("topv", [P, 2 * HP, TOP])
        topi = sb("topi", [P, 2 * HP, TOP], U32)
        idx = sb("idx", [P, HP * TOP], U32)
        idxn = sb("idxn", [P, HP * TOP], U32)
        gate = sb("gate", [P, HP * TOP])
        gaten = sb("gaten", [P, HP * TOP])
        acts = sb("acts", [P, 5, TOP])
        wts = sb("wts", [P, 2, TOP])

        ps = [ctx.enter_context(nc.psum_tensor(f"bank{b}", [P, 512], F32)) for b in range(8)]
        proj = nc.dram_tensor("proj_scratch", (S, COLS), F32, kind="Internal").ap()

        ident = cst[:, K_ID:K_ID + P]
        decayT = cst[:, K_DECAY:K_DECAY + HR * P]
        xiT = cst[0:RK, K_XI:K_XI + HR * P]
        zeta = cst[:, K_ZETA:K_ZETA + HR]
        iota = cst[:, K_IOTA:K_IOTA + TOP]
        h_next, xn_next, h_cur, xn_cur = (hx[:, i, :] for i in range(4))
        qk = work[:, 0:2 * HA * QK].rearrange("p (h d) -> p h d", d=QK)
        sq = work[:, 1536:1536 + 1536].rearrange("p (h d) -> p h d", d=QK)
        qT = work[:, 3072:4096].rearrange("p (h n) -> p h n", n=P)
        scores = work[:, 0:2048].rearrange("p (h n) -> p h n", n=NK)
        cand = work[:, 2048:4096].rearrange("p (h n) -> p h n", n=TOP * TOP)
        hot = work[:, 0:2048].rearrange("p (h k j) -> p h k j", k=TOP, j=TOP)
        kTh = kT[:, :].rearrange("p (h s) -> p h s", s=S)
        memT = kT[:, 0:KD * M].rearrange("p (k m) -> p k m", m=M)
        memN = kT[:, KD * M:KD * M + 2 * D].rearrange("p (m d) -> p m d", d=D)
        xT = vb[:, :, :].rearrange("p r d -> p (r d)").rearrange("p (k s) -> p k s", s=S)
        stage = ub[:, :, :].rearrange("p r d -> p (r d)")[:, 0:2 * T * CW].rearrange("p (b t n) -> p b t n", b=2, t=T)
        pqT, cT, res = ssb, oT, merged
        rqT, rkT = mT[0:RK, 0:HR, :], mT[0:RK, HR:2 * HR, :]
        inner = merged[:, 0:HR * P].rearrange("p (h n) -> p h n", n=P)
        rxT = merged[0:RK, HR * P:2 * HR * P].rearrange("p (h n) -> p h n", n=P)
        rstd_x, rstd_m, c_st, qk_st = small[:, 0:4], small[:, 4:6], small[:, 8:14], small[:, 16:32]
        ro_st, f_st, mem_st, l_att = small[:, 32:36], small[:, 36:37], small[:, 40:42], small[:, 48:56]
        nmax, mmax, l_mem, gsum = small[:, 56:64], small[:, 64:68], small[:, 68:72], small[:, 72:80]
        nwt = small[:, 80:112]
        posf = small[:, 112:116]
        seli = small[:, 128:256].rearrange("p (h k) -> p h k", k=TOP)
        seli2 = small[:, 256:384].rearrange("p (h k) -> p h k", k=TOP)
        besub = small[:, 384:512].rearrange("p (h k) -> p h k", k=TOP)

        s_gains, s_const, s_keys = sem("gains_in"), sem("constants_in"), sem("sub_keys_in")
        s_x, s_xT, s_memT, s_memN = sem("x_in"), sem("xT_in"), sem("memoryT_in"), sem("memory_in")
        w_in = [sem("weights_in_0"), sem("weights_in_1")]
        full = {b: sem(f"psum_full_{b}") for b in SETUP_USES}
        drained = {b: sem(f"psum_drained_{b}") for b in SETUP_USES}
        ev = {n: sem("ev_" + n) for n in EVENTS}
        s_parked = [sem("stage_parked_0"), sem("stage_parked_1")]
        s_pa, s_gt, s_h, s_mask = sem("projection_in"), sem("gates_in"), sem("residual_in"), sem("mask_in")
        s_sums, s_rope = sem("setup_sums"), sem("setup_rope")
        s_rstd, s_angles, s_mem_g, s_mem_keys = sem("setup_rstd"), sem("setup_angles"), sem("setup_mem_gain"), sem("memory_keys")
        s_x_g, s_ready = sem("setup_x_gain"), sem("setup_ready")
        s_stage_left, s_rest_parked = sem("stage_left"), sem("rest_parked")
        s_extra = sem("first_gate_chunk_in")
        units_done, unit_drained = sem("gate_units_done"), [sem("gate_unit_drained_0"), sem("gate_unit_drained_1")]
        dve_chain, act_chain = sem("dve_chain"), sem("act_chain")
        peer_chain = sem("peer_chain")
        u_in = [sem(f"u_in_{r}") for r in range(RING)]
        v_in = [sem(f"v_in_{r}") for r in range(RING)]
        dots, gelu_in, gelu_tanh = sem("dots_done"), sem("gelu_in"), sem("gelu_tanh")
        s_wts, s_diag, v_used = sem("weights_ready"), sem("diag_ready"), sem("v_used")
        s_taken, s_out = sem("sum_taken"), sem("out_stored")

        FULL = {name: full[b] for name, b in BANK.items()}
        DRAINED = {name: drained[b] for name, b in BANK.items()}

        def bank_free(name, t):
            return DRAINED[name], SETUP_USES[BANK[name]] + t * PER_BANK[BANK[name]] + ORDER[name]

        def computed(name, t):
            return FULL[name], SETUP_USES[BANK[name]] + t * PER_BANK[BANK[name]] + ORDER[name] + 1

        def in_sbuf(name, t):
            return DRAINED[name], SETUP_USES[BANK[name]] + t * PER_BANK[BANK[name]] + ORDER[name] + 1

        def event(name, t, k=None):
            return ev[name], t * EVENTS[name] + (EVENTS[name] if k is None else k)

        def key_tiles(t):
            return 1 if isinstance(t, int) else T

        def unit_of(c, t):
            return UNITS.index((c, t))

        def unit_stage(u):
            c, t = UNITS[u]
            if (c, t) in FINAL:
                return work[:, (u - unit_of(*FINAL[0])) * CW:(u - unit_of(*FINAL[0]) + 1) * CW]
            if t and c == CHUNKS - 1:
                return pa[:, (t - 1) * CW:t * CW]
            return stage[:, c % 2, t, :]

        block = ctx.enter_context(nc.Block())

        @block.sync
        def _(sp):
            def w_in_chunk(i, b):
                if isinstance(i, int):
                    sp.wait_ge(full[7], 2 * b + 1)
                else:
                    sp.wait_ge(full[5], 2 * i + b - 1)
                    sp.nop(nofuse=True)
                sp.dma_start(wring[:, b, 0:KD * CW].rearrange("p (k n) -> p k n", n=CW),
                             a["w_in"][2 * i + b] if isinstance(i, int) else
                             a["w_in"][bass.ds(2 * i + b, 1), :, :, :].rearrange("o p k n -> p (o k) n"))\
                    .then_inc(w_in[b], 16)

            def gate_chunk(c, t):
                b = c % 2
                if (c, t) in FINAL:
                    sp.wait_ge(units_done, unit_of(c + 2, t) + T - 1)
                elif t:
                    sp.wait_ge(*computed(("pq2", "pq3")[b], 0))
                elif c == EARLY:
                    sp.wait_ge(s_rope, 2)
                    sp.dma_start(work[:, 0:KD * CW].rearrange("p (k n) -> p k n", n=CW), a["w_in"][c]).then_inc(s_extra, 16)
                    return
                elif c == EARLY + 1:
                    sp.wait_ge(full[5], EARLY)
                elif c == EARLY + 2:
                    sp.wait_ge(*computed("kv1", 0))
                else:
                    sp.wait_ge(units_done, unit_of(c - 1, 0))
                sp.dma_start(wring[:, b, 0:KD * CW].rearrange("p (k n) -> p k n", n=CW), a["w_in"][c])\
                    .then_inc(w_in[b], 16)

            def park(i, b):
                for t in range(T):
                    sp.wait_ge(drained[2 + t], 2 * i + b + 1)
                sp.nop(nofuse=True)
                sp.dma_start(proj[:, bass.ds((2 * i + b) * CW, CW)].rearrange("(t p) n -> p t n", p=P),
                             stage[:, b, :, :]).then_inc(s_parked[b], 16)

            def park_gates(c, t0):
                u = unit_of(c, t0)
                t1 = 1 if t0 == 0 and c >= EARLY + 2 else T
                n = u + t1 - t0
                sp.wait_ge(unit_drained[0], (n + 1) // 2)
                sp.wait_ge(unit_drained[1], n // 2)
                parked = s_parked[c % 2]
                if t0:
                    parked = s_stage_left if c == CHUNKS - 2 else s_rest_parked
                if (c, t0) in FINAL:
                    at = (u - unit_of(*FINAL[0])) * CW
                    src = work[:, at:at + (t1 - t0) * CW].rearrange("p (t n) -> p t n", n=CW)
                elif t0 and c == CHUNKS - 1:
                    src = pa[:, 0:(t1 - t0) * CW].rearrange("p (t n) -> p t n", n=CW)
                else:
                    src = stage[:, c % 2, t0:t1, :]
                sp.dma_start(proj[t0 * P:t1 * P, c * CW:(c + 1) * CW].rearrange("(t p) n -> p t n", p=P), src)\
                    .then_inc(parked, 16)

            for k, (name, n) in enumerate((("attn_norm_g", KD), ("mem_norm_g", KD), ("mla_q_norm_g", 3),
                                           ("mla_kv_norm_g", 1), ("x_qn_g", 1))):
                at = (0, KD, 2 * KD, 2 * KD + 3, 2 * KD + 4)[k]
                sp.dma_start(gcols[:, at:at + n], a[name]).then_inc(s_gains, 16)
            sp.dma_start(memT, a["memT"].rearrange("(k p) m -> p k m", p=P)).then_inc(s_memT, 16)
            for b in range(2):
                sp.dma_start(wring[:, b, :].rearrange("p (k n) -> p k n", n=512),
                             a["w_mem_kv"].rearrange("o (k p) n -> p (o k) n", p=P)[:, :, b * 512:b * 512 + 512])\
                    .then_inc(w_in[b], 16)
                if b:
                    continue
                sp.dma_start(memN, a["mem"].rearrange("o (m p) d -> p (o m) d", p=P)).then_inc(s_memN, 16)
                sp.dma_start(cst[:, :], a["consts"]).then_inc(s_const, 16)
                sp.dma_start(posi[:, :], a["positions"]).then_inc(s_const, 16)
                for dst, name in ((grow[:, :], "ffn_norm_g"), (gnrow[:, :], "ret_gn_g"), (qkrow[:, 0, :], "mla_qn_g"),
                                  (qkrow[:, 1, :], "mla_kn_g"), (mkrow[:, :], "x_kn_g")):
                    src = a[name]
                    if name == "ret_gn_g":
                        src = src.rearrange("o h d -> o (h d)")
                    sp.dma_start(dst, src.broadcast_to((P, src.shape[1]))).then_inc(s_const, 16)
            sp.dma_start(hx[:, :, :], a["x"].rearrange("o (t p) d -> p (o t) d", p=P)).then_inc(s_x, 16)
            sp.dma_start(xT, a["xT"].rearrange("(k p) s -> p k s", p=P)).then_inc(s_xT, 16)
            w_in_chunk(0, 0)
            sp.dma_start(keysT[:, :, :], a["keysT"]).then_inc(s_keys, 16)
            w_in_chunk(0, 1)
            with sp.Fori(1, EARLY // 2) as i:
                for b in range(2):
                    w_in_chunk(i, b)
                    park(i - 1, b)

            def chunk_sources():
                for name in ("w_o_mla", "w_o_ret", "w_o_cross"):
                    yield a[name].rearrange("o (k p) n -> p (o k) n", p=P), 1024, 4
                w_out = a["w_out"].rearrange("o (k p) n -> p (o k) n", p=P)
                for c in range(2):
                    yield w_out[:, :, c * 512:c * 512 + 512], 512, 8
                w_q = a["peer_w_q"].rearrange("o (k p) n -> p (o k) n", p=P)
                for c in range(4):
                    yield w_q[:, :, c * 512:c * 512 + 512], 512, 8

            def weights(t, c):
                b = c % 2
                if c >= 2:
                    sp.wait_ge(*computed(LAST_PRODUCT[c - 2], t))
                else:
                    sp.wait_ge(*computed(LAST_PRODUCT[c - 2], t - 1))
                sp.nop(nofuse=True)
                load_weights(c)

            def load_weights(c):
                b = c % 2
                if c == 0:
                    sp.dma_start(wring[:, b, 0:3 * HA * QK].rearrange("p (k n) -> p k n", n=HA * QK),
                                 a["w_uq"].rearrange("o (k p) n -> p (o k) n", p=P)).then_inc(w_in[b], 16)
                    sp.dma_start(wring[:, b, 2304:2304 + 1024], a["w_ukv"].rearrange("o p n -> (o p) n"))\
                        .then_inc(w_in[b], 16)
                else:
                    src, n, k = list(chunk_sources())[c - 1]
                    sp.dma_start(wring[:, b, :].rearrange("p (k n) -> p k n", n=n), src).then_inc(w_in[b], 16)

            def front(t):
                rows = bass.ds(t * P, P)
                sp.wait_ge(*event("ro_done", t - 1))
                sp.nop(nofuse=True)
                sp.dma_start(pa[:, :], proj[rows, 0:GATES]).then_inc(s_pa, 16)
                sp.wait_ge(*in_sbuf(f"s{HA - 1}", t - 1))
                sp.nop(nofuse=True)
                sp.dma_start(mask[:, :], a["mask"][rows, :]).then_inc(s_mask, 16)
                sp.wait_ge(*event("handed_rest", t - 1))
                sp.nop(nofuse=True)
                sp.dma_start(h_next, a["x"].rearrange("o s d -> (o s) d")[rows, :]).then_inc(s_h, 16)
                weights(t, 0)
                weights(t, 1)
                for br in range(3):
                    sp.wait_ge(*in_sbuf(f"y{(br - 1) % 3}b", t if br else t - 1))
                    sp.nop(nofuse=True)
                    sp.dma_start(gt[:, :], proj[rows, GATES + br * D:GATES + br * D + D]).then_inc(s_gt, 16)
                    weights(t, 2 + br)
                for c in range(5, CHUNKS_PER_TILE):
                    weights(t, c)

            def store(t):
                sp.wait_ge(s_taken, t + 2)
                sp.nop(nofuse=True)
                sp.dma_start(out.rearrange("o s d -> (o s) d")[bass.ds(t * P, P), :], res[:, :]).then_inc(s_out, 16)
                sp.wait_ge(s_out, 16 * (t + 1))
                sp.nop(nofuse=True)

            def first_front():
                sp.wait_ge(full[5], EARLY - 1)
                load_weights(0)
                gate_chunk(EARLY, 0)
                park(EARLY // 2 - 1, 0)
                gate_chunk(EARLY + 1, 0)
                park(EARLY // 2 - 1, 1)
                sp.dma_start(mask[:, :], a["mask"][0:P, :]).then_inc(s_mask, 16)
                for b in range(2):
                    sp.wait_ge(s_parked[b], 16 * (EARLY // 2))
                sp.dma_start(pa[:, :], proj[0:P, 0:GATES]).then_inc(s_pa, 16)
                sp.wait_ge(s_ready, 1)
                sp.dma_start(h_next, a["x"][0, 0:P, :]).then_inc(s_h, 16)
                for c in range(EARLY + 2, CHUNKS):
                    park_gates(c - 2, 0)
                    gate_chunk(c, 0)
                park_gates(CHUNKS - 2, 0)
                sp.wait_ge(units_done, len(NEEDED))
                load_weights(1)
                for br in range(3):
                    for b in range(2):
                        sp.wait_ge(s_parked[b], 16 * (EARLY // 2 + br + 1))
                    if br:
                        sp.wait_ge(*in_sbuf(f"y{br - 1}b", 0))
                    sp.dma_start(gt[:, :], proj[0:P, GATES + br * D:GATES + br * D + D]).then_inc(s_gt, 16)
                    if br == 0:
                        park_gates(CHUNKS - 1, 0)
                        sp.wait_ge(units_done, unit_of(CHUNKS - 1, 0))
                        load_weights(2)
                    else:
                        weights(0, 2 + br)
                for c in range(5, CHUNKS_PER_TILE):
                    weights(0, c)
                for c in (CHUNKS - 2, CHUNKS - 1):
                    gate_chunk(c, 1)
                for c in (CHUNKS - 2, CHUNKS - 1):
                    gate_chunk(c - 2, 1)
                    park_gates(c, 1)
                for c in (CHUNKS - 4, CHUNKS - 3):
                    park_gates(c, 1)
                sp.wait_ge(s_stage_left, 16)
                sp.wait_ge(s_rest_parked, 16 * 3)

            first_front()
            with sp.Fori(1, T) as t:
                front(t)
                store(t - 1)
            store(T - 1)

        @block.gpsimd
        def _(pool):
            def gather(dst, table, t, h, k, arrived, used):
                n = t * (HP * TOP) + h * TOP + k
                pool.wait_ge(used, n + 1)
                pool.nop(nofuse=True)
                pool.indirect_dma_start(dst[:, k % RING, :], None, table, bass.IndirectOffsetOnAxis(
                    ap=idx[:, h * TOP + k:h * TOP + k + 1], axis=0)).then_inc(arrived[k % RING], 16)

            def head(u=None, v=None):
                for k in range(TOP):
                    if u:
                        gather(ub, a["peer_u"], *u, k, u_in, dots)
                    if v:
                        gather(vb, a["peer_v"], *v, k, v_in, v_used)

            def heads(t):
                for h in range(1, HP):
                    if h == KEPT:
                        pool.wait_ge(*event("handed_rest", t))
                    head((t, h), (t, h - 1))

            pool.wait_ge(*event("handed", 0))
            for b in range(2):
                pool.wait_ge(s_parked[b], 16 * (CHUNKS // 2))
            pool.wait_ge(s_stage_left, 16)
            head((0, 0))
            pool.wait_ge(units_done, len(UNITS))
            with pool.Fori(1, T) as t:
                heads(t - 1)
                pool.wait_ge(*event("handed", t))
                head((t, 0), (t - 1, HP - 1))
            heads(T - 1)
            head(v=(T - 1, HP - 1))

        @block.scalar
        def _(act):
            A = nc.scalar.activation

            def setup():
                act.wait_ge(s_memN, 16)
                for m in range(2):
                    if m:
                        act.wait_ge(s_sums, m)
                    A(merged[:, :], memN[:, m, :], ACT.Square, scale=D ** -0.5,
                      accum_out=rstd_m[:, m:m + 1]).then_inc(s_sums, 1)
                act.wait_ge(s_x, 16)
                for t in range(T):
                    act.wait_ge(s_sums, 2 + t)
                    A(merged[:, :], hx[:, t, :], ACT.Square, scale=D ** -0.5,
                      accum_out=rstd_x[:, t:t + 1]).then_inc(s_sums, 1)
                act.wait_ge(s_angles, 1)
                for i in range(2):
                    A(rope[:, :, i, :], work[:, 192 * (1 + i):192 * (2 + i)].rearrange("p (t n) -> p t n", n=48),
                      ACT.Sin).then_inc(s_rope, 1)

            def drain_projection(i):
                for b in range(2):
                    for t in (0, 2):
                        act.wait_ge(full[2 + t], 2 * i + b + 1)
                        if not isinstance(i, int):
                            act.wait_ge(s_parked[b], 16 * i)
                        A(stage[:, b, t, :], ps[2 + t][:, 0:CW], ACT.Copy, scale=rstd_x[:, t:t + 1])\
                            .then_inc(drained[2 + t], 1)

            def gate_unit(u):
                c, t = UNITS[u]
                if u % 2 and u < len(NEEDED):
                    return
                act.wait_ge(units_done, u + 1)
                if (c, t) in FINAL:
                    act.wait_ge(*event("handed", 0))
                elif c == CHUNKS - 1 and t:
                    act.wait_ge(*event("ro_done", 0))
                else:
                    act.wait_ge(s_parked[c % 2], 16 * (c // 2 if u < len(NEEDED) else CHUNKS // 2))
                A(unit_stage(u), ps[u % 2][:, 0:CW], ACT.Copy, scale=rstd_x[:, t:t + 1])\
                    .then_inc(unit_drained[u % 2], 1)

            setup()
            act.wait_ge(s_rstd, 1)
            drain_projection(0)
            with act.Fori(1, EARLY // 2) as i:
                drain_projection(i)

            def gate_tanh(t, br):
                act.wait_ge(s_gt, 16 * (3 * t + br + 1))
                A(gt[:, :], gt[:, :], ACT.Tanh, scale=0.5).then_inc(ev["gate_tanh"], 1)

            def front(t):
                yield STEP["stats"]
                act.wait_ge(s_pa, 16 * (t + 1))
                parts = [(C_Q, QR), (C_KV, KVR)] + [(X_Q + h * XD, XD) for h in range(HX)]
                junk = [0, QR] + [QR + KVR + h * XD for h in range(HX)]
                for j, (at, n) in enumerate(parts):
                    A(tmp[:, junk[j]:junk[j] + n], pa[:, at:at + n], ACT.Square, scale=n ** -0.5,
                      accum_out=c_st[:, j:j + 1]).then_inc(ev["c_stats"], 1)
                A(rth[:, :], pa[:, R_G:R_G + 512], ACT.Tanh, scale=0.5).then_inc(ev["rg_tanh"], 1)
                yield STEP["latent_scale"]
                act.wait_ge(*event("c_rstd", t))
                for j, (at, n) in enumerate(parts):
                    A(pa[:, at:at + n], pa[:, at:at + n], ACT.Copy, scale=c_st[:, j:j + 1]).then_inc(ev["c_normed"], 1)
                yield STEP["turn_latents"]
                act.wait_ge(*computed("cT", t))
                bank = ps[BANK["cT"]]
                for j in range(4):
                    ins = A(cT[:, j, :], bank[:, j * P:(j + 1) * P], ACT.Copy, scale=gcols[:, 2 * KD + j:2 * KD + j + 1])
                ins.then_inc(DRAINED["cT"], 1)
                act.wait_ge(*computed("xqT", t))
                bank = ps[BANK["xqT"]]
                A(xqT[:, :, :], bank[:, :], ACT.Copy, scale=gcols[:, 2 * KD + 4:2 * KD + 5]).then_inc(DRAINED["xqT"], 1)
                yield STEP["ret_out"]
                act.wait_ge(*computed("ro", t))
                bank = ps[BANK["ro"]]
                for h in range(HR):
                    A(ob[:, h * RV:(h + 1) * RV], bank[:, h * RV:(h + 1) * RV], ACT.Square, scale=RV ** -0.5,
                      accum_out=ro_st[:, h:h + 1]).then_inc(ev["ro_stats"], 1)
                nc.scalar.copy(ro[:, :, :], bank[:, :]).then_inc(DRAINED["ro"], 1)
                yield STEP["turn_q"]
                for i in range(2):
                    act.wait_ge(*computed(f"qT{i}", t))
                    nc.scalar.copy(qT[0:QK, 4 * i:4 * i + 4, :], ps[BANK[f"qT{i}"]][0:QK, :]).then_inc(DRAINED[f"qT{i}"], 1)
                yield STEP["turn_k"]
                for i in range(2):
                    act.wait_ge(*computed(f"kT{i}", t))
                    act.nop(nofuse=True)
                    nc.scalar.copy(kTh[0:QK, 4 * i:4 * i + 4, bass.ds(t * P, P)],
                                   ps[BANK[f"kT{i}"]][0:QK, :].rearrange("p (h n) -> p h n", n=P))\
                        .then_inc(DRAINED[f"kT{i}"], 1)
                for step in range(HA + 3):
                    yield STEP[f"att{step}"]
                    if 0 <= step - 1 < HA:
                        h = step - 1
                        act.wait_ge(*in_sbuf(f"s{h}", t))
                        rows = ssb[:, h % 2, 0:P * key_tiles(t)]
                        A(rows, rows, ACT.Exp, scale=-1.0, bias=nmax[:, h:h + 1],
                          accum_out=l_att[:, h:h + 1]).then_inc(ev["p_exp"], 1)
                    if 0 <= step - 2 < HA:
                        h = step - 2
                        act.wait_ge(*computed(f"pT{h}", t))
                        keys = P * key_tiles(t)
                        nc.scalar.copy(pT[:, h % 2, 0:keys], ps[BANK[f"pT{h}"]][:, 0:keys]).then_inc(DRAINED[f"pT{h}"], 1)
                yield STEP["turn_o"]
                act.wait_ge(*computed("oT", t))
                nc.scalar.copy(oT[:, :, :], ps[BANK["oT"]][:, :]).then_inc(DRAINED["oT"], 1)
                gate_tanh(t, 0)
                yield STEP["turn_ro"]
                act.wait_ge(*computed("roT", t))
                A(oT[:, :, :], ps[BANK["roT"]][:, :], ACT.Copy, scale=0.5).then_inc(DRAINED["roT"], 1)
                gate_tanh(t, 1)
                yield STEP["mem_probs"]
                for h in range(HX):
                    act.wait_ge(*event("mem_max", t, h // 2 + 1))
                    ins = A(ssb[:, h // 2, (h % 2) * M:(h % 2) * M + M], ps[6 + h // 2][:, (h % 2) * M:(h % 2) * M + M],
                            ACT.Exp, scale=MEM_SCALE, bias=mmax[:, h:h + 1], accum_out=l_mem[:, h:h + 1])
                    if h % 2:
                        ins.then_inc(DRAINED[f"ms{h // 2}"], 1)
                yield STEP["mem_turn"]
                for i in range(2):
                    act.wait_ge(*computed(f"mp{i}", t))
                    nc.scalar.copy(pT[:, i, :], ps[BANK[f"mp{i}"]][:, :]).then_inc(DRAINED[f"mp{i}"], 1)
                yield STEP["turn_mo"]
                act.wait_ge(*computed("moT", t))
                nc.scalar.copy(oT[:, :, :], ps[BANK["moT"]][:, :]).then_inc(DRAINED["moT"], 1)
                gate_tanh(t, 2)
                yield STEP["turn_merged"]
                for i in range(2):
                    act.wait_ge(*computed(f"mT{i}", t))
                    A(mT[:, 4 * i:4 * i + 4, :], ps[BANK[f"mT{i}"]][:, :], ACT.Copy, scale=0.5)\
                        .then_inc(DRAINED[f"mT{i}"], 1)
                yield STEP["f_stats"]
                act.wait_ge(*in_sbuf("ha", t))
                act.wait_ge(*in_sbuf("hb", t))
                A(tmp[:, :], h_next, ACT.Square, scale=D ** -0.5, accum_out=f_st).then_inc(ev["f_stats"], 1)
                yield STEP["xn"]
                act.wait_ge(*event("f_rstd", t))
                A(xn_next, h_next, ACT.Copy, scale=f_st).then_inc(ev["xn_scaled"], 1)
                yield STEP["turn_xn"]
                for i in range(2):
                    act.wait_ge(*computed(f"xT{i}", t))
                    nc.scalar.copy(mT[:, 4 * i:4 * i + 4, :], ps[BANK[f"xT{i}"]][:, :]).then_inc(DRAINED[f"xT{i}"], 1)
                for c in range(4):
                    yield STEP[f"query_end{c}"]
                    act.wait_ge(*computed(f"pq{c}", t))
                    nc.scalar.copy(pqT[:, c % 2, :], ps[BANK[f"pq{c}"]][:, :]).then_inc(DRAINED[f"pq{c}"], 1)
                    yield STEP[f"score{c}"]
                    act.wait_ge(*computed(f"sc{c}", t))
                    nc.scalar.copy(scores[:, 4 * c:4 * c + 4, :], ps[BANK[f"sc{c}"]][:, :]).then_inc(DRAINED[f"sc{c}"], 1)
                yield STEP["choice3"]
                act.wait_ge(*event("best_sub", t))
                A(besub, besub, ACT.Exp).then_inc(ev["best_exp"], 1)

            def peer_tanh(t, h):
                act.wait_ge(gelu_in, t * HP + h + 1)
                A(acts[:, 2, :], acts[:, 2, :], ACT.Tanh, scale=GELU_A).then_inc(gelu_tanh, 1)

            def peer(u, v, k0):
                for k in range(k0, k0 + QUANTUM):
                    if v:
                        t, h = v
                        n = t * (HP * TOP) + h * TOP + k
                        if k == 0:
                            act.wait_ge(s_wts, t * HP + h + 1)
                        act.wait_ge(v_used, n + 1)
                        A(diag[:, k % RING, :], ident, ACT.Copy, scale=wts[:, h % 2, k:k + 1]).then_inc(s_diag, 1)
                if u and k0 + QUANTUM == TOP:
                    peer_tanh(*u)

            weave(front, peer, gate_unit, act)

        @block.tensor
        def _(pe):
            mm, tr = nc.tensor.matmul, nc.tensor.transpose

            def project(i, b):
                pe.wait_ge(w_in[b], 16 * (i + 2))
                w = wring[:, b, 0:KD * CW].rearrange("p (k n) -> p k n", n=CW)
                for t in range(T):
                    if b or not isinstance(i, int):
                        pe.wait_ge(drained[2 + t], 2 * i + b)
                    for k in range(KD):
                        ins = mm(ps[2 + t][:, 0:CW], xT[:, k, t * P:(t + 1) * P], w[:, k, :],
                                 start=(k == 0), stop=(k == KD - 1))
                    ins.then_inc(full[2 + t], 1)

            def slot_loads(b):
                return 1 + EARLY // 2 + (2 if b == 0 else 3)

            def gate_unit(u):
                c, t = UNITS[u]
                b = c % 2
                if c == EARLY:
                    pe.wait_ge(s_extra, 16)
                    w = work[:, 0:KD * CW].rearrange("p (k n) -> p k n", n=CW)
                else:
                    w = wring[:, b, 0:KD * CW].rearrange("p (k n) -> p k n", n=CW)
                    if u < len(NEEDED):
                        loads = 1 + EARLY // 2 + (2 if b == 0 else 0) + (c - EARLY - (0 if b == 0 else 1)) // 2 + b
                    else:
                        loads = slot_loads(b) + 5 + (2 if b == 0 else 1) + (0 if (c, t) in LATE else 1)
                    pe.wait_ge(w_in[b], 16 * loads)
                if u >= 2:
                    pe.wait_ge(unit_drained[u % 2], u // 2)
                for k in range(KD):
                    ins = mm(ps[u % 2][:, 0:CW], xT[:, k, t * P:(t + 1) * P], w[:, k, :],
                             start=(k == 0), stop=(k == KD - 1))
                ins.then_inc(units_done, 1)
                if u == len(UNITS) - 1:
                    pe.wait_ge(unit_drained[0], len(UNITS) // 2)
                    pe.wait_ge(unit_drained[1], len(UNITS) // 2)

            def memory_product(j):
                c, m = divmod(j, 2)
                pe.wait_ge(w_in[c], 16)
                if j >= 2:
                    pe.wait_ge(drained[6 + j % 2], 2)
                w = wring[:, c, :].rearrange("p (k n) -> p k n", n=512)
                for k in range(KD):
                    ins = mm(ps[6 + j % 2][:, :], memT[:, k, m * P:(m + 1) * P], w[:, k, :],
                             start=(k == 0), stop=(k == KD - 1))
                ins.then_inc(full[6 + j % 2], 1)

            def memory_turn(j):
                pe.wait_ge(s_mem_keys, j + 1)
                for h in range(2):
                    ins = tr(ps[6 + j % 2][:, h * P:(h + 1) * P], tmp[:, 256 * j + h * XD:256 * j + (h + 1) * XD], ident)
                ins.then_inc(full[6 + j % 2], 1)

            pe.wait_ge(s_mem_g, 1)
            memory_product(0)
            memory_product(1)
            pe.wait_ge(s_const, 16 * CONSTANT_LOADS)
            memory_turn(0)
            memory_product(2)
            memory_turn(1)
            memory_product(3)
            memory_turn(2)
            pe.wait_ge(s_x_g, 1)
            project(0, 0)
            memory_turn(3)
            project(0, 1)
            pe.wait_ge(s_keys, 16)
            with pe.Fori(1, EARLY // 2) as i:
                project(i, 0)
                project(i, 1)

            def weights(t, c):
                b = c % 2
                if c == 0 and isinstance(t, int):
                    pe.wait_ge(w_in[b], 16 * (1 + EARLY // 2 + 2))
                else:
                    late = 0 if isinstance(t, int) else 2
                    pe.wait_ge(w_in[b], 16 * (slot_loads(b) + late + (2 if b == 0 else 1) + t * (6 if b == 0 else 5) + c // 2))
                return wring[:, b, :]

            def turn(bank, src, n, rows=P):
                for j in range(n):
                    ins = tr(bank[0:rows, j * P:(j + 1) * P], src(j), ident)
                return ins

            def branch_out(t, c, names, src):
                pe.wait_ge(*in_sbuf(src, t))
                w = weights(t, c).rearrange("p (k n) -> p k n", n=1024)
                for i, name in enumerate(names):
                    pe.wait_ge(*bank_free(name, t))
                    bank = ps[BANK[name]]
                    for k in range(4):
                        ins = mm(bank[:, :], oT[:, k, :], w[:, k, i * 512:i * 512 + 512], start=(k == 0), stop=(k == 3))
                    ins.then_inc(FULL[name], 1)

            def front(t):
                yield STEP["turn_latents"]
                pe.wait_ge(*event("c_normed", t))
                pe.wait_ge(*bank_free("cT", t))
                turn(ps[BANK["cT"]], lambda j: pa[:, C_Q + j * P:C_Q + (j + 1) * P], 4).then_inc(FULL["cT"], 1)
                pe.wait_ge(*bank_free("xqT", t))
                turn(ps[BANK["xqT"]], lambda j: pa[:, X_Q + j * P:X_Q + (j + 1) * P], 4).then_inc(FULL["xqT"], 1)
                yield STEP["turn_ret"]
                pe.wait_ge(*event("r_roped", t))
                for name, at in (("rqT", R_Q), ("rkT", R_K)):
                    pe.wait_ge(*bank_free(name, t))
                    pe.nop(nofuse=True)
                    turn(ps[BANK[name]], lambda j: pa[:, at + j * RK:at + (j + 1) * RK], 4, RK).then_inc(FULL[name], 1)
                yield STEP["q_proj"]
                pe.wait_ge(*in_sbuf("cT", t))
                w = weights(t, 0)
                wq = w[:, 0:2304].rearrange("p (k n) -> p k n", n=HA * QK)
                for i in range(2):
                    pe.wait_ge(*bank_free(f"q{i}", t))
                    bank = ps[BANK[f"q{i}"]]
                    for k in range(3):
                        ins = mm(bank[:, 0:384], cT[:, k, :], wq[:, k, i * 384:i * 384 + 384], start=(k == 0), stop=(k == 2))
                    ins.then_inc(FULL[f"q{i}"], 1)
                yield STEP["kv_proj"]
                for i in range(2):
                    pe.wait_ge(*bank_free(f"kv{i}", t))
                    mm(ps[BANK[f"kv{i}"]][:, :], cT[:, 3, :], w[:, 2304 + 512 * i:2304 + 512 * i + 512], start=True, stop=True)\
                        .then_inc(FULL[f"kv{i}"], 1)
                yield STEP["ret_scores"]
                pe.wait_ge(*in_sbuf("rqT", t))
                pe.wait_ge(*in_sbuf("rkT", t))
                pe.wait_ge(*bank_free("rin", t))
                for h in range(HR):
                    ins = mm(ps[BANK["rin"]][:, h * P:(h + 1) * P], rkT[:, h, :], rqT[:, h, :], start=True, stop=True)
                ins.then_inc(FULL["rin"], 1)
                yield STEP["ret_out"]
                pe.wait_ge(*in_sbuf("rin", t))
                pe.wait_ge(*bank_free("ro", t))
                for h in range(HR):
                    o = ps[BANK["ro"]][:, h * RV:(h + 1) * RV]
                    mm(o, inner[:, h, :], pa[:, R_V + h * RV:R_V + (h + 1) * RV], start=True, stop=False)
                    ins = mm(o, rxT[:, h, :], state[:, h, :], start=False, stop=True)
                ins.then_inc(FULL["ro"], 1)
                pe.wait_ge(*event("kz", t))
                pe.wait_ge(*bank_free("rinc", t))
                for h in range(HR):
                    ins = mm(ps[BANK["rinc"]][0:RK, h * RV:(h + 1) * RV], kz[:, h, :],
                             pa[:, R_V + h * RV:R_V + (h + 1) * RV], start=True, stop=True)
                ins.then_inc(FULL["rinc"], 1)
                for step, names in (("turn_q", ("qT0", "qT1")), ("turn_k", ("kT0", "kT1"))):
                    yield STEP[step]
                    pe.wait_ge(*event("qk_roped", t))
                    for name in names:
                        at = ("qT0", "qT1", "kT0", "kT1").index(name)
                        pe.wait_ge(*bank_free(name, t))
                        turn(ps[BANK[name]], lambda j: qk[:, 4 * at + j, :], 4, QK).then_inc(FULL[name], 1)
                for step in range(HA + 3):
                    yield STEP[f"att{step}"]
                    if step == 0:
                        pe.wait_ge(*in_sbuf("qT1", t))
                        pe.wait_ge(*in_sbuf("kT0", t))
                        pe.wait_ge(*in_sbuf("kT1", t))
                    if step < HA:
                        h = step
                        pe.wait_ge(*bank_free(f"s{h}", t))
                        keys = P * key_tiles(t)
                        mm(ps[BANK[f"s{h}"]][:, 0:keys], qT[0:QK, h, :], kTh[0:QK, h, 0:keys], start=True, stop=True)\
                            .then_inc(FULL[f"s{h}"], 1)
                    if 0 <= step - 2 < HA:
                        h = step - 2
                        pe.wait_ge(*event("p_exp", t, h + 1))
                        pe.wait_ge(*bank_free(f"pT{h}", t))
                        turn(ps[BANK[f"pT{h}"]], lambda j: ssb[:, h % 2, j * P:(j + 1) * P], key_tiles(t))\
                            .then_inc(FULL[f"pT{h}"], 1)
                    if 0 <= step - 3 < HA:
                        h = step - 3
                        pe.wait_ge(*in_sbuf(f"pT{h}", t))
                        if h == 0:
                            pe.wait_ge(*bank_free("o", t))
                        for j in range(key_tiles(t)):
                            ins = mm(ps[BANK["o"]][:, h * VD:(h + 1) * VD], pT[:, h % 2, j * P:(j + 1) * P],
                                     vc[:, j, h * VD:(h + 1) * VD], start=(j == 0), stop=(j == key_tiles(t) - 1))
                ins.then_inc(FULL["o"], 1)
                yield STEP["turn_o"]
                pe.wait_ge(*in_sbuf("o", t))
                pe.wait_ge(*bank_free("oT", t))
                turn(ps[BANK["oT"]], lambda j: ob[:, j * P:(j + 1) * P], 4).then_inc(FULL["oT"], 1)
                yield STEP["y0"]
                branch_out(t, 1, ("y0a", "y0b"), "oT")
                yield STEP["turn_ro"]
                pe.wait_ge(*event("ro_done", t))
                pe.wait_ge(*bank_free("roT", t))
                turn(ps[BANK["roT"]], lambda j: ro[:, j, :], 4).then_inc(FULL["roT"], 1)
                yield STEP["y1"]
                branch_out(t, 2, ("y1a", "y1b"), "roT")
                yield STEP["mem_scores"]
                for i in range(2):
                    pe.wait_ge(*bank_free(f"ms{i}", t))
                    for h in range(2):
                        ins = mm(ps[BANK[f"ms{i}"]][:, h * M:h * M + M], xqT[:, 2 * i + h, :], mkT[:, 2 * i + h, :],
                                 start=True, stop=True)
                    ins.then_inc(FULL[f"ms{i}"], 1)
                yield STEP["mem_turn"]
                for i in range(2):
                    pe.wait_ge(*in_sbuf(f"ms{i}", t))
                    pe.wait_ge(*bank_free(f"mp{i}", t))
                    turn(ps[BANK[f"mp{i}"]], lambda j: ssb[:, i, j * P:(j + 1) * P], 4).then_inc(FULL[f"mp{i}"], 1)
                yield STEP["mem_out"]
                pe.wait_ge(*in_sbuf("mp0", t))
                pe.wait_ge(*in_sbuf("mp1", t))
                pe.wait_ge(*bank_free("mo", t))
                for h in range(HX):
                    for j in range(2):
                        ins = mm(ps[BANK["mo"]][:, h * XD:(h + 1) * XD],
                                 pT[:, h // 2, (h % 2) * M + j * P:(h % 2) * M + (j + 1) * P],
                                 mv[:, j, h, :], start=(j == 0), stop=(j == 1))
                ins.then_inc(FULL["mo"], 1)
                yield STEP["turn_mo"]
                pe.wait_ge(*in_sbuf("mo", t))
                pe.wait_ge(*bank_free("moT", t))
                turn(ps[BANK["moT"]], lambda j: ob[:, j * P:(j + 1) * P], 4).then_inc(FULL["moT"], 1)
                yield STEP["y2"]
                branch_out(t, 3, ("y2a", "y2b"), "moT")
                yield STEP["turn_merged"]
                pe.wait_ge(*event("merged", t))
                for i in range(2):
                    pe.wait_ge(*bank_free(f"mT{i}", t))
                    turn(ps[BANK[f"mT{i}"]], lambda j: merged[:, (4 * i + j) * P:(4 * i + j + 1) * P], 4)\
                        .then_inc(FULL[f"mT{i}"], 1)
                for c, step, name in ((4, "h_a", "ha"), (5, "h_b", "hb")):
                    yield STEP[step]
                    pe.wait_ge(*in_sbuf(f"mT{c - 4}", t))
                    pe.wait_ge(*in_sbuf("mT1", t))
                    w = weights(t, c).rearrange("p (k n) -> p k n", n=512)
                    pe.wait_ge(*bank_free(name, t))
                    for k in range(KD):
                        ins = mm(ps[BANK[name]][:, :], mT[:, k, :], w[:, k, :], start=(k == 0), stop=(k == KD - 1))
                    ins.then_inc(FULL[name], 1)
                yield STEP["turn_xn"]
                pe.wait_ge(*event("xn_done", t))
                for i in range(2):
                    pe.wait_ge(*bank_free(f"xT{i}", t))
                    turn(ps[BANK[f"xT{i}"]], lambda j: xn_next[:, (4 * i + j) * P:(4 * i + j + 1) * P], 4)\
                        .then_inc(FULL[f"xT{i}"], 1)
                for c in range(4):
                    yield STEP[f"query{c}"]
                    if c == 0:
                        pe.wait_ge(*in_sbuf("xT0", t))
                        pe.wait_ge(*in_sbuf("xT1", t))
                    w = weights(t, 6 + c).rearrange("p (k n) -> p k n", n=512)
                    pe.wait_ge(*bank_free(f"pq{c}", t))
                    for j in range(4):
                        if j == 2:
                            yield STEP[f"query_end{c}"]
                        for k in range(KD):
                            ins = mm(ps[BANK[f"pq{c}"]][:, j * P:(j + 1) * P], w[:, k, j * P:(j + 1) * P], mT[:, k, :],
                                     start=(k == 0), stop=(k == KD - 1))
                    ins.then_inc(FULL[f"pq{c}"], 1)
                    yield STEP[f"score{c}"]
                    pe.wait_ge(*in_sbuf(f"pq{c}", t))
                    pe.wait_ge(*bank_free(f"sc{c}", t))
                    for j in range(4):
                        ins = mm(ps[BANK[f"sc{c}"]][:, j * P:(j + 1) * P], pqT[:, c % 2, j * P:(j + 1) * P],
                                 keysT[:, 4 * c + j, :], start=True, stop=True)
                    ins.then_inc(FULL[f"sc{c}"], 1)

            def peer(u, v, k0):
                if not v:
                    return
                t, h = v
                if h == 0 and k0 == 0:
                    pe.wait_ge(s_taken, t + 1)
                for k in range(k0, k0 + QUANTUM):
                    n = t * (HP * TOP) + h * TOP + k
                    pe.wait_ge(s_diag, n + 1)
                    pe.wait_ge(v_in[k % RING], 16 * (t * (HP * TOP // RING) + h * (TOP // RING) + k // RING + 1))
                    for i in range(2):
                        ins = mm(ps[i][:, :], diag[:, k % RING, :], vb[:, k % RING, i * 512:i * 512 + 512],
                                 start=(h == 0 and k == 0), stop=(h == HP - 1 and k == TOP - 1))
                    ins.then_inc(v_used, 1)

            weave(front, peer, gate_unit, pe)

        @block.vector
        def _(dve):
            V = nc.vector
            def make_link(chain, base):
                count = {"n": 0}

                def link(ins, hold=False):
                    count["n"] += 1
                    ins.then_inc(chain, 1)
                    dve.wait_ge(chain, base + count["n"])
                    if hold:
                        dve.nop(nofuse=True)
                return link, count

            def rsqrt(link, x, n):
                y, s = nwt[:, 0:n], nwt[:, 16:16 + n]
                link(V.tensor_scalar(x, x, EPS, None, ALU.add))
                link(V.tensor_scalar(y.bitcast(U32), x.bitcast(U32), 1, None, ALU.logical_shift_right))
                link(V.tensor_scalar(y.bitcast(I32), y.bitcast(I32), -1.0, 1597463007.0, ALU.mult, ALU.add))
                for _ in range(3):
                    link(V.scalar_tensor_tensor(out=s, in0=y, scalar=-0.5, in1=y, op0=ALU.mult, op1=ALU.mult))
                    link(V.tensor_tensor(s, s, x, ALU.mult))
                    link(V.scalar_tensor_tensor(out=y, in0=s, scalar=1.5, in1=y, op0=ALU.add, op1=ALU.mult))
                return y

            def rotate(link, x, half, cos, sin, heads):
                x1, x2 = x[:, :, 0:half], x[:, :, half:2 * half]
                c = cos.rearrange("p (o n) -> p o n", o=1).broadcast_to((P, heads, half))
                s = sin.rearrange("p (o n) -> p o n", o=1).broadcast_to((P, heads, half))
                r = [tmp[:, 256 * i:256 * i + heads * half].rearrange("p (h n) -> p h n", n=half) for i in range(4)]
                V.tensor_tensor(r[0], x1, c, ALU.mult)
                V.tensor_tensor(r[1], x2, s, ALU.mult)
                V.tensor_tensor(r[2], x1, s, ALU.mult)
                link(V.tensor_tensor(r[3], x2, c, ALU.mult))
                V.tensor_tensor(x1, r[0], r[1], ALU.subtract)
                return V.tensor_tensor(x2, r[2], r[3], ALU.add)

            link, setup_count = make_link(dve_chain, 0)
            V.memset(state[:, :, :], 0.0).then_inc(v_used, RING)
            V.memset(vc[:, :, :], 0.0).then_inc(s_taken, 1)
            V.memset(acts[:, 4, :], 0.0).then_inc(dots, RING)
            def memory_keys(j):
                c, m = divmod(j, 2)
                bank, use = 6 + j % 2, 2 * (j // 2)
                dve.wait_ge(full[bank], use + 1)
                dst = mv[:, m, 2 * c:2 * c + 2, :]
                kv = ps[bank][:, :].rearrange("p (h n) -> p h n", n=2 * XD)
                V.tensor_scalar(dst, kv[:, :, XD:2 * XD], rstd_m[:, m:m + 1], None, ALU.mult)
                keys = tmp[:, 256 * j:256 * j + 256].rearrange("p (h n) -> p h n", n=XD)
                sqk = kz[:, :, :].rearrange("p h n -> p (h n)").rearrange("p (h n) -> p h n", n=XD)
                V.tensor_scalar(keys, kv[:, :, 0:XD], rstd_m[:, m:m + 1], None, ALU.mult).then_inc(drained[bank], 1)
                dve.wait_ge(drained[bank], use + 1)
                link(V.tensor_tensor(sqk, keys, keys, ALU.mult))
                link(V.tensor_reduce(mem_st, sqk, AX.X, ALU.add))
                link(V.tensor_scalar(mem_st, mem_st, 1.0 / XD, None, ALU.mult))
                y = rsqrt(link, mem_st, 2)
                link(V.tensor_tensor(keys, keys, y.rearrange("p (h o) -> p h o", o=1).broadcast_to((P, 2, XD)), ALU.mult))
                V.tensor_tensor(keys, keys, mkrow[:, :].rearrange("p (o n) -> p o n", o=1).broadcast_to((P, 2, XD)),
                                ALU.mult).then_inc(s_mem_keys, 1)

            def memory_keys_out(j):
                c, m = divmod(j, 2)
                bank, use = 6 + j % 2, 2 * (j // 2)
                dve.wait_ge(full[bank], use + 2)
                V.tensor_copy(mkT[:, 2 * c:2 * c + 2, m * P:(m + 1) * P],
                              ps[bank][:, 0:256].rearrange("p (h n) -> p h n", n=P)).then_inc(drained[bank], 1)

            def angles():
                ang = work[:, 0:192].rearrange("p (t n) -> p t n", n=48)
                sn = work[:, 384:576].rearrange("p (t n) -> p t n", n=48)
                cs = work[:, 192:384].rearrange("p (t n) -> p t n", n=48)
                turns = work[:, 576:768].rearrange("p (t n) -> p t n", n=48)
                link(V.tensor_copy(posf, posi[:, :]))
                link(V.tensor_tensor(ang, posf.rearrange("p (t o) -> p t o", o=1).broadcast_to((P, T, 48)),
                                     cst[:, K_INV:K_INV + 48].rearrange("p (o n) -> p o n", o=1).broadcast_to((P, T, 48)),
                                     ALU.mult))
                link(V.tensor_scalar(turns, ang, 1.0 / TWO_PI, ROUND, ALU.mult, ALU.add))
                link(V.tensor_scalar(turns, turns, ROUND, None, ALU.subtract))
                for part in (TP1, TP2, TP3):
                    link(V.scalar_tensor_tensor(out=ang, in0=turns, scalar=-part, in1=ang, op0=ALU.mult, op1=ALU.add))
                link(V.tensor_scalar(sn, ang, PI_LOW, -PI_LOW, ALU.min, ALU.max))
                link(V.tensor_scalar(ang, ang, TWO_PI / 4, None, ALU.add))
                link(V.tensor_scalar(turns, ang, PI_LOW, -TWO_PI, ALU.is_gt, ALU.mult))
                link(V.tensor_tensor(cs, ang, turns, ALU.add))
                V.tensor_scalar(cs, cs, PI_LOW, -PI_LOW, ALU.min, ALU.max).then_inc(s_angles, 1)

            def drain_projection(i, b):
                for t in (1, 3):
                    if not isinstance(i, int):
                        dve.wait_ge(s_parked[b], 16 * i)
                    dve.wait_ge(full[2 + t], 2 * i + b + 1)
                    V.tensor_scalar(stage[:, b, t, :], ps[2 + t][:, 0:CW], rstd_x[:, t:t + 1], None, ALU.mult)\
                        .then_inc(drained[2 + t], 1)

            def gate_unit(u):
                c, t = UNITS[u]
                if u % 2 == 0 or u >= len(NEEDED):
                    return
                dve.wait_ge(units_done, u + 1)
                dve.wait_ge(s_parked[c % 2], 16 * (c // 2))
                V.tensor_scalar(unit_stage(u), ps[1][:, 0:CW], rstd_x[:, t:t + 1], None, ALU.mult)\
                    .then_inc(unit_drained[1], 1)

            dve.wait_ge(s_gains, 16 * GAIN_LOADS)
            dve.wait_ge(s_memT, 16)
            for k in range(KD):
                ins = V.tensor_scalar(memT[:, k, :], memT[:, k, :], gcols[:, KD + k:KD + k + 1], None, ALU.mult)
            ins.then_inc(s_mem_g, 1)
            dve.wait_ge(s_sums, 2)
            y = rsqrt(link, rstd_m, 2)
            link(V.tensor_copy(rstd_m, y))
            dve.wait_ge(s_const, 16 * CONSTANT_LOADS)
            memory_keys(0)
            memory_keys_out(0)
            memory_keys(1)
            dve.wait_ge(s_xT, 16)
            for k in range(KD):
                if k == KD // 2:
                    memory_keys_out(1)
                    memory_keys(2)
                ins = V.tensor_scalar(xT[:, k, :], xT[:, k, :], gcols[:, k:k + 1], None, ALU.mult)
            ins.then_inc(s_x_g, 1)
            memory_keys_out(2)
            memory_keys(3)
            dve.wait_ge(s_sums, 2 + T)
            y = rsqrt(link, rstd_x, T)
            V.tensor_copy(rstd_x, y).then_inc(s_rstd, 1)
            dve.wait_ge(s_rstd, 1)
            angles()
            drain_projection(0, 0)
            memory_keys_out(3)
            drain_projection(0, 1)
            with dve.Fori(1, EARLY // 2) as i:
                drain_projection(i, 0)
                drain_projection(i, 1)
            dve.wait_ge(s_rope, 2)
            V.memset(kT[:, :], 0.0).then_inc(s_ready, 1)
            setup_links = setup_count["n"]

            def topk(link, rows, vals, inds, pairs):
                dve.nop(nofuse=True)
                for h, to in pairs:
                    ins = V.max(vals[:, to, 0:8], rows[:, h, :])
                link(ins, hold=True)
                for h, to in pairs:
                    V.max_index(inds[:, to, 0:8], vals[:, to, 0:8], rows[:, h, :])
                for h, to in pairs:
                    ins = V.match_replace(rows[:, h, :], vals[:, to, 0:8], rows[:, h, :], -3.0e38)
                link(ins, hold=True)
                for h, to in pairs:
                    ins = V.max(vals[:, to, 8:16], rows[:, h, :])
                link(ins, hold=True)
                for h, to in pairs:
                    ins = V.max_index(inds[:, to, 8:16], vals[:, to, 8:16], rows[:, h, :])
                link(ins)

            nplace = merged[:, 0:256].rearrange("p (h k) -> p h k", k=TOP)

            def choose(link, t, c):
                pair, rows = slice(2 * c, 2 * c + 2), slice(4 * c, 4 * c + 4)
                sides = topv[:, rows, :].rearrange("p (h c) k -> p h c k", c=2)
                V.tensor_copy(nplace[:, rows, :], topi[:, rows, :])
                link(V.tensor_tensor(cand[:, pair, :].rearrange("p h (i j) -> p h i j", j=TOP),
                                     sides[:, :, 0, :].rearrange("p h (k o) -> p h k o", o=1)
                                     .broadcast_to((P, 2, TOP, TOP)),
                                     sides[:, :, 1, :].rearrange("p h (o k) -> p h o k", o=1)
                                     .broadcast_to((P, 2, TOP, TOP)), ALU.add))
                topk(link, cand, topv, topi, [(2 * c, 4 * c), (2 * c + 1, 4 * c + 1)])
                best = topv[:, 4 * c:4 * c + 2, :]
                ins = V.tensor_tensor(besub[:, pair, :], best, best[:, :, 0:1].broadcast_to((P, 2, TOP)), ALU.subtract)
                if c == 3:
                    ins.then_inc(ev["best_sub"], 1)

            def place(link, t, c):
                pair, rows = slice(2 * c, 2 * c + 2), slice(4 * c, 4 * c + 4)
                sides = nplace[:, rows, :].rearrange("p (h c) k -> p h c k", c=2)
                best, part = topi[:, 4 * c:4 * c + 2, :], topi[:, 4 * c + 2:4 * c + 4, :]
                h2 = hot[:, pair, :, :]
                for side, (sel, op, arg) in enumerate(((seli, ALU.logical_shift_right, 4), (seli2, ALU.bitwise_and, 15))):
                    dst = sel[:, pair, :]
                    link(V.tensor_scalar(part, best, arg, None, op))
                    link(V.tensor_copy(dst, part))
                    link(V.tensor_tensor(h2, dst.rearrange("p h (k o) -> p h k o", o=1).broadcast_to((P, 2, TOP, TOP)),
                                         iota.rearrange("p (a b j) -> p a b j", a=1, b=1)
                                         .broadcast_to((P, 2, TOP, TOP)), ALU.is_equal))
                    link(V.tensor_tensor(h2, h2, sides[:, :, side, :].rearrange("p h (o j) -> p h o j", o=1)
                                         .broadcast_to((P, 2, TOP, TOP)), ALU.mult))
                    link(V.tensor_reduce(dst, h2, AX.X, ALU.add))
                link(V.scalar_tensor_tensor(out=idxn[:, 2 * TOP * c:2 * TOP * (c + 1)].rearrange("p (h k) -> p h k", k=TOP),
                                            in0=seli[:, pair, :], scalar=float(NK), in1=seli2[:, pair, :],
                                            op0=ALU.mult, op1=ALU.add))

            def merge(link, t, br):
                dve.wait_ge(*event("gate_tanh", t, br + 1))
                dst = merged if br == 0 else tmp
                for i, name in enumerate((f"y{br}a", f"y{br}b")):
                    part = slice(i * 512, i * 512 + 512)
                    dve.wait_ge(*computed(name, t))
                    V.scalar_tensor_tensor(out=dst[:, part], in0=gt[:, part], scalar=1.0, in1=ps[BANK[name]][:, :],
                                           op0=ALU.add, op1=ALU.mult).then_inc(DRAINED[name], 1)
                dve.wait_ge(*in_sbuf(f"y{br}a", t))
                dve.wait_ge(*in_sbuf(f"y{br}b", t))
                if br == 1:
                    link(V.tensor_tensor(merged[:, :], merged[:, :], tmp[:, :], ALU.add))
                if br == 2:
                    V.tensor_tensor(merged[:, :], merged[:, :], tmp[:, :], ALU.add).then_inc(ev["merged"], 1)

            def spread(x, heads, n):
                return x.rearrange("p (h o) -> p h o", o=1).broadcast_to((P, heads, n))

            def front(t):
                link, n = make_link(dve_chain, setup_links + t * DVE_LINKS)
                r = pa[:, R_Q:R_Q + 2 * HR * RK].rearrange("p (h n) -> p h n", n=RK)
                yield STEP["latent_rstd"]
                link(V.tensor_copy(ropet[:, :, :].rearrange("p i n -> p (i n)").rearrange("p (o n) -> p o n", o=1),
                                   rope[:, :, :, :].rearrange("p t i n -> p t (i n)")[:, bass.ds(t, 1), :]))
                cos_a, sin_a = ropet[:, 0, 0:16], ropet[:, 1, 0:16]
                cos_r, sin_r = ropet[:, 0, 16:48], ropet[:, 1, 16:48]
                dve.wait_ge(*event("c_stats", t))
                y = rsqrt(link, c_st, 6)
                V.tensor_copy(c_st, y).then_inc(ev["c_rstd"], 1)
                yield STEP["latent_scale"]
                dve.wait_ge(*event("c_rstd", t))
                rotate(link, r, 32, cos_r, sin_r, 2 * HR).then_inc(ev["r_roped"], 1)
                dve.wait_ge(*event("r_roped", t))
                V.tensor_tensor(kz[:, :, :], r[:, HR:2 * HR, :], spread(zeta, HR, RK), ALU.mult).then_inc(ev["kz"], 1)
                yield STEP["turn_ret"]
                dve.wait_ge(*computed("rqT", t))
                V.tensor_copy(rqT[:, :, :], ps[BANK["rqT"]][0:RK, :])
                V.tensor_tensor(rxT[:, :, :], ps[BANK["rqT"]][0:RK, :], xiT, ALU.mult).then_inc(DRAINED["rqT"], 1)
                dve.wait_ge(*computed("rkT", t))
                V.tensor_scalar(rkT[:, :, :], ps[BANK["rkT"]][0:RK, :], RK ** -0.5, None, ALU.mult).then_inc(DRAINED["rkT"], 1)
                yield STEP["q_proj"]
                for i in range(2):
                    dve.wait_ge(*computed(f"q{i}", t))
                    V.tensor_copy(qk[:, 4 * i:4 * i + 4, :], ps[BANK[f"q{i}"]][:, 0:384]).then_inc(DRAINED[f"q{i}"], 1)
                yield STEP["kv_proj"]
                for i in range(2):
                    dve.wait_ge(*computed(f"kv{i}", t))
                    bank = ps[BANK[f"kv{i}"]][:, :].rearrange("p (h n) -> p h n", n=NOPE + VD)
                    V.tensor_copy(qk[:, HA + 4 * i:HA + 4 * i + 4, 0:NOPE], bank[:, :, 0:NOPE])
                    V.tensor_copy(vc[:, bass.ds(t, 1), 256 * i:256 * i + 256].rearrange("p o (h n) -> p (o h) n", n=VD),
                                  bank[:, :, NOPE:NOPE + VD]).then_inc(DRAINED[f"kv{i}"], 1)
                link(V.tensor_copy(qk[:, HA:2 * HA, NOPE:QK], pa[:, C_KR:C_KR + ROPE].rearrange(
                    "p (o n) -> p o n", o=1).broadcast_to((P, HA, ROPE))))
                yield STEP["ret_scores"]
                dve.wait_ge(*computed("rin", t))
                V.tensor_tensor(inner[:, :, :], ps[BANK["rin"]][:, :], decayT, ALU.mult).then_inc(DRAINED["rin"], 1)
                yield STEP["qk_stats"]
                link(V.tensor_tensor(sq, qk, qk, ALU.mult))
                link(V.tensor_reduce(qk_st, sq, AX.X, ALU.add))
                yield STEP["ret_out"]
                link(V.tensor_scalar(qk_st, qk_st, 1.0 / QK, None, ALU.mult))
                y = rsqrt(link, qk_st, 2 * HA)
                link(V.tensor_copy(qk_st, y))
                yield STEP["qk_norm"]
                link(V.tensor_tensor(qk, qk, spread(qk_st, 2 * HA, QK), ALU.mult))
                for i in range(2):
                    half = qk[:, HA * i:HA * i + HA, :]
                    ins = V.tensor_tensor(half, half, qkrow[:, i, :].rearrange("p (o n) -> p o n", o=1)
                                          .broadcast_to((P, HA, QK)), ALU.mult)
                link(ins)
                yield STEP["qk_rope"]
                rotate(link, qk[:, :, NOPE:QK], ROPE // 2, cos_a, sin_a, 2 * HA).then_inc(ev["qk_roped"], 1)
                dve.wait_ge(*computed("rinc", t))
                for h in range(HR):
                    ins = V.scalar_tensor_tensor(out=state[:, h, :], in0=state[:, h, :], scalar=CHUNK_DECAY[h],
                                                 in1=ps[BANK["rinc"]][0:RK, h * RV:(h + 1) * RV], op0=ALU.mult, op1=ALU.add)
                ins.then_inc(DRAINED["rinc"], 1)
                yield STEP["ret_norm"]
                dve.wait_ge(*event("ro_stats", t))
                y = rsqrt(link, ro_st, HR)
                dve.wait_ge(*in_sbuf("ro", t))
                link(V.tensor_tensor(ro[:, :, :], ro[:, :, :], spread(y, HR, RV), ALU.mult))
                dve.wait_ge(*event("rg_tanh", t))
                flat = ro[:, :, :].rearrange("p h n -> p (h n)")
                link(V.tensor_tensor(flat, flat, gnrow[:, :], ALU.mult))
                link(V.scalar_tensor_tensor(out=rth[:, :], in0=rth[:, :], scalar=1.0, in1=pa[:, R_G:R_G + 512],
                                            op0=ALU.add, op1=ALU.mult))
                V.tensor_tensor(flat, flat, rth[:, :], ALU.mult).then_inc(ev["ro_done"], 1)
                for h in range(HA):
                    yield STEP[f"att{h + 1}"]
                    if h == 0:
                        dve.wait_ge(s_mask, 16 * (t + 1))
                    dve.wait_ge(*computed(f"s{h}", t))
                    if h >= 2:
                        dve.wait_ge(*computed(f"pT{h - 2}", t))
                    dve.nop(nofuse=True)
                    keys = P * key_tiles(t)
                    V.tensor_tensor_reduce(out=ssb[:, h % 2, 0:keys], in0=ps[BANK[f"s{h}"]][:, 0:keys], in1=mask[:, 0:keys],
                                           scale=-ATT_SCALE, scalar=3.0e38, op0=ALU.add, op1=ALU.min,
                                           accum_out=nmax[:, h:h + 1]).then_inc(DRAINED[f"s{h}"], 1)
                yield STEP["att_out"]
                dve.wait_ge(*computed("o", t))
                link(V.reciprocal(l_att, l_att))
                V.tensor_tensor(ob[:, :].rearrange("p (h n) -> p h n", n=VD),
                                ps[BANK["o"]][:, :].rearrange("p (h n) -> p h n", n=VD), spread(l_att, HA, VD), ALU.mult)\
                    .then_inc(DRAINED["o"], 1)
                yield STEP["y0"]
                merge(link, t, 0)
                yield STEP["y1"]
                merge(link, t, 1)
                yield STEP["mem_scores"]
                for i in range(2):
                    dve.wait_ge(*computed(f"ms{i}", t))
                    link(V.tensor_reduce(mmax[:, 2 * i:2 * i + 2],
                                         ps[BANK[f"ms{i}"]][:, :].rearrange("p (h n) -> p h n", n=M), AX.X, ALU.max))
                    V.tensor_scalar(mmax[:, 2 * i:2 * i + 2], mmax[:, 2 * i:2 * i + 2], -MEM_SCALE, None, ALU.mult)\
                        .then_inc(ev["mem_max"], 1)
                yield STEP["mem_out"]
                dve.wait_ge(*computed("mo", t))
                link(V.reciprocal(l_mem, l_mem))
                V.tensor_tensor(ob[:, :].rearrange("p (h n) -> p h n", n=XD),
                                ps[BANK["mo"]][:, :].rearrange("p (h n) -> p h n", n=XD), spread(l_mem, HX, XD), ALU.mult)\
                    .then_inc(DRAINED["mo"], 1)
                yield STEP["y2"]
                merge(link, t, 2)
                for i, (step, name) in enumerate((("h_a", "ha"), ("h_b", "hb"))):
                    yield STEP[step]
                    if i == 0:
                        dve.wait_ge(s_h, 16 * (t + 1))
                    part = slice(i * 512, i * 512 + 512)
                    dve.wait_ge(*computed(name, t))
                    V.tensor_tensor(h_next[:, part], ps[BANK[name]][:, :], h_next[:, part], ALU.add)\
                        .then_inc(DRAINED[name], 1)
                yield STEP["f_rstd"]
                dve.wait_ge(*event("f_stats", t))
                y = rsqrt(link, f_st, 1)
                V.tensor_copy(f_st, y).then_inc(ev["f_rstd"], 1)
                yield STEP["xn"]
                dve.wait_ge(*event("xn_scaled", t))
                V.tensor_tensor(xn_next, xn_next, grow[:, :], ALU.mult).then_inc(ev["xn_done"], 1)
                for c in range(4):
                    yield STEP[f"query{c + 1}" if c < 3 else "top3"]
                    dve.wait_ge(*in_sbuf(f"sc{c}", t))
                    topk(link, scores, topv, topi, [(r, r) for r in range(4 * c, 4 * c + 4)])
                    yield STEP[f"query_end{c + 1}" if c < 3 else "choice3"]
                    choose(link, t, c)
                    yield STEP[f"score{c + 1}" if c < 3 else "place3"]
                    place(link, t, c)
                dve.wait_ge(*event("best_exp", t))
                link(V.tensor_reduce(gsum, besub, AX.X, ALU.add))
                link(V.reciprocal(gsum, gsum))
                link(V.tensor_scalar(gsum, gsum, 0.5, None, ALU.mult))
                link(V.tensor_tensor(gaten[:, :].rearrange("p (h k) -> p h k", k=TOP), besub,
                                     spread(gsum, HP, TOP), ALU.mult))
                assert n["n"] == DVE_LINKS, n["n"]

            def handoff(t):
                V.tensor_copy(idx[:, 0:KEPT * TOP], idxn[:, 0:KEPT * TOP])
                V.tensor_copy(gate[:, :], gaten[:, :])
                V.tensor_copy(xn_cur, xn_next).then_inc(ev["handed"], 1)
                dve.wait_ge(*event("handed", t))

            def handoff_rest(t):
                V.tensor_copy(idx[:, KEPT * TOP:], idxn[:, KEPT * TOP:])
                V.tensor_copy(h_cur, h_next).then_inc(ev["handed_rest"], 1)
                dve.wait_ge(*event("handed_rest", t))

            def peer(u, v, k0):
                if not u:
                    return
                t, h = u
                for k in range(k0, k0 + QUANTUM):
                    dve.wait_ge(u_in[k % RING], 16 * (t * (HP * TOP // RING) + h * (TOP // RING) + k // RING + 1))
                    V.tensor_tensor_reduce(out=ub[:, k % RING, :], in0=ub[:, k % RING, :], in1=xn_cur, scale=1.0,
                                           scalar=0.0, op0=ALU.mult, op1=ALU.add, accum_out=acts[:, 0, k:k + 1])\
                        .then_inc(dots, 1)
                if k0 + QUANTUM < TOP:
                    return
                link, n = make_link(peer_chain, t * PEER_LINKS + h * 3)
                dve.wait_ge(dots, RING + t * (HP * TOP) + (h + 1) * TOP)
                x, c = acts[:, 0, :], acts[:, 1, :]
                link(V.tensor_tensor(c, x, x, ALU.mult))
                link(V.tensor_scalar(c, c, GELU_B, 1.0, ALU.mult, ALU.add))
                V.tensor_tensor(acts[:, 2, :], c, x, ALU.mult).then_inc(gelu_in, 1)
                link(V.tensor_tensor(acts[:, 3, :], x, gate[:, h * TOP:(h + 1) * TOP], ALU.mult))
                dve.wait_ge(gelu_tanh, t * HP + h + 1)
                V.scalar_tensor_tensor(out=wts[:, h % 2, :], in0=acts[:, 2, :], scalar=1.0, in1=acts[:, 3, :],
                                       op0=ALU.add, op1=ALU.mult).then_inc(s_wts, 1)

            def finish(t):
                dve.wait_ge(v_used, RING + (t + 1) * HP * TOP)
                if isinstance(t, int):
                    dve.wait_ge(s_out, 16 * t)
                for i in range(2):
                    ins = V.tensor_tensor(res[:, i * 512:i * 512 + 512], ps[i][:, :], h_cur[:, i * 512:i * 512 + 512], ALU.add)
                ins.then_inc(s_taken, 1)
                dve.wait_ge(s_taken, t + 2)

            weave(front, peer, gate_unit, dve, handoff, handoff_rest, finish)


_LG = np.log(1.0 - 2.0 ** (-5.0 - np.arange(HR, dtype=np.float32))).astype(np.float32)
CHUNK_DECAY = [float(x) for x in np.exp(_LG * np.float32(P))]


def weave(front, peer, gate_unit, eng, handoff=None, handoff_rest=None, finish=None):
    for unit in range(UNITS_FIRST):
        gate_unit(unit)
    steps, unit = front(0), UNITS_FIRST
    reached = next(steps)
    for s, name in enumerate(STEPS):
        while reached is not None and reached <= s:
            reached = next(steps, None)
        for _ in range(UNITS_AFTER.get(name, 0)):
            gate_unit(unit)
            unit += 1
    if handoff:
        handoff(0)
        handoff_rest(0)
    for unit in range(len(NEEDED + LATE), len(UNITS)):
        gate_unit(unit)
    for k in range(0, TOP, QUANTUM):
        peer((0, 0), None, k)
    with eng.Fori(1, T) as t:
        steps = front(t)
        reached = next(steps)
        for q in range(QUANTA):
            h, k = divmod(q * QUANTUM, TOP)
            peer((t - 1, h + 1), (t - 1, h), k)
            while reached is not None and PLACE[reached] < (q + 1) / QUANTA:
                reached = next(steps, None)
        if handoff:
            handoff(t)
        for k in range(0, TOP, QUANTUM):
            peer((t, 0), (t - 1, HP - 1), k)
        if handoff:
            finish(t - 1)
            handoff_rest(t)
    for q in range(QUANTA):
        h, k = divmod(q * QUANTUM, TOP)
        peer((T - 1, h + 1), (T - 1, h), k)
    for k in range(0, TOP, QUANTUM):
        peer(None, (T - 1, HP - 1), k)
    if handoff:
        finish(T - 1)


_DIRECT = ["x", "mem", "ffn_norm_g", "ret_gn_g", "mla_qn_g", "mla_kn_g", "x_kn_g", "w_uq", "w_ukv", "w_o_mla", "w_o_ret", "w_o_cross", "w_out",
           "w_mem_kv", "peer_w_q"]


def kernel(**inputs):
    import concourse.bacc as _bacc
    from concourse.bass_utils import run_bass_kernel_spmd as _run

    f = np.float32
    laid = {n: np.asarray(inputs[n]) for n in _DIRECT}
    laid["positions"] = np.asarray(inputs["positions"])[0].reshape(T, P).T
    for n in ("attn_norm_g", "mem_norm_g", "mla_q_norm_g", "mla_kv_norm_g", "x_qn_g"):
        laid[n] = np.asarray(inputs[n])[0].reshape(-1, P).T
    laid["xT"] = np.asarray(inputs["x"])[0].T
    laid["memT"] = np.asarray(inputs["mem"])[0].T
    laid["w_in"] = np.asarray(inputs["w_in"])[0].reshape(KD, P, CHUNKS, CW).transpose(2, 1, 0, 3)
    laid["keysT"] = np.asarray(inputs["peer_keys"])[0].reshape(2 * HP, NK, P).transpose(2, 0, 1)
    laid["peer_u"] = np.asarray(inputs["peer_u"])[0]
    laid["peer_v"] = np.asarray(inputs["peer_v"])[0]
    i = np.arange(P, dtype=f)
    diff = i[None, :] - i[:, None]
    c = np.zeros((P, K_END), f)
    c[:, K_ID:K_ID + P] = np.eye(P, dtype=f)
    for h in range(HR):
        c[:, K_DECAY + h * P:K_DECAY + (h + 1) * P] = np.where(diff >= 0, np.exp(_LG[h] * np.maximum(diff, 0)), 0)
        c[:, K_XI + h * P:K_XI + (h + 1) * P] = np.exp(_LG[h] * (i + 1))[None, :]
        c[:, K_ZETA + h] = np.exp(_LG[h] * (P - 1 - i)) * f(RK ** -0.5)
    c[:, K_IOTA:K_IOTA + TOP] = np.arange(TOP)
    for at, d in ((K_INV, ROPE), (K_INV + ROPE // 2, RK)):
        c[:, at:at + d // 2] = np.power(f(10000.0), -np.arange(0, d, 2, dtype=f) / f(d))
    laid["consts"] = c
    laid["mask"] = np.where(np.arange(S)[None, :] <= np.arange(S)[:, None], f(0), f(NEG))

    nc = _bacc.Bacc("TRN2", target_bir_lowering=False, num_devices=1)
    arrays, aps = {}, {}
    for name, arr in laid.items():
        arr = np.ascontiguousarray(arr)
        arrays["in_" + name] = arr
        aps[name] = nc.dram_tensor("in_" + name, arr.shape, mybir.dt.from_np(arr.dtype), kind="ExternalInput").ap()
    out = nc.dram_tensor("out_0", (1, S, D), F32, kind="ExternalOutput").ap()
    build(nc, aps, out)
    r = _run(nc, [arrays], core_ids=[0])
    return r.results[0]["out_0"]
```
